# Optimizing a Trainium2 kernel written in Bass

```python
import math
import jax
import jax.numpy as jnp
from jax import lax
import numpy as np
import jax, jax.numpy as jnp

D_MODEL = 1024
BATCH = 1
SEQ = 256
DEPTH = 2

GRID_W = 64
CTX_LEN = 256
N_MOD = 9
D_FF = 2816
FFN_RES = 0.5
EPS = 1e-6
ROPE_THETA = 10000.0
Q_BLOCK = 128

CONV_WIDTH = 3
D_CONV = 512
D_FOURIER = 512
FOURIER_GROUPS = 4
D_FG = D_FOURIER // FOURIER_GROUPS
D_IN_EVEN = 3 * D_CONV + D_FOURIER
D_OUT_EVEN = D_CONV + D_FOURIER

DA_HEADS = 8
DA_DK = 64
DA_DV = 2 * DA_DK
DA_SCALE = DA_DK ** -0.5
MLA_HEADS = 8
MLA_NOPE = 64
MLA_ROPE = 32
MLA_DQK = MLA_NOPE + MLA_ROPE
MLA_DV = 64
MLA_Q_RANK = 384
MLA_KV_RANK = 256
MLA_SCALE = MLA_DQK ** -0.5
DA_QCOLS = DA_HEADS * 2 * DA_DK
DA_VCOLS = DA_HEADS * DA_DV
Q_COLS = DA_QCOLS + MLA_Q_RANK
KV_COLS = DA_QCOLS + DA_VCOLS + MLA_KV_RANK + MLA_ROPE
D_IN_ODD = Q_COLS + KV_COLS
D_OUT_ODD = DA_HEADS * DA_DV + MLA_HEADS * MLA_DV


def rmsnorm(x, g):
    x32 = x.astype(jnp.float32)
    y = x32 * lax.rsqrt(jnp.mean(x32 * x32, axis=-1, keepdims=True) + EPS)
    return (y * g.astype(jnp.float32)).astype(x.dtype)

def modulate(h, g, shift, scale):
    return rmsnorm(h, g) * (1 + scale) + shift

def adaln_params(cond, w, b):
    m = jax.nn.silu(cond) @ w + b
    return m.reshape(cond.shape[0], 1, N_MOD, cond.shape[-1])

def swiglu(x, w_in, w_out):
    gate, up = jnp.split(x @ w_in, 2, axis=-1)
    return (jax.nn.silu(gate) * up) @ w_out

def macaron_ffn(h, m, g, w_in, w_out, slot):
    xm = modulate(h, g[2 * slot], m[:, :, 3 * slot], m[:, :, 3 * slot + 1])
    y = swiglu(xm, w_in, w_out)
    return h + FFN_RES * m[:, :, 3 * slot + 2] * rmsnorm(y, g[2 * slot + 1])

def rope_tables(n_tokens, rot_dim):
    rows = n_tokens // GRID_W
    row = jnp.broadcast_to(jnp.arange(rows)[:, None], (rows, GRID_W)).reshape(-1)
    col = jnp.broadcast_to(jnp.arange(GRID_W)[None, :], (rows, GRID_W)).reshape(-1)
    n_freq = rot_dim // 4
    freqs = ROPE_THETA ** (-jnp.arange(n_freq, dtype=jnp.float32) / n_freq)
    ang = jnp.stack([row.astype(jnp.float32)[:, None] * freqs,
                     col.astype(jnp.float32)[:, None] * freqs], axis=1)
    ang = ang[None, :, None, :, None, :]
    return jnp.cos(ang), jnp.sin(ang)

def apply_rope(x, cos, sin):
    b_, n, h, r = x.shape
    xr = x.astype(jnp.float32).reshape(b_, n, h, 2, 2, r // 4)
    x1, x2 = xr[..., 0:1, :], xr[..., 1:2, :]
    out = jnp.concatenate([x1 * cos - x2 * sin, x2 * cos + x1 * sin], axis=-2)
    return out.reshape(b_, n, h, r).astype(x.dtype)

def short_conv_fourier_mixer(xm, w_in, conv_w, w_out):
    b_, t = xm.shape[:2]
    u = xm @ w_in
    gate_b, gate_c, xv, xf = jnp.split(u, [D_CONV, 2 * D_CONV, 3 * D_CONV], axis=-1)
    pad = CONV_WIDTH // 2
    z = jnp.pad(gate_c * xv, ((0, 0), (pad, pad), (0, 0)))
    conv = z[:, 0:t] * conv_w[0]
    for k in range(1, CONV_WIDTH):
        conv = conv + z[:, k:k + t] * conv_w[k]
    y_conv = gate_b * conv
    xf = xf.astype(jnp.float32).reshape(b_, t, FOURIER_GROUPS, D_FG)
    y_four = jnp.real(jnp.fft.fft2(xf, axes=(1, 3), norm='ortho'))
    y_four = y_four.reshape(b_, t, D_FOURIER).astype(xm.dtype)
    return jnp.concatenate([y_conv, y_four], axis=-1) @ w_out

def attn_queries(u_q, g_q, w_uq, rope_da, rope_mla):
    b_, t = u_q.shape[:2]
    q_da, c_q = jnp.split(u_q, [DA_QCOLS], axis=-1)
    q_da = q_da.reshape(b_, t, DA_HEADS * 2, DA_DK)
    q_m = (rmsnorm(c_q, g_q) @ w_uq).reshape(b_, t, MLA_HEADS, MLA_DQK)
    q_nope, q_rope = q_m[..., :MLA_NOPE], q_m[..., MLA_NOPE:]
    if rope_da is not None:
        q_da = apply_rope(q_da, *rope_da)
        q_rope = apply_rope(q_rope, *rope_mla)
    q_da = q_da.reshape(b_, t, DA_HEADS, 2, DA_DK)
    return q_da, jnp.concatenate([q_nope, q_rope], axis=-1)

def attn_keys_values(u_kv, g_kv, w_uk, w_uv, rope_da, rope_mla):
    b_, t = u_kv.shape[:2]
    k_da, v_da, c_kv, k_r = jnp.split(
        u_kv, [DA_QCOLS, DA_QCOLS + DA_VCOLS, DA_QCOLS + DA_VCOLS + MLA_KV_RANK], axis=-1)
    k_da = k_da.reshape(b_, t, DA_HEADS * 2, DA_DK)
    v_da = v_da.reshape(b_, t, DA_HEADS, DA_DV)
    c_kv = rmsnorm(c_kv, g_kv)
    k_nope = (c_kv @ w_uk).reshape(b_, t, MLA_HEADS, MLA_NOPE)
    v_m = (c_kv @ w_uv).reshape(b_, t, MLA_HEADS, MLA_DV)
    k_r = k_r.reshape(b_, t, 1, MLA_ROPE)
    if rope_da is not None:
        k_da = apply_rope(k_da, *rope_da)
        k_r = apply_rope(k_r, *rope_mla)
    k_da = k_da.reshape(b_, t, DA_HEADS, 2, DA_DK)
    k_m = jnp.concatenate([k_nope, jnp.broadcast_to(k_r, (b_, t, MLA_HEADS, MLA_ROPE))], axis=-1)
    return k_da, v_da, k_m, v_m

def attend(q_da, q_m, k_da, v_da, k_m, v_m, lam):
    f32 = jnp.float32
    s = jnp.einsum('bqhmd,bkhmd->bhmqk', q_da, k_da).astype(f32) * DA_SCALE
    p = jax.nn.softmax(s, axis=-1)
    w_diff = p[:, :, 0] - lam * p[:, :, 1]
    o_da = jnp.einsum('bhqk,bkhd->bqhd', w_diff, v_da.astype(f32))
    sm = jnp.einsum('bqhd,bkhd->bhqk', q_m, k_m).astype(f32) * MLA_SCALE
    pm = jax.nn.softmax(sm, axis=-1)
    o_m = jnp.einsum('bhqk,bkhd->bqhd', pm, v_m.astype(f32))
    return o_da.astype(q_da.dtype), o_m.astype(q_m.dtype)

def attend_latent_blocks(qs, kvs, lam):
    b_, t = qs[0].shape[:2]
    nb = t // Q_BLOCK
    blocks = tuple(jnp.moveaxis(q.reshape(b_, nb, Q_BLOCK, *q.shape[2:]), 1, 0) for q in qs)
    o_da, o_m = lax.map(lambda qb: attend(qb[0], qb[1], *kvs, lam), blocks)
    unblock = lambda o: jnp.moveaxis(o, 0, 1).reshape(b_, t, *o.shape[3:])
    return unblock(o_da), unblock(o_m)

def attn_output(o_da, o_m, g_sub, lam_init, w_out):
    b_, t = o_da.shape[:2]
    o_da = (rmsnorm(o_da, g_sub) * (1 - lam_init)).reshape(b_, t, DA_HEADS * DA_DV)
    return jnp.concatenate([o_da, o_m.reshape(b_, t, MLA_HEADS * MLA_DV)], axis=-1) @ w_out

def first_inputs(seed: int = 0) -> dict:
    key = jax.random.key(seed)
    ks = iter(jax.random.split(key, 32))
    f32 = jnp.float32
    n_even = (DEPTH + 1) // 2
    n_odd = DEPTH // 2

    def nrm(shape, scale):
        return jax.random.normal(next(ks), shape, f32) * scale

    def gain(shape):
        return 1.0 + nrm(shape, 0.05)

    return {
        'x': nrm((BATCH, SEQ, D_MODEL), 1.0),
        'c': nrm((BATCH, D_MODEL), 1.0),
        'ctx': nrm((BATCH, CTX_LEN, D_MODEL), 1.0),
        'c_ctx': nrm((D_MODEL,), 1.0),
        'w_mod': nrm((DEPTH, D_MODEL, N_MOD * D_MODEL), 0.5 * D_MODEL ** -0.5),
        'b_mod': nrm((DEPTH, N_MOD * D_MODEL), 0.01),
        'norm_g': gain((DEPTH, 6, D_MODEL)),
        'w_ffn_in': nrm((DEPTH, 2, D_MODEL, 2 * D_FF), D_MODEL ** -0.5),
        'w_ffn_out': nrm((DEPTH, 2, D_FF, D_MODEL), D_FF ** -0.5),
        'w_in_even': nrm((n_even, D_MODEL, D_IN_EVEN), D_MODEL ** -0.5),
        'conv_w': nrm((n_even, CONV_WIDTH, D_CONV), CONV_WIDTH ** -0.5),
        'w_out_even': nrm((n_even, D_OUT_EVEN, D_MODEL), D_OUT_EVEN ** -0.5),
        'w_in_odd': nrm((n_odd, D_MODEL, D_IN_ODD), D_MODEL ** -0.5),
        'g_q_mla': gain((n_odd, MLA_Q_RANK)),
        'w_uq': nrm((n_odd, MLA_Q_RANK, MLA_HEADS * MLA_DQK), MLA_Q_RANK ** -0.5),
        'g_kv_mla': gain((n_odd, MLA_KV_RANK)),
        'w_uk': nrm((n_odd, MLA_KV_RANK, MLA_HEADS * MLA_NOPE), MLA_KV_RANK ** -0.5),
        'w_uv': nrm((n_odd, MLA_KV_RANK, MLA_HEADS * MLA_DV), MLA_KV_RANK ** -0.5),
        'lam_q1': nrm((n_odd, DA_DK), 0.1),
        'lam_k1': nrm((n_odd, DA_DK), 0.1),
        'lam_q2': nrm((n_odd, DA_DK), 0.1),
        'lam_k2': nrm((n_odd, DA_DK), 0.1),
        'g_subln': gain((n_odd, DA_DV)),
        'w_out_odd': nrm((n_odd, D_OUT_ODD, D_MODEL), D_OUT_ODD ** -0.5),
    }

def first_block(x, c, ctx, c_ctx, w_mod, b_mod, norm_g, w_ffn_in, w_ffn_out,
              w_in_even, conv_w, w_out_even,
              w_in_odd, g_q_mla, w_uq, g_kv_mla, w_uk, w_uv,
              lam_q1, lam_k1, lam_q2, lam_k2, g_subln, w_out_odd):
    f32 = jnp.float32
    n_lat = x.shape[1]
    rope_da = rope_tables(n_lat, DA_DK)
    rope_mla = rope_tables(n_lat, MLA_ROPE)
    h, hc = x, ctx
    for l in range(DEPTH):
        last = l == DEPTH - 1
        odd = l % 2 == 1
        ctx_live = (not last) or odd
        g = norm_g[l]
        m_x = adaln_params(c, w_mod[l], b_mod[l])
        h = macaron_ffn(h, m_x, g, w_ffn_in[l, 0], w_ffn_out[l, 0], 0)
        if ctx_live:
            m_c = adaln_params(c_ctx[None, :], w_mod[l], b_mod[l])
            hc = macaron_ffn(hc, m_c, g, w_ffn_in[l, 0], w_ffn_out[l, 0], 0)

        if not odd:
            e = l // 2
            xm = modulate(h, g[2], m_x[:, :, 3], m_x[:, :, 4])
            y = short_conv_fourier_mixer(xm, w_in_even[e], conv_w[e], w_out_even[e])
            h = h + m_x[:, :, 5] * rmsnorm(y, g[3])
            if ctx_live:
                xc = modulate(hc, g[2], m_c[:, :, 3], m_c[:, :, 4])
                yc = short_conv_fourier_mixer(xc, w_in_even[e], conv_w[e], w_out_even[e])
                hc = hc + m_c[:, :, 5] * rmsnorm(yc, g[3])
        else:
            o = l // 2
            lam_init = 0.8 - 0.6 * math.exp(-0.3 * l)
            lam = (jnp.exp(jnp.sum(lam_q1[o].astype(f32) * lam_k1[o].astype(f32)))
                   - jnp.exp(jnp.sum(lam_q2[o].astype(f32) * lam_k2[o].astype(f32))) + lam_init)
            w_in = w_in_odd[o]
            xm = modulate(h, g[2], m_x[:, :, 3], m_x[:, :, 4])
            xc = modulate(hc, g[2], m_c[:, :, 3], m_c[:, :, 4])
            u = xm @ w_in
            q_x = attn_queries(u[..., :Q_COLS], g_q_mla[o], w_uq[o], rope_da, rope_mla)
            kv_x = attn_keys_values(u[..., Q_COLS:], g_kv_mla[o], w_uk[o], w_uv[o], rope_da, rope_mla)
            kv_c = attn_keys_values(xc @ w_in[:, Q_COLS:], g_kv_mla[o], w_uk[o], w_uv[o], None, None)
            kv_all = tuple(jnp.concatenate([kc, kx], axis=1) for kc, kx in zip(kv_c, kv_x))
            o_da, o_m = attend_latent_blocks(q_x, kv_all, lam)
            y = attn_output(o_da, o_m, g_subln[o], lam_init, w_out_odd[o])
            if not last:
                q_c = attn_queries(xc @ w_in[:, :Q_COLS], g_q_mla[o], w_uq[o], None, None)
                oc_da, oc_m = attend(q_c[0], q_c[1], *kv_c, lam)
                yc = attn_output(oc_da, oc_m, g_subln[o], lam_init, w_out_odd[o])
                hc = hc + m_c[:, :, 5] * rmsnorm(yc, g[3])
            h = h + m_x[:, :, 5] * rmsnorm(y, g[3])

        h = macaron_ffn(h, m_x, g, w_ffn_in[l, 1], w_ffn_out[l, 1], 2)
        if not last:
            hc = macaron_ffn(hc, m_c, g, w_ffn_in[l, 1], w_ffn_out[l, 1], 2)
    return h


N_META = 16
BLOCK = 128
A_HEADS = 8
A_HEAD_DIM = 64
IDX_HEADS = 8
IDX_DIM = 64
TOPK_MAX = 256
N_BUCKETS = 32
MAX_DISTANCE = 128
B_HEADS = 4
B_QK_DIM = 128
B_V_DIM = 256
ROPE_BASE = 10000.0
C_HEADS = 16
C_HEAD_DIM = 64

A_Q = A_HEADS * A_HEAD_DIM
A_IQ = IDX_HEADS * IDX_DIM
B_QK = B_HEADS * B_QK_DIM
B_V = B_HEADS * B_V_DIM
EVEN_SPLITS = [A_Q, A_Q, A_Q, A_IQ, IDX_DIM, IDX_HEADS, B_QK, B_QK, B_V, B_V]
EVEN_IN = sum(EVEN_SPLITS)
EVEN_OUT = A_Q + B_V
C_W = C_HEADS * C_HEAD_DIM
ODD_IN = 3 * C_W


def rmsnorm_2(x, g):
    xf = x.astype(jnp.float32)
    y = xf * lax.rsqrt(jnp.mean(jnp.square(xf), axis=-1, keepdims=True) + EPS)
    return (y * g.astype(jnp.float32)).astype(x.dtype)

def t5_bucket(rel):
    n = jnp.maximum(rel, 0)
    max_exact = N_BUCKETS // 2
    large = max_exact + (jnp.log(jnp.maximum(n, 1).astype(jnp.float32) / max_exact)
                         / math.log(MAX_DISTANCE / max_exact)
                         * (N_BUCKETS - max_exact)).astype(jnp.int32)
    large = jnp.minimum(large, N_BUCKETS - 1)
    return jnp.where(n < max_exact, n, large)

def rotary(x, pos):
    half = x.shape[-1] // 2
    inv = 1.0 / (ROPE_BASE ** (jnp.arange(half, dtype=jnp.float32) / half))
    ang = pos.astype(jnp.float32)[:, None] * inv[None, :]
    cos = jnp.cos(ang)[:, None, :]
    sin = jnp.sin(ang)[:, None, :]
    xf = x.astype(jnp.float32)
    x1, x2 = xf[..., :half], xf[..., half:]
    return jnp.concatenate([x1 * cos - x2 * sin, x2 * cos + x1 * sin], axis=-1).astype(x.dtype)

def dsa_attention(q, k, v, qi, ki, wi, rel_bias, n_keep):
    Bsz, L = q.shape[:2]
    nblk = L // BLOCK
    kpos = jnp.arange(L)
    is_meta = kpos < N_META

    def block(args):
        qb, qib, wib, qpos = args
        s = jnp.einsum('bqhd,bkd->bqhk', qib, ki).astype(jnp.float32) * (IDX_DIM ** -0.5)
        score = jnp.einsum('bqhk,bqh->bqk', jax.nn.relu(s), wib.astype(jnp.float32))
        causal = kpos[None, :] <= qpos[:, None]
        score = jnp.where(causal[None], jnp.where(is_meta[None, None, :], jnp.inf, score), -jnp.inf)
        _, idx = lax.top_k(score, n_keep)
        gather = jax.vmap(lambda a, i: a[i])
        ksel = gather(k, idx)
        vsel = gather(v, idx)
        rel = qpos[None, :, None] - idx
        bias = jnp.moveaxis(rel_bias[t5_bucket(rel)], -1, 2)
        logits = jnp.einsum('bqhd,bqkhd->bqhk', qb, ksel).astype(jnp.float32) * (A_HEAD_DIM ** -0.5)
        logits = logits + bias.astype(jnp.float32)
        logits = jnp.where((rel >= 0)[:, :, None, :], logits, -jnp.inf)
        p = jax.nn.softmax(logits, axis=-1).astype(v.dtype)
        return jnp.einsum('bqhk,bqkhd->bqhd', p, vsel)

    to_blocks = lambda a: jnp.moveaxis(a.reshape(Bsz, nblk, BLOCK, *a.shape[2:]), 1, 0)
    out = lax.map(block, (to_blocks(q), to_blocks(qi), to_blocks(wi), kpos.reshape(nblk, BLOCK)))
    return jnp.moveaxis(out, 0, 1).reshape(Bsz, L, *q.shape[2:])

def retention(q, k, v):
    Bsz, L, H, dk = q.shape
    dv = v.shape[-1]
    C = BLOCK
    N = L // C
    lg = jnp.log(1.0 - 2.0 ** (-5.0 - jnp.arange(H, dtype=jnp.float32)))
    n = jnp.arange(C, dtype=jnp.float32)
    diff = n[:, None] - n[None, :]
    dmat = jnp.where(diff[None] >= 0, jnp.exp(jnp.maximum(diff, 0.0)[None] * lg[:, None, None]), 0.0)
    xi = jnp.exp((n[None, :] + 1.0) * lg[:, None])[..., None]
    zeta = jnp.exp((C - 1.0 - n[None, :]) * lg[:, None])[..., None]
    g_chunk = jnp.exp(C * lg)[:, None, None]
    chunks = lambda a: a.astype(jnp.float32).reshape(Bsz, N, C, H, a.shape[-1]).transpose(1, 0, 3, 2, 4)
    qc, kc, vc = chunks(q), chunks(k * (dk ** -0.5)), chunks(v)

    def step(R, inp):
        qi, ki, vi = inp
        inner = jnp.einsum('bhcd,bhed->bhce', qi, ki) * dmat
        o = jnp.einsum('bhce,bhef->bhcf', inner, vi) + jnp.einsum('bhcd,bhdf->bhcf', qi, R) * xi
        R = R * g_chunk + jnp.einsum('bhcd,bhcf->bhdf', ki * zeta, vi)
        return R, o

    R0 = jnp.zeros((Bsz, H, dk, dv), jnp.float32)
    _, o = lax.scan(step, R0, (qc, kc, vc))
    return o.transpose(1, 0, 3, 2, 4).reshape(Bsz, L, H, dv)

def stick_breaking(q, k, v):
    L = q.shape[1]
    scale = q.shape[-1] ** -0.5
    outs = []
    for i in range(L // BLOCK):
        s, e = i * BLOCK, (i + 1) * BLOCK
        z = jnp.einsum('bqhd,bkhd->bhqk', q[:, s:e], k[:, :e]).astype(jnp.float32) * scale
        mask = (jnp.arange(e)[None, :] < jnp.arange(s, e)[:, None])[None, None]
        log_1m = jnp.where(mask, jax.nn.log_sigmoid(-z), 0.0)
        rest = lax.cumsum(log_1m, axis=3, reverse=True) - log_1m
        a = jnp.where(mask, jnp.exp(jax.nn.log_sigmoid(z) + rest), 0.0)
        outs.append(jnp.einsum('bhqk,bkhd->bqhd', a.astype(v.dtype), v[:, :e]))
    return jnp.concatenate(outs, axis=1)

def even_mixer(h, w_in, gn_gain, w_out, rel_bias, n_keep):
    Bsz, L, _ = h.shape
    p = h @ w_in
    splits = [int(s) for s in np.cumsum(EVEN_SPLITS)[:-1]]
    aq, ak, av, iq, ik, iw, bq, bk, bv, bg = jnp.split(p, splits, axis=-1)
    heads = lambda t, nh: t.reshape(Bsz, L, nh, -1)
    a_out = dsa_attention(heads(aq, A_HEADS), heads(ak, A_HEADS), heads(av, A_HEADS),
                          heads(iq, IDX_HEADS), ik, iw * (IDX_HEADS ** -0.5), rel_bias, n_keep)
    a_out = a_out.reshape(Bsz, L, A_Q)
    pos = jnp.arange(L)
    bq = rotary(heads(bq, B_HEADS), pos)
    bk = rotary(heads(bk, B_HEADS), pos)
    lead = (-N_META) % BLOCK
    frame = lambda t: jnp.pad(t[:, :L - lead], ((0, 0), (lead, 0), (0, 0), (0, 0)))
    r = retention(frame(bq), frame(bk), frame(heads(bv, B_HEADS)))
    r = jnp.pad(r[:, lead:], ((0, 0), (0, lead), (0, 0), (0, 0)))
    mu = jnp.mean(r, axis=-1, keepdims=True)
    var = jnp.mean(jnp.square(r - mu), axis=-1, keepdims=True)
    r = ((r - mu) * lax.rsqrt(var + EPS)).reshape(Bsz, L, B_V) * gn_gain.astype(jnp.float32)
    r_out = (r * jax.nn.silu(bg.astype(jnp.float32))).astype(h.dtype)
    return jnp.concatenate([a_out, r_out], axis=-1) @ w_out

def odd_mixer(h, w_in, w_out):
    Bsz, L, _ = h.shape
    q, k, v = jnp.split(h @ w_in, 3, axis=-1)
    heads = lambda t: t.reshape(Bsz, L, C_HEADS, C_HEAD_DIM)
    return stick_breaking(heads(q), heads(k), heads(v)).reshape(Bsz, L, C_W) @ w_out

def conv_ffn(h, w_up, w_gate, conv_w, conv_b, w_down):
    u = h @ w_up
    g = h @ w_gate
    g = lax.conv_general_dilated(g, conv_w[:, None, :].astype(g.dtype), window_strides=(1,),
                                 padding=[(CONV_WIDTH - 1, 0)],
                                 dimension_numbers=('NWC', 'WIO', 'NWC'),
                                 feature_group_count=D_FF) + conv_b
    return (jax.nn.silu(g) * u) @ w_down

def second_inputs(seed: int = 0) -> dict:
    key = jax.random.key(seed)
    ks = jax.random.split(key, 20)
    f32 = jnp.float32
    ne, no = (DEPTH + 1) // 2, DEPTH // 2
    nrm = lambda k, shape, fan_in: jax.random.normal(k, shape, f32) * (fan_in ** -0.5)
    gain = lambda k, shape: 1.0 + 0.05 * jax.random.normal(k, shape, f32)
    return {
        "x": jax.random.normal(ks[0], (BATCH, SEQ, D_MODEL), f32),
        "meta_tokens": jax.random.normal(ks[1], (N_META, D_MODEL), f32),
        "rel_bias": 0.5 * jax.random.normal(ks[2], (N_BUCKETS, A_HEADS), f32),
        "norm_mix": gain(ks[3], (DEPTH, D_MODEL)),
        "norm_ffn": gain(ks[4], (DEPTH, D_MODEL)),
        "norm_final": gain(ks[5], (D_MODEL,)),
        "even_w_in": nrm(ks[6], (ne, D_MODEL, EVEN_IN), D_MODEL),
        "even_gn_gain": gain(ks[7], (ne, B_V)),
        "even_w_out": nrm(ks[8], (ne, EVEN_OUT, D_MODEL), EVEN_OUT),
        "odd_w_in": nrm(ks[9], (no, D_MODEL, ODD_IN), D_MODEL),
        "odd_w_out": nrm(ks[10], (no, C_W, D_MODEL), C_W),
        "ffn_w_up": nrm(ks[11], (DEPTH, D_MODEL, D_FF), D_MODEL),
        "ffn_w_gate": nrm(ks[12], (DEPTH, D_MODEL, D_FF), D_MODEL),
        "ffn_conv_w": nrm(ks[13], (DEPTH, CONV_WIDTH, D_FF), CONV_WIDTH),
        "ffn_conv_b": 0.01 * jax.random.normal(ks[14], (DEPTH, D_FF), f32),
        "ffn_w_down": nrm(ks[15], (DEPTH, D_FF, D_MODEL), D_FF),
    }

def second_block(x, meta_tokens, rel_bias, norm_mix, norm_ffn, norm_final,
              even_w_in, even_gn_gain, even_w_out, odd_w_in, odd_w_out,
              ffn_w_up, ffn_w_gate, ffn_conv_w, ffn_conv_b, ffn_w_down):
    Bsz, S, D = x.shape
    lead = (-N_META) % BLOCK
    n_keep = min(TOPK_MAX, S // 4)
    meta = jnp.broadcast_to(meta_tokens[None].astype(x.dtype), (Bsz, N_META, D))
    h = jnp.concatenate([meta, x, jnp.zeros((Bsz, lead, D), x.dtype)], axis=1)
    for l in range(DEPTH):
        hn = rmsnorm_2(h, norm_mix[l])
        if l % 2 == 0:
            j = l // 2
            h = h + even_mixer(hn, even_w_in[j], even_gn_gain[j], even_w_out[j], rel_bias, n_keep)
        else:
            j = l // 2
            h = h + odd_mixer(hn, odd_w_in[j], odd_w_out[j])
        h = h + conv_ffn(rmsnorm_2(h, norm_ffn[l]), ffn_w_up[l], ffn_w_gate[l],
                         ffn_conv_w[l], ffn_conv_b[l], ffn_w_down[l])
    return rmsnorm_2(h, norm_final)[:, N_META:N_META + S]


def setup_inputs(seed=0):
    out = dict(first_inputs(seed))
    for name, value in second_inputs(seed + 1).items():
        if name != "x":
            out[name + "_2"] = value
    return out


def reference(
    x, c, ctx, c_ctx, w_mod, b_mod, norm_g, w_ffn_in, w_ffn_out, w_in_even, conv_w, w_out_even,
    w_in_odd, g_q_mla, w_uq, g_kv_mla, w_uk, w_uv, lam_q1, lam_k1, lam_q2, lam_k2, g_subln,
    w_out_odd, meta_tokens_2, rel_bias_2, norm_mix_2, norm_ffn_2, norm_final_2, even_w_in_2,
    even_gn_gain_2, even_w_out_2, odd_w_in_2, odd_w_out_2, ffn_w_up_2, ffn_w_gate_2,
    ffn_conv_w_2, ffn_conv_b_2, ffn_w_down_2,
):
    x = first_block(
        x, c, ctx, c_ctx, w_mod, b_mod, norm_g, w_ffn_in, w_ffn_out, w_in_even, conv_w,
        w_out_even, w_in_odd, g_q_mla, w_uq, g_kv_mla, w_uk, w_uv, lam_q1, lam_k1, lam_q2,
        lam_k2, g_subln, w_out_odd,
    )
    return second_block(
        x, meta_tokens_2, rel_bias_2, norm_mix_2, norm_ffn_2, norm_final_2, even_w_in_2,
        even_gn_gain_2, even_w_out_2, odd_w_in_2, odd_w_out_2, ffn_w_up_2, ffn_w_gate_2,
        ffn_conv_w_2, ffn_conv_b_2, ffn_w_down_2,
    )


_drawn_inputs = setup_inputs


def setup_inputs(seed=0):
    import zlib

    import numpy as np

    out = dict(_drawn_inputs(seed))
    spreads = {}
    factors = {'g_q_mla': 8.0,
     'g_kv_mla': 5.638,
     'lam_q2': 14.482,
     'ffn_conv_b_2': 8.0,
     'lam_q1': 3.253,
     'lam_k2': 3.877,
     'g_subln': 8.0}
    for name, (base, spread) in spreads.items():
        noise = np.random.default_rng([zlib.crc32(name.encode()), seed]).standard_normal(out[name].shape)
        drawn = base * np.exp(spread * noise) if base else spread * noise
        out[name] = jnp.asarray(drawn.astype(out[name].dtype))
    for name, factor in factors.items():
        out[name] = (out[name] * factor).astype(out[name].dtype)
    return out
```

```python
from contextlib import ExitStack

import concourse.bass as bass
from concourse import mybir

ALU = mybir.AluOpType
ACT = mybir.ActivationFunctionType
F32 = mybir.dt.float32
AX_X = mybir.AxisListType.X

P = 128
D = 1024
KD = D // P
SEQ = 256
CTX = 256
TB = SEQ + CTX
META = 16
T2 = META + SEQ
DFF = 2816
KF = DFF // P
EPS = 1e-6
NEG = -1e30
TAKEN = -3e38
BANK = 512
SLOTS = 6
KG = 8

DA_HEADS, DA_DK, DA_DV = 8, 64, 128
MLA_HEADS, MLA_NOPE, MLA_ROPE, MLA_DV = 8, 64, 32, 64
MLA_DQK = MLA_NOPE + MLA_ROPE
DA_SCALE = DA_DK ** -0.5
MLA_SCALE = MLA_DQK ** -0.5
Q_COLS = 1024 + 384
LAM_INIT = 0.8 - 0.6 * 2.718281828459045 ** -0.3
DSA_HEADS, DSA_D = 8, 64
KEEP = min(256, SEQ // 4)
RET_HEADS, RET_DK, RET_DV = 4, 128, 256
SB_HEADS, SB_D = 16, 64
BIAS_W = 400


class Count:

    def __init__(self, sem):
        self.sem, self.n = sem, 0


def chained(eng, ins, count):
    ins.then_inc(count.sem, 1)
    count.n += 1
    eng.wait_ge(count.sem, count.n)


def signal(ins, count):
    ins.then_inc(count.sem, 1)
    count.n += 1


class Gemm:

    def __init__(self, name, K, sources, half=P, last=None):
        self.name, self.kt = name, K // P
        self.groups = -(-self.kt // KG)
        self.pairs = sources
        self.half = half
        self.last = last or (half, half)
        self.units = len(sources) * self.groups
        self.per_rot = SLOTS // self.groups
        self.full = (len(sources) - (last is not None)) // self.per_rot

    def widths(self, p):
        return self.last if p == len(self.pairs) - 1 else (self.half, self.half)

    def source(self, unit, rot=0):
        pair, g = unit // self.groups, unit % self.groups
        w, c0 = self.pairs[pair]
        width = sum(self.widths(pair))
        k0, kn = g * KG, min(KG, self.kt - g * KG)
        rows = w[k0 * P:(k0 + kn) * P, :].rearrange("(k p) n -> p k n", p=P)
        if isinstance(rot, int) and rot == 0:
            return rows[:, :, c0:c0 + width], kn, width
        step = self.pairs[pair + self.per_rot][1] - c0
        return rows[:, :, bass.ds(rot * step + c0, width)], kn, width


def finish(nc, a, out, H, XM, Y, sqf, stored, transposes, ctx, src=None):
    src = src or H
    tok = Y[:, :, :].rearrange("p a b -> p (a b)")[:, 0:2 * D].rearrange("p (t n) -> p t n", t=2)
    transposes([([src[:, 4 * h + j, META + t * P:META + (t + 1) * P] for j in range(4)], P, P,
                 tok[:, t, 4 * h * P:4 * (h + 1) * P].rearrange("p (j c) -> p j c", j=4)) for t in range(2) for h in range(2)])
    with nc.Block() as block:
        @block.sync
        def _(sp):
            sp.dma_start(out[0].rearrange("(t p) n -> p t n", p=P), tok).then_inc(stored.sem, 16)
            stored.n += 16
            sp.wait_ge(stored.sem, stored.n)


def build(nc, a, out, bias_rows):
    ctx = ExitStack()
    with ctx:
        def sb(name, shape):
            return ctx.enter_context(nc.sbuf_tensor(name, shape, F32))

        def sem(name):
            return Count(ctx.enter_context(nc.semaphore(name)))

        H = sb("H", [P, KD, T2 + CTX])
        XM = sb("XM", [P, KD, TB])
        Y = sb("Y", [P, KD, TB])
        SQ = sb("SQ", [P, KD, 2 * T2])
        GU = sb("GU", [P, KF * TB])
        EX = sb("EX", [P, 6144])
        ring = sb("ring", [P, SLOTS, KG, 256])
        ident = sb("ident", [P, P])
        ones = sb("ones", [P, P])
        swap = sb("swap", [P, 3, P])
        tri = sb("tri", [P, 3, P])
        kb = sb("kb", [P, 2304])
        dft1 = kb[:, 0:256]
        dft2 = kb[:, 256:1280].rearrange("p (t c n) -> p t c n", t=2, c=2)
        rope_da = kb[:, 1280:1792].rearrange("p (c t) -> p c t", c=2)
        rope_mla = kb[:, 1792:2304].rearrange("p (c t) -> p c t", c=2)
        rope_ret = kb[:, 0:2 * T2].rearrange("p (c t) -> p c t", c=2)
        decay = kb[:, 2 * T2:6 * T2].rearrange("p (h t) -> p h t", h=RET_HEADS)
        prm = sb("prm", [P, 5, P])
        cs = sb("cs", [P, KD, 2])
        mod = sb("mod", [P, 72, 2])
        co = sb("co", [P, 9, KD, 2])
        std = sb("std", [P, TB])
        rstd = sb("rstd", [P, TB])
        epsb = sb("epsb", [P, 1])
        lam4 = sb("lam4", [1, 4, 64])
        lamv = sb("lamv", [1, 8])
        nlam = sb("nlam", [P, 2])
        gsub = sb("gsub", [P, 1])
        small = sb("small", [P, 64])
        ps = ctx.enter_context(nc.psum_tensor("ps", [P, 8, BANK], F32))

        loaded = sem("loaded")
        slot_loaded = [sem(f"slot_loaded{i}") for i in range(SLOTS)]
        w_used = sem("w_used")
        first_done = sem("first_done")
        act_freed = sem("act_freed")
        dve_freed = sem("dve_freed")
        conv_step = sem("conv_step")
        conv_done = sem("conv_done")
        silu_done = sem("silu_done")
        dve_step, act_step, pool_step, pe_step = (sem(x) for x in ("dve_step", "act_step", "pool_step", "pe_step"))
        sq_ready = sem("sq_ready")
        sum_ready = sem("sum_ready")
        std_ready = sem("std_ready")
        scaled = sem("scaled")
        pe_out = sem("pe_out")
        act_out = sem("act_out")
        dve_out = sem("dve_out")
        pe_out2 = sem("pe_out2")
        pe_out3 = sem("pe_out3")
        dve_out3 = sem("dve_out3")
        act_out2 = sem("act_out2")
        dve_out2 = sem("dve_out2")
        stored = sem("stored")

        def g_col(layer, i, k):
            return prm[:, 0, layer * 48 + i * 8 + k:layer * 48 + i * 8 + k + 1]

        def cols(w, c0, n):
            return [(w, c0 + 256 * i) for i in range(n)]

        def gate_up(wg, g0, wu, u0):
            return [x for j in range(DFF // 256) for x in ((wg, g0 + 256 * j), (wu, u0 + 256 * j))]

        def mod_gemm(layer):
            return Gemm(f"mod{layer}", D, cols(a["w_mod"][layer], 0, 36))

        def ffn_gemms(layer, s):
            w = a["w_ffn_in"][layer, s]
            return [Gemm("ffn_in", D, gate_up(w, 0, w, DFF)), Gemm("ffn_out", DFF, cols(a["w_ffn_out"][layer, s], 0, 4))]

        def ffn2_gemms(layer):
            return [Gemm("ffn2_in", D, gate_up(a["ffn_w_gate_2"][layer], 0, a["ffn_w_up_2"][layer], 0)),
                    Gemm("ffn2_out", DFF, cols(a["ffn_w_down_2"][layer], 0, 4))]

        w_in_odd = a["w_in_odd"][0]
        w_in_2 = a["even_w_in_2"][0]
        plan = [mod_gemm(0), *ffn_gemms(0, 0),
                Gemm("even_in", D, cols(a["w_in_even"][0], 0, 8)),
                Gemm("even_out", D, cols(a["w_out_even"][0], 0, 4)), *ffn_gemms(0, 1),
                mod_gemm(1), *ffn_gemms(1, 0),
                Gemm("odd_q", D, cols(w_in_odd, 0, 6), last=(P, 0)),
                Gemm("odd_kv", D, cols(w_in_odd, Q_COLS, 10), last=(MLA_ROPE, 0)),
                Gemm("uq", 384, [(a["w_uq"][0], 192 * i) for i in range(4)], half=MLA_DQK),
                Gemm("uk", 256, [(a["w_uk"][0], 128 * i) for i in range(4)], half=MLA_NOPE),
                Gemm("uv", 256, cols(a["w_uv"][0], 0, 2)),
                Gemm("odd_out", 1536, cols(a["w_out_odd"][0], 0, 4)), *ffn_gemms(1, 1),
                Gemm("even2_a", D, cols(w_in_2, 0, 8)),
                Gemm("even2_i", D, [(w_in_2, 2048)], last=(64, 8)),
                Gemm("even2_b", D, cols(w_in_2, 2120, 12)),
                Gemm("even2_out", 1536, cols(a["even_w_out_2"][0], 0, 4)), *ffn2_gemms(0),
                Gemm("odd2_in", D, cols(a["odd_w_in_2"][0], 0, 12)),
                Gemm("odd2_out", D, cols(a["odd_w_out_2"][0], 0, 4)), *ffn2_gemms(1)]
        first_unit = [0]
        for g in plan:
            first_unit.append(first_unit[-1] + g.units)
        at = [0]

        def load_unit(sp, g, unit, n, rot=0, turn=0):
            src, kn, width = g.source(unit, rot)
            slot = n % SLOTS
            if n >= SLOTS or not isinstance(turn, int):
                sp.wait_ge(w_used.sem, turn * SLOTS + n - SLOTS + 1)
            sp.dma_start(ring[:, slot, 0:kn, 0:width], src).then_inc(slot_loaded[slot].sem, 16)

        def load_ahead(sp, p):
            lo, hi = first_unit[p] + SLOTS, min(first_unit[p + 1] + SLOTS, first_unit[-1])
            g, base = plan[p], first_unit[p]
            n = lo
            if g.full > 2:
                with sp.Fori(1, g.full) as r:
                    for i in range(SLOTS):
                        load_unit(sp, g, i, base + i, rot=r, turn=r)
                n = base + SLOTS * g.full
            while n < hi:
                q = max(i for i in range(len(plan)) if first_unit[i] <= n)
                load_unit(sp, plan[q], n - first_unit[q], n)
                n += 1

        def rotations(eng, g, body):
            def run(r, first=False):
                for i in range(g.per_rot):
                    body(i, r, first)
            done = 1 if g.full > 0 else 0
            if done:
                run(0, True)
            if g.full > 2:
                with eng.Fori(1, g.full) as r:
                    run(r)
                done = g.full
            for p in range(done * g.per_rot, len(g.pairs)):
                body(p % g.per_rot, p // g.per_rot, p < g.per_rot)

        def product(rhs, T, evac, group=1):
            p = at[0]
            at[0] += 1
            g, base = plan[p], first_unit[p]
            assert w_used.n == base
            NB = 4 if (g.groups == 3 or group == 2) else 6
            fb, ab, db = first_done.n, act_freed.n, dve_freed.n

            def owner(i):
                return "act" if i % (2 * group) < group else "dve"

            def order(i):
                return i // (2 * group) * group + i % group

            def widths(i, r):
                return g.widths(r * g.per_rot + i) if isinstance(r, int) else (g.half, g.half)

            class Tile:
                def __init__(self, i, r, m):
                    t = 2 * i + m
                    self.t, self.m, self.w = r * (2 * g.per_rot) + t, m, widths(i, r)[m]
                    self.owner = owner(t)
                    self.src = ps[0:self.w, t % NB:t % NB + 1, 0:T]
                    self.first = isinstance(r, int) and r == 0
                    self.n = r * g.per_rot + order(t)
                    self.local = order(t)
                    alone = widths(i, r)[1] == 0
                    if m == 0 and not alone:
                        self.ready = (first_done, r * g.per_rot + fb + i + 1)
                    else:
                        self.ready = (w_used, r * SLOTS + base + (i + 1) * g.groups)

                def wait(self, eng):
                    eng.wait_ge(self.ready[0].sem, self.ready[1])

            with nc.Block() as block:
                @block.sync
                def _(sp):
                    load_ahead(sp, p)

                @block.tensor
                def _(pe):
                    def pair(i, r, first):
                        w = widths(i, r)
                        for gr in range(g.groups):
                            n = base + i * g.groups + gr
                            slot = n % SLOTS
                            pe.wait_ge(slot_loaded[slot].sem, 16 * r + 16 * (n // SLOTS + 1))
                            kn = min(KG, g.kt - gr * KG)
                            for m in range(2 if w[1] else 1):
                                t = 2 * i + m
                                if gr == 0 and not (first and t < NB):
                                    freed, b0 = (act_freed, ab) if owner(t) == "act" else (dve_freed, db)
                                    pe.wait_ge(freed.sem, r * g.per_rot + b0 + order(t) - order(NB) + 1)
                                for k in range(kn):
                                    mm = pe.matmul(ps[0:w[m], t % NB, 0:T],
                                                   ring[:, slot, k, m * w[0]:m * w[0] + w[m]],
                                                   rhs(gr * KG + k), start=(gr == 0 and k == 0),
                                                   stop=(gr == g.groups - 1 and k == kn - 1))
                                if m == 0 and w[1] and gr == g.groups - 1:
                                    mm.then_inc(first_done.sem, 1)
                            mm.then_inc(w_used.sem, 1)
                    rotations(pe, g, pair)

                def evacuate(eng, who):
                    def pair(i, r, first):
                        tiles = [Tile(i, r, m) for m in range(2) if widths(i, r)[m]]
                        for tile in tiles:
                            evac(eng, tile.owner == who, tile)
                    rotations(eng, g, pair)

                @block.scalar
                def _(act):
                    evacuate(act, "act")

                @block.vector
                def _(dve):
                    evacuate(dve, "dve")

            w_used.n += g.units
            tiles = [(p_, m) for p_ in range(len(g.pairs)) for m in range(2) if g.widths(p_)[m]]
            first_done.n += sum(1 for p_ in range(len(g.pairs)) if g.widths(p_)[1])
            act_freed.n += sum(owner(2 * p_ + m) == "act" for p_, m in tiles)
            dve_freed.n += sum(owner(2 * p_ + m) == "dve" for p_, m in tiles)
            return ab, db

        def copy_out(dest):
            def evac(eng, mine, tile):
                if not mine:
                    return
                tile.wait(eng)
                if tile.owner == "act":
                    eng.activation(dest(tile), tile.src, ACT.Copy).then_inc(act_freed.sem, 1)
                else:
                    eng.tensor_copy(dest(tile), tile.src).then_inc(dve_freed.sem, 1)
            return evac

        def into(buf, first_tile=0, T=TB):
            return lambda tile: buf[0:tile.w, bass.ds(tile.t + first_tile, 1), 0:T]

        def adaln(layer):
            p = at[0]
            at[0] += 1
            g, base = plan[p], first_unit[p]
            out_cols = ps[:, 6, 0:144]
            with nc.Block() as block:
                @block.sync
                def _(sp):
                    load_ahead(sp, p)

                @block.tensor
                def _(pe):
                    def pair(i, r, first):
                        n = base + i
                        slot = n % SLOTS
                        pe.wait_ge(slot_loaded[slot].sem, 16 * r + 16 * (n // SLOTS + 1))
                        for m in range(2):
                            for k in range(KD):
                                mm = pe.matmul(ps[:, 6, bass.ds(r * (4 * g.per_rot) + 4 * i + 2 * m, 2)],
                                               ring[:, slot, k, m * P:(m + 1) * P], cs[:, k, :],
                                               start=(k == 0), stop=(k == KD - 1))
                        mm.then_inc(w_used.sem, 1)
                    rotations(pe, g, pair)

                @block.vector
                def _(dve):
                    dve.wait_ge(w_used.sem, base + g.units)
                    m72 = out_cols.rearrange("p (t s) -> p t s", s=2)
                    for s in range(2):
                        ins = dve.tensor_tensor(mod[:, :, s], m72[:, :, s], prm[:, 1 + layer, 0:72], ALU.add)
                        chained(dve, ins, dve_step)
                    for slot in range(3):
                        pre = prm[:, 0, layer * 48 + 16 * slot:layer * 48 + 16 * slot + 8]
                        post = prm[:, 0, layer * 48 + 16 * slot + 8:layer * 48 + 16 * slot + 16]
                        for s in range(2):
                            m = [mod[:, (3 * slot + j) * 8:(3 * slot + j + 1) * 8, s] for j in range(3)]
                            signal(dve.scalar_tensor_tensor(co[:, 3 * slot, :, s], m[1], 1.0, pre, ALU.add, ALU.mult), dve_step)
                            signal(dve.tensor_copy(co[:, 3 * slot + 1, :, s], m[0]), dve_step)
                            signal(dve.scalar_tensor_tensor(co[:, 3 * slot + 2, :, s], m[2], 1.0 if slot == 1 else 0.5, post,
                                                            ALU.mult, ALU.mult), dve_step)
            w_used.n += g.units

        def norm(src, Kt, T, dve_part, act_part=None, sumsq=True, dim=None, parts=P):
            dim = dim or Kt * P
            qb, mb, tb_ = sq_ready.n, sum_ready.n, std_ready.n
            with nc.Block() as block:
                @block.scalar
                def _(act):
                    for k in range(Kt):
                        act.activation(SQ[0:parts, k, 0:T], src(k), ACT.Square).then_inc(sq_ready.sem, 1)
                    act.wait_ge(sum_ready.sem, mb + 1)
                    act.activation(std[:, 0:T], ps[:, 7, 0:T], ACT.Sqrt, bias=epsb[:, 0:1], scale=1.0 / dim).then_inc(std_ready.sem, 1)
                    if act_part:
                        act_part(act)

                @block.tensor
                def _(pe):
                    for k in range(Kt):
                        pe.wait_ge(sq_ready.sem, qb + k + 1)
                        mm = pe.matmul(ps[:, 7, 0:T], ones[0:parts, :], SQ[0:parts, k, 0:T], start=(k == 0), stop=(k == Kt - 1))
                    mm.then_inc(sum_ready.sem, 1)

                @block.vector
                def _(dve):
                    dve.wait_ge(std_ready.sem, tb_ + 1)
                    chained(dve, dve.reciprocal(rstd[:, 0:T], std[:, 0:T]), dve_step)
                    dve_part(dve)
            sq_ready.n += Kt
            sum_ready.n += 1
            std_ready.n += 1

        def streams(T):
            return [(0, SEQ, 0)] + ([(SEQ, TB, 1)] if T == TB else [])

        def h1(k, T=TB):
            return H[:, k, META:META + T]

        def modulate(slot, T=TB):
            b = scaled.n

            def dve_part(dve):
                for k in range(KD):
                    dve.tensor_tensor(SQ[:, k, 0:T], h1(k, T), rstd[:, 0:T], ALU.mult).then_inc(scaled.sem, 1)

            def act_part(act):
                for k in range(KD):
                    act.wait_ge(scaled.sem, b + k + 1)
                    for lo, hi, s in streams(T):
                        act.activation(XM[:, k, lo:hi], SQ[:, k, lo:hi], ACT.Identity,
                                       bias=co[:, 3 * slot + 1, k, s:s + 1], scale=co[:, 3 * slot, k, s:s + 1])
            norm(lambda k: h1(k, T), KD, T, dve_part, act_part)
            scaled.n += KD

        def residual(slot, T=TB, src=None):
            src = src or Y

            def dve_part(dve):
                for k in range(KD):
                    dve.tensor_tensor(SQ[:, k, 0:T], src[:, k, 0:T], rstd[:, 0:T], ALU.mult).then_inc(dve_step.sem, 1)
                    dve_step.n += 1
                b = dve_step.n - KD
                for k in range(KD):
                    dve.wait_ge(dve_step.sem, b + k + 1)
                    for lo, hi, s in streams(T):
                        dve.scalar_tensor_tensor(h1(k)[:, lo:hi], SQ[:, k, lo:hi], co[:, 3 * slot + 2, k, s:s + 1],
                                                 h1(k)[:, lo:hi], ALU.mult, ALU.add)
            norm(lambda k: src[:, k, 0:T], KD, T, dve_part)

        def gained(gain, src, dst, Kt, T, dim=None):
            def dve_part(dve):
                for k in range(Kt):
                    dve.scalar_tensor_tensor(dst(k), src(k), gain(k), rstd[:, 0:T], ALU.mult, ALU.mult)
            norm(src, Kt, T, dve_part, dim=dim)

        def transposes(groups):
            pb, ab, db = pe_out.n, act_out.n, dve_out.n
            with nc.Block() as block:
                @block.tensor
                def _(pe):
                    for n, (srcs, rows, width, dst) in enumerate(groups):
                        if n >= 8:
                            pe.wait_ge((act_out, dve_out)[n % 2].sem, (ab, db)[n % 2] + (n - 8) // 2 + 1)
                        for j, src in enumerate(srcs):
                            kp = src.shape[0]
                            mm = pe.transpose(ps[0:rows, n % 8, j * width:j * width + kp], src, ident[0:kp, 0:kp])
                        mm.then_inc(pe_out.sem, 1)

                def copies(eng, who, count):
                    for n, (srcs, rows, width, dst) in enumerate(groups):
                        if n % 2 != who:
                            continue
                        eng.wait_ge(pe_out.sem, pb + n + 1)
                        src = ps[0:rows, n % 8, 0:len(srcs) * width].rearrange("p (j c) -> p j c", j=len(srcs))[:, :, 0:srcs[0].shape[0]]
                        if who == 0:
                            eng.activation(dst, src, ACT.Copy).then_inc(count.sem, 1)
                        else:
                            eng.tensor_copy(dst, src).then_inc(count.sem, 1)

                @block.scalar
                def _(act):
                    copies(act, 0, act_out)

                @block.vector
                def _(dve):
                    copies(dve, 1, dve_out)
            pe_out.n += len(groups)
            act_out.n += (len(groups) + 1) // 2
            dve_out.n += len(groups) // 2

        gu = GU[:, :].rearrange("p (k t) -> p k t", t=TB)

        def ffn(slot, T=TB):
            modulate(slot, T)
            hold = SQ[:, 0:6, 0:TB]
            ab, db = act_freed.n, dve_freed.n

            def evac(eng, mine, tile):
                if not mine:
                    return
                j = tile.local
                tile.wait(eng)
                if tile.owner == "act":
                    if not tile.first:
                        eng.wait_ge(dve_freed.sem, tile.n + db - 5)
                    eng.activation(hold[:, j:j + 1, 0:T], tile.src, ACT.Silu).then_inc(act_freed.sem, 1)
                else:
                    eng.wait_ge(act_freed.sem, tile.n + ab + 1)
                    eng.tensor_tensor(gu[:, bass.ds(tile.n, 1), 0:T], hold[:, j:j + 1, 0:T], tile.src, ALU.mult).then_inc(dve_freed.sem, 1)
            product(lambda k: XM[:, k, 0:T], T, evac, group=2)
            product(lambda k: gu[:, k, 0:T], T, copy_out(into(Y, 0, T)))
            residual(slot, T)

        sqf = SQ[:, :, :].rearrange("p a b -> p (a b)")
        xmf = XM[:, :, :].rearrange("p a b -> p (a b)")
        yf = Y[:, :, :].rearrange("p a b -> p (a b)")
        raw = xmf[:, 0:5 * P].rearrange("p (i n) -> p i n", i=5)
        tok = yf.rearrange("p (t n) -> p t n", t=4)
        meta_tok = sqf[0:META, 0:D]
        onehot, relb, brow = EX[0:32, 0:BIAS_W], EX[0:32, 512:520], EX[0:8, 1024:1024 + BIAS_W]
        rows = lambda ap, n: ap.rearrange("(r p) -> r p", p=P) if n == 1 else ap.rearrange("a (r p) -> (a r) p", p=P)
        row_list = [
            (0, 0, a["norm_g"].rearrange("l i (r p) -> (l i r) p", p=P), 96),
            (0, 96, rows(a["c"], 2), 8), (0, 104, rows(a["c_ctx"], 1), 8),
            (1, 0, rows(a["b_mod"][0:1], 2), 72), (1, 72, rows(a["g_q_mla"], 2), 3), (1, 75, rows(a["g_kv_mla"], 2), 2),
            (1, 77, rows(a["g_subln"], 2), 1), (1, 78, rows(a["conv_w"][0], 2), 12),
            (2, 0, rows(a["b_mod"][1:2], 2), 72), (2, 72, rows(a["norm_mix_2"], 2), 16), (2, 88, rows(a["norm_ffn_2"], 2), 16),
            (2, 104, rows(a["norm_final_2"], 1), 8), (2, 112, rows(a["even_gn_gain_2"], 2), 8),
            (3, 0, rows(a["ffn_conv_w_2"][0], 2), 66), (3, 66, rows(a["ffn_conv_b_2"][0:1], 2), 22),
            (4, 0, rows(a["ffn_conv_w_2"][1], 2), 66), (4, 66, rows(a["ffn_conv_b_2"][1:2], 2), 22)]
        row_counts = [112, 90, 120, 88, 88]
        first_loads = [
            (ident[:, :], a["k_ident"]), (ones[:, :], a["k_ones"]), (swap[:, :, :], a["k_swap"]), (tri[:, :, :], a["k_tri"]),
            (kb[:, :], a["k_first"]), (onehot, a["k_bucket"]), (relb, a["rel_bias_2"]),
            (tok[:, 0:2, :], a["x"][0].rearrange("(t p) n -> p t n", p=P)),
            (tok[:, 2:4, :], a["ctx"][0].rearrange("(t p) n -> p t n", p=P)), (meta_tok, a["meta_tokens_2"]),
            (lam4[:, 0, :], a["lam_q1"]), (lam4[:, 1, :], a["lam_k1"]), (lam4[:, 2, :], a["lam_q2"]), (lam4[:, 3, :], a["lam_k2"]),
            *[(raw[r:r + n, i, :], src) for i, r, src, n in row_list]]
        with nc.Block() as block:
            @block.sync
            def _(sp):
                for dst, src in first_loads:
                    sp.dma_start(dst, src).then_inc(loaded.sem, 16)
                for n in range(SLOTS):
                    q = max(i for i in range(len(plan)) if first_unit[i] <= n)
                    load_unit(sp, plan[q], n - first_unit[q], n)
                sp.wait_ge(loaded.sem, 16 * len(first_loads))

            @block.gpsimd
            def _(pool):
                pool.memset(epsb[:, :], EPS)
        loaded.n += 16 * len(first_loads)

        transposes([([raw[0:n, i, :]], P, P, prm[:, i:i + 1, 0:n]) for i, n in enumerate(row_counts)]
                   + [([tok[:, t, (4 * h + j) * P:(4 * h + j + 1) * P] for j in range(4)], P, P,
                       H[:, 4 * h:4 * h + 4, META + t * P:META + (t + 1) * P]) for t in range(4) for h in range(2)]
                   + [([meta_tok[:, (4 * h + j) * P:(4 * h + j + 1) * P] for j in range(4)], P, P,
                       H[:, 4 * h:4 * h + 4, 0:META]) for h in range(2)])

        ab, db, pb = act_out.n, dve_out.n, pe_out.n
        with nc.Block() as block:
            @block.tensor
            def _(pe):
                pe.matmul(ps[0:8, 0, 0:BIAS_W], relb, onehot, start=True, stop=True).then_inc(pe_out.sem, 1)
                pe.wait_ge(dve_out.sem, db + 2)
                pe.matmul(ps[:, 1, 0:2], ones[0:1, :], lamv[:, 4:6], start=True, stop=True).then_inc(pe_out.sem, 1)

            @block.vector
            def _(dve):
                dve.tensor_tensor(lam4[:, 0, :], lam4[:, 0, :], lam4[:, 1, :], ALU.mult)
                chained(dve, dve.tensor_tensor(lam4[:, 2, :], lam4[:, 2, :], lam4[:, 3, :], ALU.mult), dve_step)
                dve.tensor_reduce(lamv[:, 0:1], lam4[:, 0, :], AX_X, ALU.add)
                dve.tensor_reduce(lamv[:, 1:2], lam4[:, 2, :], AX_X, ALU.add).then_inc(dve_out.sem, 1)
                dve.wait_ge(act_out.sem, ab + 1)
                chained(dve, dve.tensor_tensor(lamv[:, 4:5], lamv[:, 3:4], lamv[:, 2:3], ALU.subtract), dve_step)
                chained(dve, dve.tensor_scalar(lamv[:, 4:5], lamv[:, 4:5], -LAM_INIT, None, ALU.add), dve_step)
                dve.tensor_copy(lamv[:, 5:6], lamv[:, 4:5]).then_inc(dve_out.sem, 1)
                dve.wait_ge(pe_out.sem, pb + 2)
                dve.tensor_copy(nlam[:, :], ps[:, 1, 0:2])
                dve.tensor_copy(brow, ps[0:8, 0, 0:BIAS_W]).then_inc(dve_out.sem, 1)
                dve.tensor_scalar(gsub[:, :], prm[:, 1, 77:78], 1.0 - LAM_INIT, None, ALU.mult)

            @block.scalar
            def _(act):
                act.wait_ge(dve_out.sem, db + 1)
                act.activation(lamv[:, 2:4], lamv[:, 0:2], ACT.Exp).then_inc(act_out.sem, 1)
                for s in range(2):
                    act.activation(cs[:, :, s], prm[:, 0, 96 + 8 * s:104 + 8 * s], ACT.Silu)

            @block.sync
            def _(sp):
                sp.wait_ge(dve_out.sem, db + 3)
                sp.dma_start(bias_rows, brow).then_inc(stored.sem, 16)
                sp.wait_ge(stored.sem, 16)
        act_out.n += 1
        dve_out.n += 3
        pe_out.n += 2
        stored.n += 16

        adaln(0)
        ffn(0)
        modulate(1)
        product(lambda k: XM[:, k, :], TB, copy_out(into(gu)))

        z = sqf[:, 0:4 * 2 * 258].rearrange("p (j s t) -> p j s t", j=4, s=2)
        cv = EX[:, 0:4 * TB].rearrange("p (j s t) -> p j s t", j=4, s=2)
        spectrum = yf.rearrange("p (i c n) -> p i c n", c=2, n=P)
        pb, ab = pe_out.n, act_out.n
        with nc.Block() as block:
            @block.vector
            def _(dve):
                dve.memset(z[:, :, :, 0:1], 0.0)
                dve.memset(z[:, :, :, 257:258], 0.0)
                st = lambda ap: ap.rearrange("p (s t) -> p s t", s=2)
                for j in range(4):
                    ins = dve.tensor_tensor(z[:, j, :, 1:257], st(gu[:, 4 + j, :]), st(gu[:, 8 + j, :]), ALU.mult)
                chained(dve, ins, dve_step)
                w = lambda k, j: prm[:, 1, 78 + 4 * k + j:79 + 4 * k + j]
                for j in range(4):
                    ins = dve.tensor_scalar(cv[:, j], z[:, j, :, 0:256], w(0, j), None, ALU.mult)
                chained(dve, ins, dve_step)
                for k in (1, 2):
                    for j in range(4):
                        ins = dve.scalar_tensor_tensor(cv[:, j], z[:, j, :, k:k + 256], w(k, j), cv[:, j], ALU.mult, ALU.add)
                    chained(dve, ins, dve_step)
                for j in range(4):
                    dve.tensor_tensor(st(XM[:, j, :]), cv[:, j], st(gu[:, j, :]), ALU.mult)

            @block.tensor
            def _(pe):
                n = 0
                for s in range(2):
                    for g in range(4):
                        for t in range(2):
                            if n >= 6:
                                pe.wait_ge(act_out.sem, ab + n - 5)
                            c0 = s * SEQ + t * P
                            pe.matmul(ps[:, n % 6, 0:256], gu[:, 12 + g, c0:c0 + P], dft1, start=True, stop=True).then_inc(pe_out.sem, 1)
                            n += 1
                for m in range(8):
                    pe.wait_ge(act_out.sem, ab + 16 + max(0, m - 1))
                    for t in range(2):
                        for c in range(2):
                            mm = pe.matmul(ps[:, 6 + m % 2, 0:256], spectrum[:, 2 * m + t, c, :], dft2[:, t, c, :],
                                           start=(t == 0 and c == 0), stop=(t == 1 and c == 1))
                    mm.then_inc(pe_out.sem, 1)

            @block.scalar
            def _(act):
                for n in range(16):
                    act.wait_ge(pe_out.sem, pb + n + 1)
                    act.activation(spectrum[:, n, :, :].rearrange("p c n -> p (c n)"), ps[:, n % 6, 0:256], ACT.Copy).then_inc(act_out.sem, 1)
                for m in range(8):
                    s, g = m // 4, m % 4
                    act.wait_ge(pe_out.sem, pb + 16 + m + 1)
                    act.activation(XM[:, 4 + g, s * SEQ:(s + 1) * SEQ], ps[:, 6 + m % 2, 0:256], ACT.Copy).then_inc(act_out.sem, 1)
        pe_out.n += 24
        act_out.n += 24
        product(lambda k: XM[:, k, :], TB, copy_out(into(Y)))
        residual(1)
        ffn(2)

        adaln(1)
        ffn(0)
        modulate(1)
        view = lambda buf, lo, k, t: buf[:, lo:lo + k * t].rearrange("p (k t) -> p k t", k=k)
        qda, kda = view(GU, 0, 8, SEQ), view(GU, 2048, 8, TB)
        vda, cq = view(GU, 6144, 4, D), view(GU, 10240, 3, SEQ)
        qm, km = view(EX, 0, 8, SEQ), view(EX, 2048, 8, TB)
        ckv, krope = SQ[:, 4:6, 0:TB], SQ[:, 6:7, 0:TB]
        vm = xmf[:, 2048:4096].rearrange("p (t n) -> p t n", t=4)
        heads_out = view(yf, 0, 12, SEQ)

        product(lambda k: XM[:, k, 0:SEQ], SEQ,
                copy_out(lambda tile: qda[:, tile.t:tile.t + 1, :] if tile.t < 8 else cq[:, tile.t - 8:tile.t - 7, :]))

        def kv_dest(tile):
            t = tile.t
            if t < 8:
                return kda[:, t:t + 1, :]
            if t < 16:
                return Y[:, t - 8:t - 7, :]
            if t < 18:
                return ckv[:, t - 16:t - 15, :]
            return krope[MLA_NOPE:MLA_DQK, :, :]
        product(lambda k: XM[:, k, :], TB, copy_out(kv_dest))
        transposes([([Y[:, 4 * h + j, t * P:(t + 1) * P] for j in range(4)], P, P,
                     vda[:, t, 4 * h * P:4 * (h + 1) * P].rearrange("p (j c) -> p j c", j=4)) for t in range(4) for h in range(2)])

        def rope(tiles, table, which, T, plain):
            pb, gb, db = pe_out.n, pool_step.n, dve_out.n
            second = (std, rstd)
            with nc.Block() as block:
                @block.gpsimd
                def _(pool):
                    for n, x in enumerate(tiles):
                        lo = x.start_partition()
                        hi = lo + x.shape[0]
                        if n and lo != tiles[n - 1].start_partition():
                            pool.wait_ge(pool_step.sem, gb + n)
                        pool.tensor_tensor(plain[lo:hi, n, :], x, table[lo:hi, 0, :], ALU.mult).then_inc(pool_step.sem, 1)

                @block.tensor
                def _(pe):
                    for n, x in enumerate(tiles):
                        lo = x.start_partition()
                        hi = lo + x.shape[0]
                        if n >= 8:
                            pe.wait_ge(dve_out.sem, db + n - 7)
                        pe.matmul(ps[lo:hi, n % 8, 0:T], swap[lo:hi, which, lo:hi], x, start=True, stop=True).then_inc(pe_out.sem, 1)

                @block.vector
                def _(dve):
                    for n, x in enumerate(tiles):
                        lo = x.start_partition()
                        hi = lo + x.shape[0]
                        dve.wait_ge(pe_out.sem, pb + n + 1)
                        ins = dve.tensor_tensor(second[n % 2][lo:hi, 0:T], ps[lo:hi, n % 8, 0:T], table[lo:hi, 1, :], ALU.mult)
                        ins.then_inc(dve_out.sem, 1)
                        dve.wait_ge(dve_out.sem, db + n + 1)
                        dve.wait_ge(pool_step.sem, gb + n + 1)
                        dve.tensor_tensor(x, plain[lo:hi, n, :], second[n % 2][lo:hi, 0:T], ALU.add)
            pe_out.n += len(tiles)
            dve_out.n += len(tiles)
            pool_step.n += len(tiles)

        rope([qda[:, i, :] for i in range(8)] + [kda[:, i, 0:SEQ] for i in range(8)], rope_da, 0, SEQ, view(xmf, 0, 16, SEQ))
        gained(lambda k: prm[:, 1, 72 + k:73 + k], lambda k: cq[:, k, :], lambda k: cq[:, k, :], 3, SEQ)
        gained(lambda k: prm[:, 1, 75 + k:76 + k], lambda k: ckv[:, k, :], lambda k: ckv[:, k, :], 2, TB)
        product(lambda k: cq[:, k, :], SEQ, copy_out(lambda tile: qm[0:MLA_DQK, tile.t:tile.t + 1, :]))
        rope([qm[0:MLA_DQK, i, :] for i in range(8)] + [krope[MLA_NOPE:MLA_DQK, 0, 0:SEQ]], rope_mla, 1, SEQ, view(xmf, 0, 9, SEQ))
        with nc.Block() as block:
            @block.gpsimd
            def _(pool):
                for h in range(MLA_HEADS):
                    pool.tensor_copy(km[MLA_NOPE:MLA_DQK, h, :], krope[MLA_NOPE:MLA_DQK, 0, :])
        product(lambda k: ckv[:, k, :], TB, copy_out(lambda tile: km[0:MLA_NOPE, tile.t:tile.t + 1, :]))
        product(lambda k: ckv[:, k, :], TB, copy_out(lambda tile: XM[:, tile.t:tile.t + 1, :]))
        transposes([([XM[:, j, t * P:(t + 1) * P] for j in range(4)], P, P,
                     vm[:, t, :].rearrange("p (j c) -> p j c", j=4)) for t in range(4)])

        NK = TB // P
        items = []
        for h in range(DA_HEADS):
            for qt in range(SEQ // P):
                q = slice(qt * P, (qt + 1) * P)
                items.append(dict(
                    scores=[(qda[64 * m:64 * m + 64, h, q], kda[64 * m:64 * m + 64, h, :]) for m in range(2)], scale=DA_SCALE,
                    v=[vda[:, kt, h * P:(h + 1) * P] for kt in range(NK)], rows=(0, P), out=heads_out[:, h, q]))
        for h in range(MLA_HEADS):
            for qt in range(SEQ // P):
                q, lo = slice(qt * P, (qt + 1) * P), 64 * (h % 2)
                items.append(dict(
                    scores=[(qm[0:MLA_DQK, h, q], km[0:MLA_DQK, h, :])], scale=MLA_SCALE,
                    v=[vm[:, kt, h * 64:h * 64 + 64] for kt in range(NK)], rows=(lo, lo + 64), out=heads_out[lo:lo + 64, 8 + h // 2, q]))
        N = len(items)
        e = sqf[:, 0:2048].rearrange("p (b m k) -> p b m k", b=2, m=2)
        wT = sqf[:, 2048:3072].rearrange("p (b k q) -> p b k q", b=2, k=NK)
        scored, turned, summed = pe_out, pe_out2, pe_out3
        maxed, weighted, kept = dve_out, dve_out2, dve_out3
        raised, copied = act_out, act_out2
        sc0, tu0, su0, ma0, we0, ke0, ra0, co0 = (c.n for c in (scored, turned, summed, maxed, weighted, kept, raised, copied))
        with nc.Block() as block:
            @block.tensor
            def _(pe):
                def scores(n):
                    b = n % 2
                    if n >= 2:
                        pe.wait_ge(raised.sem, ra0 + n - 1)
                    for m, (q, k) in enumerate(items[n]["scores"]):
                        mm = pe.matmul(ps[:, 2 * b + m, :], q, k, start=True, stop=True)
                    mm.then_inc(scored.sem, 1)

                scores(0)
                for n in range(N):
                    if n + 1 < N:
                        scores(n + 1)
                    b = n % 2
                    pe.wait_ge(weighted.sem, we0 + n + 1)
                    if n >= 2:
                        pe.wait_ge(copied.sem, co0 + n - 1)
                    for kt in range(NK):
                        mm = pe.transpose(ps[:, 4 + b, kt * P:(kt + 1) * P], e[:, b, 0, kt * P:(kt + 1) * P], ident[:, :])
                    mm.then_inc(turned.sem, 1)
                    pe.wait_ge(copied.sem, co0 + n + 1)
                    if n >= 2:
                        pe.wait_ge(kept.sem, ke0 + n - 1)
                    lo, hi = items[n]["rows"]
                    for kt in range(NK):
                        mm = pe.matmul(ps[lo:hi, 6 + b, 0:P], items[n]["v"][kt], wT[:, b, kt, :], start=(kt == 0), stop=(kt == NK - 1))
                    mm.then_inc(summed.sem, 1)

            @block.vector
            def _(dve):
                def maxima(n):
                    b, nm = n % 2, len(items[n]["scores"])
                    s0 = 8 * b
                    dve.wait_ge(scored.sem, sc0 + n + 1)
                    chained(dve, dve.tensor_reduce(small[:, s0:s0 + nm], ps[:, 2 * b:2 * b + nm, :], AX_X, ALU.max), dve_step)
                    dve.tensor_scalar(small[:, s0 + 2:s0 + 2 + nm], small[:, s0:s0 + nm], -items[n]["scale"], None, ALU.mult).then_inc(maxed.sem, 1)

                def weights(n):
                    b, nm = n % 2, len(items[n]["scores"])
                    s0 = 8 * b
                    dve.wait_ge(raised.sem, ra0 + n + 1)
                    chained(dve, dve.reciprocal(small[:, s0 + 6:s0 + 6 + nm], small[:, s0 + 4:s0 + 4 + nm]), dve_step)
                    if nm == 1:
                        dve.tensor_scalar(e[:, b, 0, :], e[:, b, 0, :], small[:, s0 + 6:s0 + 7], None, ALU.mult).then_inc(weighted.sem, 1)
                        return
                    dve.tensor_scalar(small[:, s0 + 7:s0 + 8], small[:, s0 + 7:s0 + 8], nlam[:, 0:1], None, ALU.mult)
                    chained(dve, dve.tensor_scalar(e[:, b, 0, :], e[:, b, 0, :], small[:, s0 + 6:s0 + 7], None, ALU.mult), dve_step)
                    dve.scalar_tensor_tensor(e[:, b, 0, :], e[:, b, 1, :], small[:, s0 + 7:s0 + 8], e[:, b, 0, :],
                                             ALU.mult, ALU.add).then_inc(weighted.sem, 1)

                def keep(n):
                    dve.wait_ge(summed.sem, su0 + n + 1)
                    lo, hi = items[n]["rows"]
                    dve.tensor_copy(items[n]["out"], ps[lo:hi, 6 + n % 2, 0:P]).then_inc(kept.sem, 1)

                maxima(0)
                for n in range(N):
                    if n + 1 < N:
                        maxima(n + 1)
                    weights(n)
                    if n >= 1:
                        keep(n - 1)
                keep(N - 1)

            @block.scalar
            def _(act):
                def exps(n):
                    b, nm = n % 2, len(items[n]["scores"])
                    s0 = 8 * b
                    act.wait_ge(maxed.sem, ma0 + n + 1)
                    if n >= 2:
                        act.wait_ge(turned.sem, tu0 + n - 1)
                    for m in range(nm):
                        ins = act.activation(e[:, b, m, :], ps[:, 2 * b + m, :], ACT.Exp, bias=small[:, s0 + 2 + m:s0 + 3 + m],
                                             scale=items[n]["scale"], accum_out=small[:, s0 + 4 + m:s0 + 5 + m])
                    ins.then_inc(raised.sem, 1)

                exps(0)
                for n in range(N):
                    if n + 1 < N:
                        exps(n + 1)
                    b = n % 2
                    act.wait_ge(turned.sem, tu0 + n + 1)
                    if n >= 2:
                        act.wait_ge(summed.sem, su0 + n - 1)
                    act.activation(wT[:, b, :, :].rearrange("p k q -> p (k q)"), ps[:, 4 + b, :], ACT.Copy).then_inc(copied.sem, 1)
        for c in (scored, turned, summed, maxed, weighted, kept, raised, copied):
            c.n += N

        da_out = yf[:, 0:2048]
        sb0, mb0, tb0 = sq_ready.n, sum_ready.n, std_ready.n
        with nc.Block() as block:
            @block.scalar
            def _(act):
                act.activation(sqf[:, 0:2048], da_out, ACT.Square).then_inc(sq_ready.sem, 1)
                act.wait_ge(sum_ready.sem, mb0 + 1)
                act.activation(sqf[:, 2048:4096].rearrange("p (b n) -> p b n", b=4), ps[:, 0:4, :], ACT.Sqrt,
                               bias=epsb[:, 0:1], scale=1.0 / DA_DV).then_inc(std_ready.sem, 1)

            @block.tensor
            def _(pe):
                pe.wait_ge(sq_ready.sem, sb0 + 1)
                for b in range(4):
                    mm = pe.matmul(ps[:, b, :], ones[:, :], sqf[:, b * 512:(b + 1) * 512], start=True, stop=True)
                mm.then_inc(sum_ready.sem, 1)

            @block.vector
            def _(dve):
                dve.wait_ge(std_ready.sem, tb0 + 1)
                chained(dve, dve.reciprocal(sqf[:, 0:2048], sqf[:, 2048:4096]), dve_step)
                dve.scalar_tensor_tensor(da_out, da_out, gsub[:, 0:1], sqf[:, 0:2048], ALU.mult, ALU.mult)
        for c in (sq_ready, sum_ready, std_ready):
            c.n += 1
        product(lambda k: heads_out[:, k, :], SEQ, copy_out(into(XM, 0, SEQ)))
        residual(1, SEQ, src=XM)
        ffn(2, SEQ)

        flat2 = lambda k: H[:, k, 0:T2]
        pj = view(GU, 0, 40, T2)
        cat = view(xmf, 0, 12, T2)
        exf = EX[:, :]
        va = view(exf, 0, 3, 512)
        vr = view(exf, 1536, 3, D)
        iw = view(exf, 4608, 3, 8)
        ikd, iwf = exf[:, 4640:4640 + T2], exf[0:8, 4912:4912 + T2]
        chosen = view(exf, 5184, 3, T2)
        m8 = small[:, 0:8]
        token_tiles = [(0, P), (P, P), (2 * P, T2 - 2 * P)]

        def gain2(row):
            return lambda k: prm[:, 2, row + k:row + k + 1]

        def add_to_h():
            with nc.Block() as block:
                @block.vector
                def _(dve):
                    dve.tensor_tensor(H[:, :, 0:T2], H[:, :, 0:T2], Y[:, :, 0:T2], ALU.add)

        def conv_ffn(layer):
            gained(gain2(88 + 8 * layer), flat2, lambda k: XM[:, k, 0:T2], KD, T2)
            gp = sqf[:, 0:6 * (T2 + 2)].rearrange("p (j t) -> p j t", j=6)
            cv2 = sqf[:, 6 * (T2 + 2):6 * (2 * T2 + 2)].rearrange("p (j t) -> p j t", j=6)
            gu2 = view(GU, 0, KF, T2)
            with nc.Block() as block:
                @block.vector
                def _(dve):
                    dve.memset(gp[:, :, 0:2], 0.0)
            ab, db, sb_, cb, vb = act_freed.n, dve_freed.n, silu_done.n, conv_done.n, conv_step.n

            def evac(eng, mine, tile):
                j, n = tile.local, tile.n
                gate, is_act = tile.owner == "act", (tile.owner == "act") == mine
                if is_act and gate:
                    tile.wait(eng)
                    if not tile.first:
                        eng.wait_ge(conv_done.sem, n + cb - 5)
                    eng.activation(gp[:, j:j + 1, 2:2 + T2], tile.src, ACT.Copy).then_inc(act_freed.sem, 1)
                elif is_act:
                    eng.wait_ge(conv_done.sem, n + cb + 1)
                    eng.activation(cv2[:, j, :], cv2[:, j, :], ACT.Silu,
                                   bias=prm[:, 3 + layer, bass.ds(n + 66, 1)]).then_inc(silu_done.sem, 1)
                elif gate:
                    eng.wait_ge(act_freed.sem, n + ab + 1)
                    w = lambda k: prm[:, 3 + layer, bass.ds(n + KF * k, 1)]
                    eng.tensor_scalar(cv2[:, j, :], gp[:, j, 0:T2], w(0), None, ALU.mult).then_inc(conv_step.sem, 1)
                    eng.wait_ge(conv_step.sem, 2 * n + vb + 1)
                    eng.scalar_tensor_tensor(cv2[:, j, :], gp[:, j, 1:T2 + 1], w(1), cv2[:, j, :], ALU.mult, ALU.add).then_inc(conv_step.sem, 1)
                    eng.wait_ge(conv_step.sem, 2 * n + vb + 2)
                    eng.scalar_tensor_tensor(cv2[:, j, :], gp[:, j, 2:T2 + 2], w(2), cv2[:, j, :], ALU.mult, ALU.add).then_inc(conv_done.sem, 1)
                else:
                    tile.wait(eng)
                    eng.wait_ge(silu_done.sem, n + sb_ + 1)
                    eng.tensor_tensor(gu2[:, bass.ds(n, 1), :], cv2[:, j:j + 1, :], tile.src, ALU.mult).then_inc(dve_freed.sem, 1)
            product(lambda k: XM[:, k, 0:T2], T2, evac, group=2)
            silu_done.n += KF
            conv_done.n += KF
            conv_step.n += 2 * KF
            product(lambda k: gu2[:, k, :], T2, copy_out(into(Y, 0, T2)))
            add_to_h()

        with nc.Block() as block:
            @block.sync
            def _(sp):
                sp.dma_start(kb[:, :], a["k_second"]).then_inc(loaded.sem, 16)
                sp.dma_start(tri[:, :, :], a["k_sparse"]).then_inc(loaded.sem, 16)
                sp.wait_ge(loaded.sem, loaded.n + 32)
        loaded.n += 32
        gained(gain2(72), flat2, lambda k: XM[:, k, 0:T2], KD, T2)
        product(lambda k: XM[:, k, 0:T2], T2, copy_out(into(pj, 0, T2)))
        product(lambda k: XM[:, k, 0:T2], T2,
                copy_out(lambda tile: ikd[0:64, :].rearrange("p (a t) -> p a t", a=1) if tile.t == 0
                         else iwf.rearrange("p (a t) -> p a t", a=1)))
        product(lambda k: XM[:, k, 0:T2], T2, copy_out(into(pj, 16, T2)))
        transposes([([pj[:, first + 4 * h + j, t0:t0 + tn] for j in range(4)], tn, P,
                     dst[0:tn, t, 4 * h * P:4 * (h + 1) * P].rearrange("p (j c) -> p j c", j=4))
                    for t, (t0, tn) in enumerate(token_tiles) for first, dst, n in ((8, va, 1), (24, vr, 2)) for h in range(n)]
                   + [([iwf[:, t0:t0 + tn]], tn, P, iw[0:tn, t:t + 1, :]) for t, (t0, tn) in enumerate(token_tiles)])
        with nc.Block() as block:
            @block.vector
            def _(dve):
                dve.tensor_copy(ikd[64:P, :], ikd[0:64, :])
                for t, (t0, tn) in enumerate(token_tiles):
                    dve.tensor_scalar(iw[0:tn, t, :], iw[0:tn, t, :], 8 ** -0.5, None, ALU.mult)
        rope([pj[:, 16 + i, :] for i in range(8)], rope_ret, 2, T2, view(yf, 0, 8, T2))

        relu_s = view(sqf, 0, 8, T2)
        bias = view(yf, 0, 8, T2)
        pT = yf[:, 2176:2176 + 1536].rearrange("p (k h q) -> p k h q", k=3, h=4)
        pT2 = sqf[:, 2176:2176 + 1536].rearrange("p (k h q) -> p k h q", k=3, h=4)
        prob = view(sqf, 0, 8, T2)
        score, work = std[:, 0:T2], rstd[:, 0:T2]
        causal = tri[:, 1, :]
        for qt, (q0, nq) in enumerate(token_tiles):
            nk = min(T2, q0 + P)
            kts = token_tiles[:qt + 1]
            pb, ab, lb = pe_out.n, act_out.n, loaded.n
            with nc.Block() as block:
                @block.sync
                def _(sp):
                    src = bass.AP(bias_rows.tensor, T2 - q0 - nq, [[1, nq], [BIAS_W, DSA_HEADS], [1, nk]])
                    sp.dma_start(bias[0:nq, :, 0:nk], src).then_inc(loaded.sem, 16)
                    sp.wait_ge(loaded.sem, lb + 16)

                @block.tensor
                def _(pe):
                    for h in range(8):
                        lo = 64 * (h % 2)
                        pe.matmul(ps[0:nq, h, 0:nk], pj[lo:lo + 64, 12 + h // 2, q0:q0 + nq], ikd[lo:lo + 64, 0:nk],
                                  start=True, stop=True).then_inc(pe_out.sem, 1)

                @block.scalar
                def _(act):
                    for h in range(8):
                        act.wait_ge(pe_out.sem, pb + h + 1)
                        act.activation(relu_s[0:nq, h, 0:nk], ps[0:nq, h, 0:nk], ACT.Relu, scale=DSA_D ** -0.5).then_inc(act_out.sem, 1)

                @block.vector
                def _(dve):
                    for h in range(8):
                        dve.wait_ge(act_out.sem, ab + h + 1)
                        w = iw[0:nq, qt, h:h + 1]
                        if h == 0:
                            ins = dve.tensor_scalar(score[0:nq, 0:nk], relu_s[0:nq, 0, 0:nk], w, None, ALU.mult)
                        else:
                            ins = dve.scalar_tensor_tensor(score[0:nq, 0:nk], relu_s[0:nq, h, 0:nk], w, score[0:nq, 0:nk], ALU.mult, ALU.add)
                        chained(dve, ins, dve_step)
                    chained(dve, dve.tensor_tensor(score[0:nq, q0:nk], score[0:nq, q0:nk], causal[0:nq, 0:nk - q0], ALU.add), dve_step)
                    wk = work[0:nq, META:nk]
                    src = score[0:nq, META:nk]
                    for _ in range((KEEP - META) // 8):
                        chained(dve, dve.max(m8[0:nq, :], src), dve_step)
                        chained(dve, dve.match_replace(wk, m8[0:nq, :], src, TAKEN), dve_step)
                        src = wk
                    ch = chosen[0:nq, qt, 0:nk]
                    dve.memset(ch[:, 0:META], 0.0)
                    chained(dve, dve.tensor_scalar(ch[:, META:nk], wk, TAKEN * 0.9, NEG, ALU.is_gt, ALU.mult), dve_step)
                    dve.tensor_tensor(ch[:, q0:nk], ch[:, q0:nk], causal[0:nq, 0:nk - q0], ALU.add)
            pe_out.n += 8
            act_out.n += 8
            loaded.n += 16

            pb, ab, db, tb = pe_out.n, act_out.n, dve_out.n, pe_out2.n
            ob, cb = pe_out3.n, act_out2.n
            with nc.Block() as block:
                @block.tensor
                def _(pe):
                    for gr in range(2):
                        for j in range(4):
                            lo = 64 * (j % 2)
                            f = 2 * gr + j // 2
                            pe.matmul(ps[0:nq, 4 * gr + j, 0:nk], pj[lo:lo + 64, f, q0:q0 + nq], pj[lo:lo + 64, 4 + f, 0:nk],
                                      start=True, stop=False)
                            mm = pe.matmul(ps[0:nq, 4 * gr + j, 0:nk], tri[0:nq, 0 if nq == P else 2, 0:nq], bias[0:nq, 4 * gr + j, 0:nk],
                                           start=False, stop=True)
                        mm.then_inc(pe_out.sem, 1)
                    for gr in range(2):
                        pe.wait_ge(dve_out.sem, db + gr + 1)
                        for kt, (k0, kn) in enumerate(kts):
                            for j in range(4):
                                mm = pe.transpose(ps[0:kn, 4 * gr + kt, j * P:j * P + nq], prob[0:nq, 4 * gr + j, k0:k0 + kn],
                                                  ident[0:nq, 0:nq])
                            mm.then_inc(pe_out2.sem, 1)
                    for gr in range(2):
                        pe.wait_ge(act_out2.sem, cb + (gr + 1) * len(kts))
                        for j in range(4):
                            h, lo = 4 * gr + j, 64 * (j % 2)
                            for kt, (k0, kn) in enumerate(kts):
                                mm = pe.matmul(ps[lo:lo + 64, 4 * gr + 3, (j // 2) * P:(j // 2) * P + nq], va[0:kn, kt, h * 64:h * 64 + 64],
                                               (pT, pT2)[gr][0:kn, kt, j, 0:nq], start=(kt == 0), stop=(kt == len(kts) - 1))
                        mm.then_inc(pe_out3.sem, 1)

                @block.vector
                def _(dve):
                    for gr in range(2):
                        hs = slice(4 * gr, 4 * gr + 4)
                        pr = prob[0:nq, hs, 0:nk]
                        row = lambda c: small[0:nq, 16 + 16 * gr + 4 * c:20 + 16 * gr + 4 * c]
                        wide = lambda x: x.unsqueeze(2).broadcast_to((nq, 4, nk))
                        dve.wait_ge(pe_out.sem, pb + gr + 1)
                        mask = chosen[0:nq, qt, 0:nk].unsqueeze(1).broadcast_to((nq, 4, nk))
                        chained(dve, dve.scalar_tensor_tensor(pr, ps[0:nq, hs, 0:nk], DSA_D ** -0.5, mask, ALU.mult, ALU.add), dve_step)
                        chained(dve, dve.tensor_reduce(row(0), pr, AX_X, ALU.max), dve_step)
                        dve.tensor_tensor(pr, pr, wide(row(0)), ALU.subtract).then_inc(dve_out2.sem, 1)
                    for gr in range(2):
                        hs = slice(4 * gr, 4 * gr + 4)
                        pr = prob[0:nq, hs, 0:nk]
                        row = lambda c: small[0:nq, 16 + 16 * gr + 4 * c:20 + 16 * gr + 4 * c]
                        wide = lambda x: x.unsqueeze(2).broadcast_to((nq, 4, nk))
                        dve.wait_ge(act_out.sem, ab + gr + 1)
                        chained(dve, dve.tensor_reduce(row(1), pr, AX_X, ALU.add), dve_step)
                        chained(dve, dve.reciprocal(row(2), row(1)), dve_step)
                        dve.tensor_tensor(pr, pr, wide(row(2)), ALU.mult).then_inc(dve_out.sem, 1)
                    for gr in range(2):
                        dve.wait_ge(pe_out3.sem, ob + gr + 1)
                        dve.tensor_copy(cat[:, 2 * gr:2 * gr + 2, q0:q0 + nq],
                                        ps[:, 4 * gr + 3, 0:2 * P].rearrange("p (j q) -> p j q", j=2)[:, :, 0:nq])

                @block.scalar
                def _(act):
                    for gr in range(2):
                        pr = prob[0:nq, 4 * gr:4 * gr + 4, 0:nk]
                        act.wait_ge(dve_out2.sem, dve_out2.n + gr + 1)
                        act.activation(pr, pr, ACT.Exp).then_inc(act_out.sem, 1)
                    for gr in range(2):
                        for kt, (k0, kn) in enumerate(kts):
                            act.wait_ge(pe_out2.sem, tb + gr * len(kts) + kt + 1)
                            src = ps[0:kn, 4 * gr + kt, :].rearrange("p (h q) -> p h q", h=4)[:, :, 0:nq]
                            act.activation((pT, pT2)[gr][0:kn, kt, :, 0:nq], src, ACT.Copy).then_inc(act_out2.sem, 1)
            pe_out.n += 2
            pe_out2.n += 2 * len(kts)
            pe_out3.n += 2
            act_out.n += 2
            act_out2.n += 2 * len(kts)
            dve_out.n += 2
            dve_out2.n += 2

        inner = yf[:, 0:6 * T2].rearrange("p (b t q) -> p b t q", b=2, t=3)
        pb, db, ob, ab = pe_out.n, dve_out.n, pe_out3.n, act_out.n
        with nc.Block() as block:
            @block.tensor
            def _(pe):
                def scores(h):
                    b = h % 2
                    if h >= 2:
                        pe.wait_ge(dve_out.sem, db + h - 1)
                    for t, (k0, kn) in enumerate(token_tiles):
                        mm = pe.matmul(ps[0:kn, 3 * b + t, 0:T2 - k0], pj[:, 20 + h, k0:k0 + kn], pj[:, 16 + h, k0:T2], start=True, stop=True)
                    mm.then_inc(pe_out.sem, 1)

                scores(0)
                for h in range(RET_HEADS):
                    if h + 1 < RET_HEADS:
                        scores(h + 1)
                    pe.wait_ge(dve_out.sem, db + h + 1)
                    for f in range(2):
                        n = 2 * h + f
                        if n >= 2:
                            pe.wait_ge(act_out.sem, ab + n - 1)
                        for t, (k0, kn) in enumerate(token_tiles):
                            c0 = h * RET_DV + f * P
                            mm = pe.matmul(ps[:, 6 + f, k0:T2], vr[0:kn, t, c0:c0 + P], inner[0:kn, h % 2, t, 0:T2 - k0],
                                           start=(t == 0), stop=(t == 2), skip_group_check=True)
                        mm.then_inc(pe_out3.sem, 1)

            @block.vector
            def _(dve):
                for h in range(RET_HEADS):
                    dve.wait_ge(pe_out.sem, pb + h + 1)
                    if h >= 2:
                        dve.wait_ge(pe_out3.sem, ob + 2 * h - 2)
                    for t, (k0, kn) in enumerate(token_tiles):
                        ins = dve.tensor_tensor(inner[0:kn, h % 2, t, 0:T2 - k0], ps[0:kn, 3 * (h % 2) + t, 0:T2 - k0],
                                                decay[0:kn, h, 0:T2 - k0], ALU.mult)
                    ins.then_inc(dve_out.sem, 1)

            @block.scalar
            def _(act):
                for n in range(2 * RET_HEADS):
                    act.wait_ge(pe_out3.sem, ob + n + 1)
                    act.activation(cat[:, 4 + n, :], ps[:, 6 + n % 2, 0:T2], ACT.Copy).then_inc(act_out.sem, 1)
                act.activation(pj[:, 32:40, :], pj[:, 32:40, :], ACT.Silu)
        pe_out.n += RET_HEADS
        pe_out3.n += 2 * RET_HEADS
        dve_out.n += RET_HEADS
        act_out.n += 2 * RET_HEADS

        pb, db, ab, tb0 = pe_out.n, dve_out.n, act_out.n, std_ready.n
        sq2 = view(sqf, 0, 8, T2)
        dev = view(sqf, 8 * T2, 4, T2)
        with nc.Block() as block:
            @block.tensor
            def _(pe):
                for h in range(RET_HEADS):
                    for f in range(2):
                        mm = pe.matmul(ps[:, h, 0:T2], ones[:, :], cat[:, 4 + 2 * h + f, :], start=(f == 0), stop=(f == 1))
                    mm.then_inc(pe_out.sem, 1)
                for h in range(RET_HEADS):
                    pe.wait_ge(act_out.sem, ab + h + 1)
                    for f in range(2):
                        mm = pe.matmul(ps[:, 4 + h, 0:T2], ones[:, :], sq2[:, 2 * h + f, :], start=(f == 0), stop=(f == 1))
                mm.then_inc(pe_out.sem, 1)

            @block.vector
            def _(dve):
                for h in range(RET_HEADS):
                    dve.wait_ge(pe_out.sem, pb + h + 1)
                    for f in range(2):
                        r = cat[:, 4 + 2 * h + f, :]
                        ins = dve.scalar_tensor_tensor(r, ps[:, h, 0:T2], -1.0 / RET_DV, r, ALU.mult, ALU.add)
                    ins.then_inc(dve_out.sem, 1)
                dve.wait_ge(std_ready.sem, tb0 + 1)
                chained(dve, dve.reciprocal(dev, dev), dve_step)
                for n in range(8):
                    r = cat[:, 4 + n, :]
                    ins = dve.scalar_tensor_tensor(r, r, prm[:, 2, 112 + n:113 + n], dev[:, n // 2, :], ALU.mult, ALU.mult)
                chained(dve, ins, dve_step)
                dve.tensor_tensor(cat[:, 4:12, :], cat[:, 4:12, :], pj[:, 32:40, :], ALU.mult)

            @block.scalar
            def _(act):
                for h in range(RET_HEADS):
                    act.wait_ge(dve_out.sem, db + h + 1)
                    act.activation(sq2[:, 2 * h:2 * h + 2, :], cat[:, 4 + 2 * h:6 + 2 * h, :], ACT.Square).then_inc(act_out.sem, 1)
                act.wait_ge(pe_out.sem, pb + RET_HEADS + 1)
                act.activation(dev, ps[:, 4:8, 0:T2], ACT.Sqrt, bias=epsb[:, 0:1], scale=1.0 / RET_DV).then_inc(std_ready.sem, 1)
        pe_out.n += RET_HEADS + 1
        dve_out.n += RET_HEADS
        act_out.n += RET_HEADS
        std_ready.n += 1
        product(lambda k: cat[:, k, :], T2, copy_out(into(Y, 0, T2)))
        add_to_h()
        conv_ffn(0)

        with nc.Block() as block:
            @block.sync
            def _(sp):
                sp.dma_start(tri[:, :, :], a["k_tri"]).then_inc(loaded.sem, 16)
                sp.wait_ge(loaded.sem, loaded.n + 16)
        loaded.n += 16
        gained(gain2(80), flat2, lambda k: XM[:, k, 0:T2], KD, T2)
        product(lambda k: XM[:, k, 0:T2], T2, copy_out(into(pj, 0, T2)))
        vs = view(exf, 0, 3, D)
        transposes([([pj[:, 16 + 4 * h + j, t0:t0 + tn] for j in range(4)], tn, P,
                     vs[0:tn, t, 4 * h * P:4 * (h + 1) * P].rearrange("p (j c) -> p j c", j=4))
                    for t, (t0, tn) in enumerate(token_tiles) for h in range(2)])
        offs = [0, T2, T2 + (T2 - P)]
        full_w, all_w = offs[2], offs[2] + T2 - 2 * P
        last = T2 - 2 * P
        zs, sp_, lg, aw = (sqf[:, 1000 * i:1000 * i + 864].rearrange("p (b n) -> p b n", b=2) for i in range(4))
        parts = [(slice(0, P), slice(0, full_w)), (slice(0, last), slice(full_w, all_w))]
        zd, spd, ld, inc, exps_, out_ = pe_out, dve_out, act_out, pe_out2, dve_out2, act_out2
        vd, kd_ = pe_out3, dve_out3
        z0, s0_, l0, i0, t0_, a0, v0, k0_, c0_ = (c.n for c in (zd, spd, ld, inc, exps_, out_, vd, kd_, scaled))

        with nc.Block() as block:
            @block.tensor
            def _(pe):
                def logits(h):
                    b, lo = h % 2, 64 * (h % 2)
                    if h >= 2:
                        pe.wait_ge(scaled.sem, c0_ + h - 1)
                    for t, (k0, kn) in enumerate(token_tiles):
                        mm = pe.matmul(ps[0:kn, b, offs[t]:offs[t] + T2 - k0], pj[lo:lo + 64, 8 + h // 2, k0:k0 + kn],
                                       pj[lo:lo + 64, h // 2, k0:T2], start=True, stop=True)
                    mm.then_inc(zd.sem, 1)

                logits(0)
                for h in range(SB_HEADS):
                    if h + 1 < SB_HEADS:
                        logits(h + 1)
                    b, lo = h % 2, 64 * (h % 2)
                    pe.wait_ge(spd.sem, s0_ + h + 1)
                    if h >= 2:
                        pe.wait_ge(exps_.sem, t0_ + h - 1)
                    for t, (k0, kn) in enumerate(token_tiles):
                        for u in range(t, 3):
                            u0, un = token_tiles[u]
                            c = offs[t] + u0 - k0
                            lhs = tri[0:kn, 0, 0:kn] if u == t else ones[0:un, 0:kn]
                            mm = pe.matmul(ps[0:kn, 2 + b, c:c + T2 - u0], lhs, sp_[0:un, b, offs[u]:offs[u] + T2 - u0],
                                           start=(u == t), stop=(u == 2), skip_group_check=True)
                    mm.then_inc(inc.sem, 1)
                    pe.wait_ge(out_.sem, a0 + h + 1)
                    if h >= 2:
                        pe.wait_ge(kd_.sem, k0_ + h - 1)
                    for t, (k0, kn) in enumerate(token_tiles):
                        mm = pe.matmul(ps[lo:lo + 64, 4 + b, k0:T2], vs[0:kn, t, h * 64:h * 64 + 64], aw[0:kn, b, offs[t]:offs[t] + T2 - k0],
                                       start=(t == 0), stop=(t == 2), skip_group_check=True)
                    mm.then_inc(vd.sem, 1)

            @block.scalar
            def _(act):
                def softplus_tail(h):
                    b = h % 2
                    act.wait_ge(scaled.sem, c0_ + h + 1)
                    if h >= 2:
                        act.wait_ge(spd.sem, s0_ + h - 1)
                    for r, c in parts:
                        ins = act.activation(lg[r, b, c], zs[r, b, c], ACT.Abs)
                    chained(act, ins, act_step)
                    for r, c in parts:
                        ins = act.activation(lg[r, b, c], lg[r, b, c], ACT.Exp, scale=-1.0)
                    chained(act, ins, act_step)
                    for r, c in parts:
                        ins = act.activation(lg[r, b, c], lg[r, b, c], ACT.Ln, bias=1.0)
                    ins.then_inc(ld.sem, 1)

                softplus_tail(0)
                for h in range(SB_HEADS):
                    if h + 1 < SB_HEADS:
                        softplus_tail(h + 1)
                    b = h % 2
                    act.wait_ge(exps_.sem, t0_ + h + 1)
                    if h >= 2:
                        act.wait_ge(vd.sem, v0 + h - 1)
                    for r, c in parts:
                        ins = act.activation(aw[r, b, c], zs[r, b, c], ACT.Exp)
                    ins.then_inc(out_.sem, 1)

            @block.vector
            def _(dve):
                def mask(buf, b, which, op):
                    for t, (k0, kn) in enumerate(token_tiles):
                        x = buf[0:kn, b, offs[t]:offs[t] + kn]
                        ins = dve.tensor_tensor(x, x, tri[0:kn, which, 0:kn], op)
                    return ins

                def softplus(h):
                    b = h % 2
                    dve.wait_ge(zd.sem, z0 + h + 1)
                    if h >= 2:
                        dve.wait_ge(out_.sem, a0 + h - 1)
                        dve.wait_ge(inc.sem, i0 + h - 1)
                    for r, c in parts:
                        ins = dve.tensor_scalar(zs[r, b, c], ps[r, b, c], SB_D ** -0.5, None, ALU.mult)
                    ins.then_inc(scaled.sem, 1)
                    dve.wait_ge(scaled.sem, c0_ + h + 1)
                    dve.wait_ge(ld.sem, l0 + h + 1)
                    for r, c in parts:
                        ins = dve.scalar_tensor_tensor(sp_[r, b, c], zs[r, b, c], 0.0, lg[r, b, c], ALU.max, ALU.add)
                    chained(dve, ins, dve_step)
                    mask(sp_, b, 1, ALU.mult).then_inc(spd.sem, 1)

                def keep(h):
                    b, lo = h % 2, 64 * (h % 2)
                    dve.wait_ge(vd.sem, v0 + h + 1)
                    dve.tensor_copy(cat[lo:lo + 64, h // 2, :], ps[lo:lo + 64, 4 + b, 0:T2]).then_inc(kd_.sem, 1)

                softplus(0)
                for h in range(SB_HEADS):
                    if h + 1 < SB_HEADS:
                        softplus(h + 1)
                    b = h % 2
                    dve.wait_ge(inc.sem, i0 + h + 1)
                    for r, c in parts:
                        ins = dve.tensor_tensor(zs[r, b, c], zs[r, b, c], ps[r, 2 + b, c], ALU.subtract)
                    chained(dve, ins, dve_step)
                    mask(zs, b, 2, ALU.add).then_inc(exps_.sem, 1)
                    if h >= 1:
                        keep(h - 1)
                keep(SB_HEADS - 1)
        for c in (zd, spd, ld, inc, exps_, out_, vd, kd_, scaled):
            c.n += SB_HEADS
        product(lambda k: cat[:, k, :], T2, copy_out(into(Y, 0, T2)))
        add_to_h()
        conv_ffn(1)
        gained(gain2(104), flat2, lambda k: XM[:, k, 0:T2], KD, T2)
        finish(nc, a, out, H, XM, Y, sqf, stored, transposes, ctx, src=XM)


def constants():
    import numpy as np
    f = np.float32
    k = np.arange(P)
    c = {"k_ident": np.eye(P, dtype=f), "k_ones": np.ones((P, P), f)}

    def swap_of(dim, offset, quarter, period):
        R = np.zeros((P, P), f)
        for i in range(offset, dim):
            r = (i - offset) % period
            if r < quarter:
                R[i, i + quarter] = -1
            else:
                R[i, i - quarter] = 1
        return R.T

    swap = np.stack([swap_of(P, 0, 16, 32), swap_of(96, 64, 8, 16), swap_of(P, 0, 64, 128)], 1)
    c["k_swap"] = np.ascontiguousarray(swap)
    c["k_tri"] = np.ascontiguousarray(np.stack([
        (k[:, None] >= k[None, :]).astype(f),
        (k[:, None] < k[None, :]).astype(f),
        np.where(k[:, None] < k[None, :], 0, NEG).astype(f)], 1))
    short = np.zeros((P, P), f)
    n = T2 - 2 * P
    short[:n, :n] = np.eye(n)[::-1] * DSA_D ** 0.5
    c["k_sparse"] = np.ascontiguousarray(np.stack([
        np.eye(P, dtype=f)[::-1] * f(DSA_D ** 0.5), np.where(k[None, :] > k[:, None], NEG, 0).astype(f), short], 1))

    def angles(n_tokens, dim):
        t = np.arange(n_tokens)
        nf = dim // 4
        freqs = (f(10000.0) ** (-np.arange(nf, dtype=f) / f(nf))).astype(f)
        pos = np.stack([(t // 64).astype(f), (t % 64).astype(f)], 0)
        ang = pos[:, None, :] * freqs[None, :, None]
        return np.concatenate([ang[ax] for ax in (0, 0, 1, 1)], 0)

    first = np.zeros((P, 2304), f)
    th = 2 * np.pi * np.outer(k, k) / P
    first[:, 0:128], first[:, 128:256] = np.cos(th), np.sin(th)
    t = np.arange(SEQ)
    tt = 2 * np.pi * (np.outer(t, t) % SEQ) / SEQ
    s = 1.0 / np.sqrt(SEQ * P)
    d2 = np.stack([np.cos(tt) * s, -np.sin(tt) * s], 1).reshape(2, P, 2, SEQ).transpose(1, 0, 2, 3)
    first[:, 256:1280] = d2.reshape(P, 1024)
    da = np.tile(angles(SEQ, 64), (2, 1))
    first[:, 1280:1536], first[:, 1536:1792] = np.cos(da), np.sin(da)
    first[:, 1792:2048] = 1
    ml = angles(SEQ, 32)
    first[64:96, 1792:2048], first[64:96, 2048:2304] = np.cos(ml), np.sin(ml)
    c["k_first"] = first

    second = np.zeros((P, 2304), f)
    inv = (f(1) / (f(10000.0) ** (np.arange(64, dtype=f) / f(64)))).astype(f)
    ang = np.arange(T2, dtype=f)[None, :] * np.tile(inv, 2)[:, None]
    second[:, 0:T2], second[:, T2:2 * T2] = np.cos(ang), np.sin(ang)
    diff = np.arange(T2)[None, :] - k[:, None]
    for h in range(RET_HEADS):
        lg = np.log(1.0 - 2.0 ** (-5.0 - h))
        second[:, (2 + h) * T2:(3 + h) * T2] = np.where(diff >= 0, np.exp(np.maximum(diff, 0) * lg), 0) * RET_DK ** -0.5
    c["k_second"] = second

    dist = np.maximum(T2 - 1 - np.arange(BIAS_W), 0)
    large = 16 + (np.log(np.maximum(dist, 1).astype(f) / f(16)) / f(np.log(8.0)) * f(16)).astype(np.int32)
    bucket = np.where(dist < 16, dist, np.minimum(large, 31))
    c["k_bucket"] = (np.arange(32)[:, None] == bucket[None, :]).astype(f)
    return c


def kernel(**inputs):
    import numpy as np
    import concourse.bacc as bacc
    from concourse.bass_utils import run_bass_kernel_spmd as run

    nc = bacc.Bacc("TRN2", target_bir_lowering=False, num_devices=1)
    arrays, args = {}, {}
    for name, value in [*inputs.items(), *constants().items()]:
        v = np.ascontiguousarray(value)
        arrays[f"in_{name}"] = v
        args[name] = nc.dram_tensor(f"in_{name}", v.shape, mybir.dt.from_np(v.dtype), kind="ExternalInput").ap()
    out = nc.dram_tensor("out_0", (1, SEQ, D), F32, kind="ExternalOutput").ap()
    bias_rows = nc.dram_tensor("bias_rows", (DSA_HEADS, BIAS_W), F32, kind="Internal").ap()
    build(nc, args, out, bias_rows)
    r = run(nc, [arrays], core_ids=[0])
    return r.results[0]["out_0"]
```

```python
from contextlib import ExitStack

import concourse.bass as bass
from concourse import mybir

ALU = mybir.AluOpType
ACT = mybir.ActivationFunctionType
F32 = mybir.dt.float32
F32R = mybir.dt.float32r
AX_X = mybir.AxisListType.X

P = 128
D = 1024
KD = D // P
SEQ = 256
CTX = 256
TB = SEQ + CTX
META = 16
T2 = META + SEQ
DFF = 2816
KF = DFF // P
EPS = 1e-6
NEG = -1e30
TAKEN = -3e38
BANK = 512
SLOTS = 4
HI_SLOTS = 2
NB = 4
KG = 8

DA_HEADS, DA_DK, DA_DV = 8, 64, 128
MLA_HEADS, MLA_NOPE, MLA_ROPE, MLA_DV = 8, 64, 32, 64
MLA_DQK = MLA_NOPE + MLA_ROPE
DA_SCALE = DA_DK ** -0.5
MLA_SCALE = MLA_DQK ** -0.5
Q_COLS = 1024 + 384
LAM_INIT = 0.8 - 0.6 * 2.718281828459045 ** -0.3
DSA_HEADS, DSA_D = 8, 64
KEEP = min(256, SEQ // 4)
RET_HEADS, RET_DK, RET_DV = 4, 128, 256
SB_HEADS, SB_D = 16, 64
BIAS_W = 400


class Count:

    def __init__(self, sem):
        self.sem, self.n = sem, 0


def chained(eng, ins, count):
    ins.then_inc(count.sem, 1)
    count.n += 1
    eng.wait_ge(count.sem, count.n)


def signal(ins, count):
    ins.then_inc(count.sem, 1)
    count.n += 1


class Gemm:

    def __init__(self, name, K, pairs, half=P, last=None, side=None, only_side=False):
        self.name, self.kt = name, K // P
        self.only_side = only_side
        self.groups = 0 if only_side else -(-self.kt // KG)
        self.pairs, self.half, self.side = pairs, half, side
        self.last = last or (half, half)
        self.per_pair = self.groups + (side is not None)
        self.units = len(pairs) * self.per_pair
        self.per_rot = SLOTS
        self.rot_units = self.per_rot * self.per_pair
        self.full = (len(pairs) - (last is not None)) // self.per_rot

    def widths(self, p):
        return self.last if p == len(self.pairs) - 1 else (self.half, self.half)

    def source(self, unit, rot=0):
        pair, g = unit // self.per_pair, unit % self.per_pair - (self.per_pair - self.groups)
        if g < 0:
            w, _, first = self.side
            c0, step, width, k0, kn = 256 * (first + pair), 256 * self.per_rot, 256, 0, KD
        else:
            w, c0 = self.pairs[pair]
            k0, kn = g * KG, min(KG, self.kt - g * KG)
            width = sum(self.widths(pair))
            step = 0 if isinstance(rot, int) else self.pairs[pair + self.per_rot][1] - c0
        rows = w[k0 * P:(k0 + kn) * P, :].rearrange("(k p) n -> p k n", p=P)
        if isinstance(rot, int):
            return rows[:, :, c0:c0 + width], kn, width
        return rows[:, :, bass.ds(rot * step + c0, width)], kn, width


def finish(nc, a, out, H, XM, Y, sqf, stored, transposes, ctx, src=None):
    src = src or H
    tok = Y[:, :, :].rearrange("p a b -> p (a b)")[:, 0:2 * D].rearrange("p (t n) -> p t n", t=2)
    transposes([([src[:, 4 * h + j, META + t * P:META + (t + 1) * P] for j in range(4)], P, P,
                 tok[:, t, 4 * h * P:4 * (h + 1) * P].rearrange("p (j c) -> p j c", j=4)) for t in range(2) for h in range(2)])
    with nc.Block() as block:
        @block.sync
        def _(sp):
            sp.dma_start(out[0].rearrange("(t p) n -> p t n", p=P), tok).then_inc(stored.sem, 16)
            stored.n += 16
            sp.wait_ge(stored.sem, stored.n)


def build(nc, a, out, bias_rows):
    ctx = ExitStack()
    with ctx:
        def sb(name, shape):
            return ctx.enter_context(nc.sbuf_tensor(name, shape, F32))

        def sb_split(name, shape):
            at = nc.sbuf_base
            return sb(name, shape), nc.alloc_sbuf_tensor_at(name + "_r", shape, F32R, offset=at)

        def sem(name):
            return Count(ctx.enter_context(nc.semaphore(name)))

        H = sb("H", [P, KD, T2 + CTX])
        XM, XM_R = sb_split("XM", [P, KD, TB])
        Y, Y_R = sb_split("Y", [P, KD, TB])
        SQ, SQ_R = sb_split("SQ", [P, KD, 2 * T2])
        GU, GU_R = sb_split("GU", [P, KF * TB])
        EX, EX_R = sb_split("EX", [P, 6144])
        ring, ring_lo = sb_split("ring", [P, SLOTS, KG, 256])
        ring_hi = ctx.enter_context(nc.sbuf_tensor("ring_hi", [P, HI_SLOTS, KG, 256], F32R))
        ident = sb("ident", [P, P])
        ones = sb("ones", [P, P])
        swap = sb("swap", [P, 3, P])
        tri = sb("tri", [P, 3, P])
        kb = sb("kb", [P, 2304])
        dft1 = kb[:, 0:256]
        dft2 = kb[:, 256:1280].rearrange("p (t c n) -> p t c n", t=2, c=2)
        rope_da = kb[:, 1280:1792].rearrange("p (c t) -> p c t", c=2)
        rope_mla = kb[:, 1792:2304].rearrange("p (c t) -> p c t", c=2)
        rope_ret = kb[:, 0:2 * T2].rearrange("p (c t) -> p c t", c=2)
        decay = kb[:, 2 * T2:6 * T2].rearrange("p (h t) -> p h t", h=RET_HEADS)
        prm = sb("prm", [P, 5, P])
        cs = sb("cs", [P, KD, 2])
        mod = sb("mod", [P, 2, 72, 2])
        co = sb("co", [P, 9, KD, 2])
        adac = sb("adac", [P, 2, 256])
        std = sb("std", [P, TB])
        rstd = sb("rstd", [P, TB])
        epsb = sb("epsb", [P, 1])
        lam4 = sb("lam4", [1, 4, 64])
        lamv = sb("lamv", [1, 8])
        nlam = sb("nlam", [P, 2])
        gsub = sb("gsub", [P, 1])
        small = sb("small", [P, 64])
        ps = ctx.enter_context(nc.psum_tensor("ps", [P, 8, BANK], F32))

        loaded = sem("loaded")
        slot_loaded = [sem(f"slot_loaded{i}") for i in range(SLOTS)]
        w_used = sem("w_used")
        w_hi = sem("w_hi")
        w_split = sem("w_split")
        rhs_hi = sem("rhs_hi")
        rhs_split = sem("rhs_split")
        first_done = sem("first_done")
        act_freed = sem("act_freed")
        dve_freed = sem("dve_freed")
        side_step = sem("side_step")
        side_read = sem("side_read")
        side_summed = sem("side_summed")
        side_freed = sem("side_freed")
        conv_step = sem("conv_step")
        conv_done = sem("conv_done")
        silu_done = sem("silu_done")
        dve_step, act_step, pool_step, pe_step = (sem(x) for x in ("dve_step", "act_step", "pool_step", "pe_step"))
        sq_ready = sem("sq_ready")
        sum_ready = sem("sum_ready")
        std_ready = sem("std_ready")
        scaled = sem("scaled")
        pe_out = sem("pe_out")
        act_out = sem("act_out")
        dve_out = sem("dve_out")
        pe_out2 = sem("pe_out2")
        pe_out3 = sem("pe_out3")
        dve_out3 = sem("dve_out3")
        act_out2 = sem("act_out2")
        dve_out2 = sem("dve_out2")
        stored = sem("stored")

        def g_col(layer, i, k):
            return prm[:, 0, layer * 48 + i * 8 + k:layer * 48 + i * 8 + k + 1]

        def cols(w, c0, n):
            return [(w, c0 + 256 * i) for i in range(n)]

        def gate_up(wg, g0, wu, u0):
            return [x for j in range(DFF // 256) for x in ((wg, g0 + 256 * j), (wu, u0 + 256 * j))]

        def mod_gemm(layer, first, n):
            return Gemm("mod", D, [None] * n, side=(a["w_mod"][layer], layer, first), only_side=True)

        def ffn_gemms(layer, s, side=None):
            w = a["w_ffn_in"][layer, s]
            return [Gemm("ffn_in", D, gate_up(w, 0, w, DFF), side=side), Gemm("ffn_out", DFF, cols(a["w_ffn_out"][layer, s], 0, 4))]

        def ffn2_gemms(layer):
            return [Gemm("ffn2_in", D, gate_up(a["ffn_w_gate_2"][layer], 0, a["ffn_w_up_2"][layer], 0)),
                    Gemm("ffn2_out", DFF, cols(a["ffn_w_down_2"][layer], 0, 4))]

        w_in_odd = a["w_in_odd"][0]
        w_in_2 = a["even_w_in_2"][0]
        MOD_PAIRS = 36
        AT_ONCE = MOD_PAIRS - DFF // 128
        LEFT = MOD_PAIRS - DFF // 128 - 12
        w_mod = [a["w_mod"][layer] for layer in range(2)]
        plan = [mod_gemm(0, 0, AT_ONCE), *ffn_gemms(0, 0, side=(w_mod[0], 0, AT_ONCE)),
                Gemm("even_in", D, cols(a["w_in_even"][0], 0, 8), side=(w_mod[1], 1, 0)),
                Gemm("even_out", D, cols(a["w_out_even"][0], 0, 4), side=(w_mod[1], 1, 8)),
                *ffn_gemms(0, 1, side=(w_mod[1], 1, 12)),
                mod_gemm(1, MOD_PAIRS - LEFT, LEFT), *ffn_gemms(1, 0),
                Gemm("odd_q", D, cols(w_in_odd, 0, 6), last=(P, 0)),
                Gemm("odd_kv", D, cols(w_in_odd, Q_COLS, 10), last=(MLA_ROPE, 0)),
                Gemm("uq", 384, [(a["w_uq"][0], 192 * i) for i in range(4)], half=MLA_DQK),
                Gemm("uk", 256, [(a["w_uk"][0], 128 * i) for i in range(4)], half=MLA_NOPE),
                Gemm("uv", 256, cols(a["w_uv"][0], 0, 2)),
                Gemm("odd_out", 1536, cols(a["w_out_odd"][0], 0, 4)), *ffn_gemms(1, 1),
                Gemm("even2_a", D, cols(w_in_2, 0, 8)),
                Gemm("even2_i", D, [(w_in_2, 2048)], last=(64, 8)),
                Gemm("even2_b", D, cols(w_in_2, 2120, 12)),
                Gemm("even2_out", 1536, cols(a["even_w_out_2"][0], 0, 4)), *ffn2_gemms(0),
                Gemm("odd2_in", D, cols(a["odd_w_in_2"][0], 0, 12)),
                Gemm("odd2_out", D, cols(a["odd_w_out_2"][0], 0, 4)), *ffn2_gemms(1)]
        first_unit = [0]
        for g in plan:
            first_unit.append(first_unit[-1] + g.units)
        at = [0]
        kinds, seen = [], [0, 0]
        weight_units = []
        for g in plan:
            for u in range(g.units):
                side = g.side is not None and u % g.per_pair == 0
                if not side:
                    weight_units.append((len(kinds), *g.source(u)[1:]))
                kinds.append((side, seen[side]))
                seen[side] += 1

        def load_unit(sp, g, unit, n, rot=0, turn=0):
            src, kn, width = g.source(unit, rot)
            slot = n % SLOTS
            if n >= SLOTS or not isinstance(turn, int):
                m = n - SLOTS + (0 if isinstance(turn, int) else g.rot_units)
                side, before = kinds[m]
                step = g.per_rot * (1 if side else g.groups)
                count = side_read if side else w_used
                if isinstance(turn, int):
                    sp.wait_ge(count.sem, before + 1)
                else:
                    sp.wait_ge(count.sem, (turn - 1) * step + before + 1)
            sp.dma_start(ring[:, slot, 0:kn, 0:width], src).then_inc(slot_loaded[slot].sem, 16)

        def load_ahead(sp, p):
            lo, hi = first_unit[p] + SLOTS, min(first_unit[p + 1] + SLOTS, first_unit[-1])
            g, base = plan[p], first_unit[p]
            n = lo
            if g.full > 2:
                while n < base + g.rot_units:
                    load_unit(sp, g, n - base, n)
                    n += 1
                with sp.Fori(1, g.full) as r:
                    for i in range(g.rot_units):
                        load_unit(sp, g, i, base + i, rot=r, turn=r)
                n = base + g.rot_units * g.full
            while n < hi:
                q = max(i for i in range(len(plan)) if first_unit[i] <= n)
                load_unit(sp, plan[q], n - first_unit[q], n)
                n += 1

        def rotations(eng, g, body):
            def run(r, first=False):
                for i in range(g.per_rot):
                    body(i, r, first)
            done = 1 if g.full > 0 else 0
            if done:
                run(0, True)
            if g.full > 2:
                with eng.Fori(1, g.full) as r:
                    run(r)
                done = g.full
            for p in range(done * g.per_rot, len(g.pairs)):
                body(p % g.per_rot, p // g.per_rot, p < g.per_rot)

        def landed(eng, n, r=0, rot_units=0):
            eng.wait_ge(slot_loaded[n % SLOTS].sem, r * (16 * (rot_units // SLOTS)) + 16 * (n // SLOTS + 1))

        def split_weights(eng, who, w, r=0, step=0, rot_units=0):
            if w >= len(weight_units):
                return
            n, kn, width = weight_units[w]
            raw, hi = ring[:, n % SLOTS, 0:kn, 0:width], ring_hi[:, w % HI_SLOTS, 0:kn, 0:width]
            if who == "act":
                if w >= HI_SLOTS or not isinstance(r, int):
                    eng.wait_ge(w_used.sem, r * step + w - HI_SLOTS + 1)
                landed(eng, n, r, rot_units)
                eng.activation(hi, raw, ACT.Copy).then_inc(w_hi.sem, 1)
            else:
                eng.wait_ge(w_hi.sem, r * step + w + 1)
                eng.tensor_tensor(ring_lo[:, n % SLOTS, 0:kn, 0:width], raw, hi, ALU.subtract).then_inc(w_split.sem, 1)

        class Split:

            def __init__(self, src, hi, lo):
                self.src, self.hi, self.lo = src, hi, lo

        def product(x, T, evac, group=1, fresh=True):
            p = at[0]
            at[0] += 1
            g, base = plan[p], first_unit[p]
            assert base == w_used.n + side_read.n
            ub, rb_ = w_used.n, side_read.n
            extra = g.per_pair - g.groups
            fb, ab, db, mb = first_done.n, act_freed.n, dve_freed.n, side_summed.n
            hb, xb = rhs_hi.n, rhs_split.n
            unit_step = g.per_rot * g.groups

            def owner(i):
                return "act" if i % (2 * group) < group else "dve"

            def order(i):
                return i // (2 * group) * group + i % group

            def widths(i, r):
                return g.widths(r * g.per_rot + i) if isinstance(r, int) else (g.half, g.half)

            class Tile:
                def __init__(self, i, r, m):
                    t = 2 * i + m
                    self.t, self.m, self.w = r * (2 * g.per_rot) + t, m, widths(i, r)[m]
                    self.owner = owner(t)
                    self.src = ps[0:self.w, t % NB:t % NB + 1, 0:T]
                    self.first = isinstance(r, int) and r == 0
                    self.n = r * g.per_rot + order(t)
                    self.local = order(t)
                    alone = widths(i, r)[1] == 0
                    if m == 0 and not alone:
                        self.ready = (first_done, r * g.per_rot + fb + i + 1)
                    else:
                        self.ready = (w_used, r * (g.per_rot * g.groups) + ub + (i + 1) * g.groups)

                def wait(self, eng):
                    eng.wait_ge(self.ready[0].sem, self.ready[1])

            with nc.Block() as block:
                @block.sync
                def _(sp):
                    load_ahead(sp, p)

                @block.tensor
                def _(pe):
                    def pair(i, r, first):
                        w = widths(i, r)
                        for gr in range(g.groups):
                            n, w_ = base + i * g.per_pair + extra + gr, ub + i * g.groups + gr
                            pe.wait_ge(w_split.sem, r * unit_step + w_ + 1)
                            kn = min(KG, g.kt - gr * KG)
                            for m in range(2 if w[1] else 1):
                                t = 2 * i + m
                                if gr == 0 and not (first and t < NB):
                                    freed, b0 = (act_freed, ab) if owner(t) == "act" else (dve_freed, db)
                                    pe.wait_ge(freed.sem, r * g.per_rot + b0 + order(t) - order(NB) + 1)
                                c = slice(m * w[0], m * w[0] + w[m])
                                for k in range(kn):
                                    kx = gr * KG + k
                                    if fresh and first and i == 0 and m == 0:
                                        pe.wait_ge(rhs_split.sem, xb + kx + 1)
                                    hi, lo = ring_hi[:, w_ % HI_SLOTS, k, c], ring_lo[:, n % SLOTS, k, c]
                                    passes = [(hi, x.hi(kx)[:, 0:T]), (hi, x.lo(kx)[:, 0:T]), (lo, x.hi(kx)[:, 0:T])]
                                    for j, (lhs, rhs) in enumerate(passes):
                                        mm = pe.matmul(ps[0:w[m], t % NB, 0:T], lhs, rhs, start=(kx == 0 and j == 0),
                                                       stop=(kx == g.kt - 1 and j == 2))
                                if m == 0 and w[1] and gr == g.groups - 1:
                                    mm.then_inc(first_done.sem, 1)
                            mm.then_inc(w_used.sem, 1)
                        if g.side:
                            adaln_sum(pe, r * g.per_rot + rb_ + i + 1)
                    rotations(pe, g, pair)

                def split_input(eng, who, gr):
                    for k in range(gr * KG, min(gr * KG + KG, g.kt)):
                        if who == "act":
                            eng.activation(x.hi(k), x.src(k), ACT.Copy).then_inc(rhs_hi.sem, 1)
                        else:
                            eng.wait_ge(rhs_hi.sem, hb + k + 1)
                            eng.tensor_tensor(x.lo(k), x.src(k), x.hi(k), ALU.subtract).then_inc(rhs_split.sem, 1)

                def evacuate(eng, who):
                    def pair(i, r, first):
                        if g.side and who == "dve":
                            if fresh and first and i == 0:
                                split_input(eng, who, 0)
                            landed(eng, base + i * g.per_pair, r, g.rot_units)
                            adaln_products(eng, (base + i * g.per_pair) % SLOTS, r * g.per_rot + i)
                        for gr in range(g.groups):
                            if fresh and first and i == 0 and not (g.side and who == "dve"):
                                split_input(eng, who, gr)
                            w_ = ub + i * g.groups + gr + 1
                            if isinstance(r, int):
                                split_weights(eng, who, w_ + r * unit_step)
                            else:
                                split_weights(eng, who, w_, r, unit_step, g.rot_units)
                        for m in range(2):
                            if widths(i, r)[m]:
                                tile = Tile(i, r, m)
                                evac(eng, tile.owner == who, tile)
                        if g.side and who == "dve":
                            adaln_columns(eng, g.side[1], r * (2 * g.per_rot) + 2 * (g.side[2] + i), r * g.per_rot + mb + i + 1)
                    rotations(eng, g, pair)

                @block.scalar
                def _(act):
                    evacuate(act, "act")

                @block.vector
                def _(dve):
                    evacuate(dve, "dve")

            w_used.n += len(g.pairs) * g.groups
            tiles = [(p_, m) for p_ in range(len(g.pairs)) for m in range(2) if g.widths(p_)[m]]
            first_done.n += sum(1 for p_ in range(len(g.pairs)) if g.widths(p_)[1])
            act_freed.n += sum(owner(2 * p_ + m) == "act" for p_, m in tiles)
            dve_freed.n += sum(owner(2 * p_ + m) == "dve" for p_, m in tiles)
            if g.side:
                side_done(len(g.pairs))
            w_hi.n = w_split.n = w_used.n + 1
            if fresh:
                rhs_hi.n += g.kt
                rhs_split.n += g.kt

        def copy_out(dest):
            def evac(eng, mine, tile):
                if not mine:
                    return
                tile.wait(eng)
                if tile.owner == "act":
                    eng.activation(dest(tile), tile.src, ACT.Copy).then_inc(act_freed.sem, 1)
                else:
                    eng.tensor_copy(dest(tile), tile.src).then_inc(dve_freed.sem, 1)
            return evac

        def into(buf, first_tile=0, T=TB):
            return lambda tile: buf[0:tile.w, bass.ds(tile.t + first_tile, 1), 0:T]

        def adaln_products(dve, slot, pair):
            for k in range(KD):
                for s in range(2):
                    w = ring[:, slot, k, :]
                    if k == 0:
                        ins = dve.tensor_scalar(adac[:, s, :], w, cs[:, k, s:s + 1], None, ALU.mult)
                    else:
                        ins = dve.scalar_tensor_tensor(adac[:, s, :], w, cs[:, k, s:s + 1], adac[:, s, :], ALU.mult, ALU.add)
                if k < KD - 1:
                    ins.then_inc(side_step.sem, 1)
                    dve.wait_ge(side_step.sem, (KD - 1) * pair + side_step.n + k + 1)
                else:
                    ins.then_inc(side_read.sem, 1)

        def adaln_sum(pe, count):
            pe.wait_ge(side_read.sem, count)
            for m in range(2):
                for s in range(2):
                    mm = pe.matmul(ps[:, 7, 2 * m + s:2 * m + s + 1], adac[:, s, m * P:(m + 1) * P], ones[:, 0:1], start=True, stop=True)
            mm.then_inc(side_summed.sem, 1)

        def adaln_columns(dve, layer, tile, count):
            dve.wait_ge(side_summed.sem, count)
            b = prm[:, 1 + layer, bass.ds(tile, 2)].unsqueeze(2).broadcast_to((P, 2, 2))
            dve.tensor_tensor(mod[:, layer, bass.ds(tile, 2), :], ps[:, 7, 0:4].rearrange("p (t s) -> p t s", s=2), b,
                              ALU.add).then_inc(side_freed.sem, 1)

        def side_done(pairs):
            side_read.n += pairs
            side_summed.n += pairs
            side_freed.n += pairs
            side_step.n += (KD - 1) * pairs

        def adaln(layer, first):
            p = at[0]
            at[0] += 1
            g, base = plan[p], first_unit[p]
            assert base == w_used.n + side_read.n
            rb_, mb = side_read.n, side_summed.n
            with nc.Block() as block:
                @block.sync
                def _(sp):
                    load_ahead(sp, p)

                @block.tensor
                def _(pe):
                    for i in range(len(g.pairs)):
                        adaln_sum(pe, rb_ + i + 1)

                @block.vector
                def _(dve):
                    for i in range(len(g.pairs)):
                        n = base + i
                        landed(dve, n)
                        adaln_products(dve, n % SLOTS, i)
                        adaln_columns(dve, layer, 2 * (first + i), mb + i + 1)
                    if w_used.n == 0:
                        split_weights(dve, "dve", 0)

                if w_used.n == 0:
                    @block.scalar
                    def _(act):
                        split_weights(act, "act", 0)
            side_done(len(g.pairs))

        def coefficients(layer, slots):
            with nc.Block() as block:
                @block.vector
                def _(dve):
                    for slot in slots:
                        pre = prm[:, 0, layer * 48 + 16 * slot:layer * 48 + 16 * slot + 8]
                        post = prm[:, 0, layer * 48 + 16 * slot + 8:layer * 48 + 16 * slot + 16]
                        for s in range(2):
                            m = [mod[:, layer, (3 * slot + j) * 8:(3 * slot + j + 1) * 8, s] for j in range(3)]
                            dve.scalar_tensor_tensor(co[:, 3 * slot, :, s], m[1], 1.0, pre, ALU.add, ALU.mult)
                            dve.tensor_copy(co[:, 3 * slot + 1, :, s], m[0])
                            dve.scalar_tensor_tensor(co[:, 3 * slot + 2, :, s], m[2], 1.0 if slot == 1 else 0.5, post,
                                                     ALU.mult, ALU.mult)

        def norm(src, Kt, T, dve_part, act_part=None, dim=None, squares=SQ):
            dim = dim or Kt * P
            qb, mb, tb_ = sq_ready.n, sum_ready.n, std_ready.n
            with nc.Block() as block:
                @block.scalar
                def _(act):
                    for k in range(Kt):
                        act.activation(squares[:, k, 0:T], src(k), ACT.Square).then_inc(sq_ready.sem, 1)
                    act.wait_ge(sum_ready.sem, mb + 1)
                    act.activation(std[:, 0:T], ps[:, 7, 0:T], ACT.Sqrt, bias=epsb[:, 0:1], scale=1.0 / dim).then_inc(std_ready.sem, 1)
                    if act_part:
                        act_part(act)

                @block.tensor
                def _(pe):
                    for k in range(Kt):
                        pe.wait_ge(sq_ready.sem, qb + k + 1)
                        mm = pe.matmul(ps[:, 7, 0:T], ones[:, :], squares[:, k, 0:T], start=(k == 0), stop=(k == Kt - 1))
                    mm.then_inc(sum_ready.sem, 1)

                @block.vector
                def _(dve):
                    dve.wait_ge(std_ready.sem, tb_ + 1)
                    chained(dve, dve.reciprocal(rstd[:, 0:T], std[:, 0:T]), dve_step)
                    dve_part(dve)
            sq_ready.n += Kt
            sum_ready.n += 1
            std_ready.n += 1

        def streams(T):
            return [(0, SEQ, 0)] + ([(SEQ, TB, 1)] if T == TB else [])

        def h1(k, T=TB):
            return H[:, k, META:META + T]

        def modulate(slot, T=TB):
            b = scaled.n

            def dve_part(dve):
                for k in range(KD):
                    dve.tensor_tensor(SQ[:, k, 0:T], h1(k, T), rstd[:, 0:T], ALU.mult).then_inc(scaled.sem, 1)

            def act_part(act):
                for k in range(KD):
                    act.wait_ge(scaled.sem, b + k + 1)
                    for lo, hi, s in streams(T):
                        act.activation(Y[:, k, lo:hi], SQ[:, k, lo:hi], ACT.Identity,
                                       bias=co[:, 3 * slot + 1, k, s:s + 1], scale=co[:, 3 * slot, k, s:s + 1])
            norm(lambda k: h1(k, T), KD, T, dve_part, act_part)
            scaled.n += KD

        def residual(slot, T=TB, src=SQ, temp=XM):

            def dve_part(dve):
                for k in range(KD):
                    dve.tensor_tensor(temp[:, k, 0:T], src[:, k, 0:T], rstd[:, 0:T], ALU.mult).then_inc(dve_step.sem, 1)
                    dve_step.n += 1
                b = dve_step.n - KD
                for k in range(KD):
                    dve.wait_ge(dve_step.sem, b + k + 1)
                    for lo, hi, s in streams(T):
                        dve.scalar_tensor_tensor(h1(k)[:, lo:hi], temp[:, k, lo:hi], co[:, 3 * slot + 2, k, s:s + 1],
                                                 h1(k)[:, lo:hi], ALU.mult, ALU.add)
            norm(lambda k: src[:, k, 0:T], KD, T, dve_part, squares=temp)

        def gained(gain, src, dst, Kt, T, dim=None):
            def dve_part(dve):
                for k in range(Kt):
                    dve.scalar_tensor_tensor(dst(k), src(k), gain(k), rstd[:, 0:T], ALU.mult, ALU.mult)
            norm(src, Kt, T, dve_part, dim=dim)

        def normed(T):
            return Split(lambda k: Y[:, k, 0:T], lambda k: XM_R[:, k, 0:T], lambda k: EX_R[:, k * TB:k * TB + T])

        def in_place(src, src_r):
            return Split(lambda k: src[:, k, :], lambda k: EX_R[:, k * TB:k * TB + src.shape[2]], lambda k: src_r[:, k, :])

        def narrow(src, src_r):
            T = src.shape[2]
            return Split(lambda k: src[:, k, :], lambda k: EX_R[:, k * T:(k + 1) * T], lambda k: src_r[:, k, :])

        def hidden(T):
            def hi(k):
                if k < KD:
                    return XM_R[:, k, 0:T]
                return Y_R[:, k - KD, 0:T] if k < 2 * KD else EX_R[:, (k - 2 * KD) * TB:(k - 2 * KD) * TB + T]
            return Split(lambda k: GU[:, k * T:(k + 1) * T], hi, lambda k: GU_R[:, k * T:(k + 1) * T])

        def transposes(groups):
            pb, ab, db = pe_out.n, act_out.n, dve_out.n
            with nc.Block() as block:
                @block.tensor
                def _(pe):
                    for n, (srcs, rows, width, dst) in enumerate(groups):
                        if n >= 8:
                            pe.wait_ge((act_out, dve_out)[n % 2].sem, (ab, db)[n % 2] + (n - 8) // 2 + 1)
                        for j, src in enumerate(srcs):
                            kp = src.shape[0]
                            mm = pe.transpose(ps[0:rows, n % 8, j * width:j * width + kp], src, ident[0:kp, 0:kp])
                        mm.then_inc(pe_out.sem, 1)

                def copies(eng, who, count):
                    for n, (srcs, rows, width, dst) in enumerate(groups):
                        if n % 2 != who:
                            continue
                        eng.wait_ge(pe_out.sem, pb + n + 1)
                        src = ps[0:rows, n % 8, 0:len(srcs) * width].rearrange("p (j c) -> p j c", j=len(srcs))[:, :, 0:srcs[0].shape[0]]
                        if who == 0:
                            eng.activation(dst, src, ACT.Copy).then_inc(count.sem, 1)
                        else:
                            eng.tensor_copy(dst, src).then_inc(count.sem, 1)

                @block.scalar
                def _(act):
                    copies(act, 0, act_out)

                @block.vector
                def _(dve):
                    copies(dve, 1, dve_out)
            pe_out.n += len(groups)
            act_out.n += (len(groups) + 1) // 2
            dve_out.n += len(groups) // 2

        gu = GU[:, :].rearrange("p (k t) -> p k t", t=TB)

        def ffn(slot, T=TB):
            modulate(slot, T)
            hold = SQ[:, 0:4, 0:TB]
            hid = GU[:, 0:KF * T].rearrange("p (k t) -> p k t", t=T)
            ab, db = act_freed.n, dve_freed.n

            def evac(eng, mine, tile):
                if not mine:
                    return
                j = tile.local
                tile.wait(eng)
                if tile.owner == "act":
                    if not tile.first:
                        eng.wait_ge(dve_freed.sem, tile.n + db - 3)
                    eng.activation(hold[:, j:j + 1, 0:T], tile.src, ACT.Silu).then_inc(act_freed.sem, 1)
                else:
                    eng.wait_ge(act_freed.sem, tile.n + ab + 1)
                    eng.tensor_tensor(hid[:, bass.ds(tile.n, 1), :], hold[:, j:j + 1, 0:T], tile.src, ALU.mult).then_inc(dve_freed.sem, 1)
            product(normed(T), T, evac, group=2)
            product(hidden(T), T, copy_out(into(SQ, 0, T)))
            residual(slot, T)

        sqf = SQ[:, :, :].rearrange("p a b -> p (a b)")
        xmf = XM[:, :, :].rearrange("p a b -> p (a b)")
        yf = Y[:, :, :].rearrange("p a b -> p (a b)")
        raw = xmf[:, 0:5 * P].rearrange("p (i n) -> p i n", i=5)
        tok = yf.rearrange("p (t n) -> p t n", t=4)
        meta_tok = sqf[0:META, 0:D]
        onehot, relb, brow = EX[0:32, 0:BIAS_W], EX[0:32, 512:520], EX[0:8, 1024:1024 + BIAS_W]
        rows = lambda ap, n: ap.rearrange("(r p) -> r p", p=P) if n == 1 else ap.rearrange("a (r p) -> (a r) p", p=P)
        row_list = [
            (0, 0, a["norm_g"].rearrange("l i (r p) -> (l i r) p", p=P), 96),
            (0, 96, rows(a["c"], 2), 8), (0, 104, rows(a["c_ctx"], 1), 8),
            (1, 0, rows(a["b_mod"][0:1], 2), 72), (1, 72, rows(a["g_q_mla"], 2), 3), (1, 75, rows(a["g_kv_mla"], 2), 2),
            (1, 77, rows(a["g_subln"], 2), 1), (1, 78, rows(a["conv_w"][0], 2), 12),
            (2, 0, rows(a["b_mod"][1:2], 2), 72), (2, 72, rows(a["norm_mix_2"], 2), 16), (2, 88, rows(a["norm_ffn_2"], 2), 16),
            (2, 104, rows(a["norm_final_2"], 1), 8), (2, 112, rows(a["even_gn_gain_2"], 2), 8),
            (3, 0, rows(a["ffn_conv_w_2"][0], 2), 66), (3, 66, rows(a["ffn_conv_b_2"][0:1], 2), 22),
            (4, 0, rows(a["ffn_conv_w_2"][1], 2), 66), (4, 66, rows(a["ffn_conv_b_2"][1:2], 2), 22)]
        row_counts = [112, 90, 120, 88, 88]
        first_loads = [
            (ident[:, :], a["k_ident"]), (ones[:, :], a["k_ones"]), (swap[:, :, :], a["k_swap"]), (tri[:, :, :], a["k_tri"]),
            (kb[:, :], a["k_first"]), (onehot, a["k_bucket"]), (relb, a["rel_bias_2"]),
            (tok[:, 0:2, :], a["x"][0].rearrange("(t p) n -> p t n", p=P)),
            (tok[:, 2:4, :], a["ctx"][0].rearrange("(t p) n -> p t n", p=P)), (meta_tok, a["meta_tokens_2"]),
            (lam4[:, 0, :], a["lam_q1"]), (lam4[:, 1, :], a["lam_k1"]), (lam4[:, 2, :], a["lam_q2"]), (lam4[:, 3, :], a["lam_k2"]),
            *[(raw[r:r + n, i, :], src) for i, r, src, n in row_list]]
        with nc.Block() as block:
            @block.sync
            def _(sp):
                for dst, src in first_loads:
                    sp.dma_start(dst, src).then_inc(loaded.sem, 16)
                for n in range(SLOTS):
                    q = max(i for i in range(len(plan)) if first_unit[i] <= n)
                    load_unit(sp, plan[q], n - first_unit[q], n)
                sp.wait_ge(loaded.sem, 16 * len(first_loads))

            @block.gpsimd
            def _(pool):
                pool.memset(epsb[:, :], EPS)
        loaded.n += 16 * len(first_loads)

        transposes([([raw[0:n, i, :]], P, P, prm[:, i:i + 1, 0:n]) for i, n in enumerate(row_counts)]
                   + [([tok[:, t, (4 * h + j) * P:(4 * h + j + 1) * P] for j in range(4)], P, P,
                       H[:, 4 * h:4 * h + 4, META + t * P:META + (t + 1) * P]) for t in range(4) for h in range(2)]
                   + [([meta_tok[:, (4 * h + j) * P:(4 * h + j + 1) * P] for j in range(4)], P, P,
                       H[:, 4 * h:4 * h + 4, 0:META]) for h in range(2)])

        ab, db, pb = act_out.n, dve_out.n, pe_out.n
        with nc.Block() as block:
            @block.tensor
            def _(pe):
                pe.matmul(ps[0:8, 0, 0:BIAS_W], relb, onehot, start=True, stop=True).then_inc(pe_out.sem, 1)
                pe.wait_ge(dve_out.sem, db + 2)
                pe.matmul(ps[:, 1, 0:2], ones[0:1, :], lamv[:, 4:6], start=True, stop=True).then_inc(pe_out.sem, 1)

            @block.vector
            def _(dve):
                dve.tensor_tensor(lam4[:, 0, :], lam4[:, 0, :], lam4[:, 1, :], ALU.mult)
                chained(dve, dve.tensor_tensor(lam4[:, 2, :], lam4[:, 2, :], lam4[:, 3, :], ALU.mult), dve_step)
                dve.tensor_reduce(lamv[:, 0:1], lam4[:, 0, :], AX_X, ALU.add)
                dve.tensor_reduce(lamv[:, 1:2], lam4[:, 2, :], AX_X, ALU.add).then_inc(dve_out.sem, 1)
                dve.wait_ge(act_out.sem, ab + 1)
                chained(dve, dve.tensor_tensor(lamv[:, 4:5], lamv[:, 3:4], lamv[:, 2:3], ALU.subtract), dve_step)
                chained(dve, dve.tensor_scalar(lamv[:, 4:5], lamv[:, 4:5], -LAM_INIT, None, ALU.add), dve_step)
                dve.tensor_copy(lamv[:, 5:6], lamv[:, 4:5]).then_inc(dve_out.sem, 1)
                dve.wait_ge(pe_out.sem, pb + 2)
                dve.tensor_copy(nlam[:, :], ps[:, 1, 0:2])
                dve.tensor_copy(brow, ps[0:8, 0, 0:BIAS_W]).then_inc(dve_out.sem, 1)
                dve.tensor_scalar(gsub[:, :], prm[:, 1, 77:78], 1.0 - LAM_INIT, None, ALU.mult)

            @block.scalar
            def _(act):
                act.wait_ge(dve_out.sem, db + 1)
                act.activation(lamv[:, 2:4], lamv[:, 0:2], ACT.Exp).then_inc(act_out.sem, 1)
                for s in range(2):
                    act.activation(cs[:, :, s], prm[:, 0, 96 + 8 * s:104 + 8 * s], ACT.Silu)

            @block.sync
            def _(sp):
                sp.wait_ge(dve_out.sem, db + 3)
                sp.dma_start(bias_rows, brow).then_inc(stored.sem, 16)
                sp.wait_ge(stored.sem, 16)
        act_out.n += 1
        dve_out.n += 3
        pe_out.n += 2
        stored.n += 16

        adaln(0, 0)
        coefficients(0, [0])
        ffn(0)
        coefficients(0, [1, 2])
        modulate(1)
        product(normed(TB), TB, copy_out(into(gu)))

        z = sqf[:, 0:4 * 2 * 258].rearrange("p (j s t) -> p j s t", j=4, s=2)
        cv = EX[:, 0:4 * TB].rearrange("p (j s t) -> p j s t", j=4, s=2)
        spectrum = yf.rearrange("p (i c n) -> p i c n", c=2, n=P)
        pb, ab = pe_out.n, act_out.n
        with nc.Block() as block:
            @block.vector
            def _(dve):
                dve.memset(z[:, :, :, 0:1], 0.0)
                dve.memset(z[:, :, :, 257:258], 0.0)
                st = lambda ap: ap.rearrange("p (s t) -> p s t", s=2)
                for j in range(4):
                    ins = dve.tensor_tensor(z[:, j, :, 1:257], st(gu[:, 4 + j, :]), st(gu[:, 8 + j, :]), ALU.mult)
                chained(dve, ins, dve_step)
                w = lambda k, j: prm[:, 1, 78 + 4 * k + j:79 + 4 * k + j]
                for j in range(4):
                    ins = dve.tensor_scalar(cv[:, j], z[:, j, :, 0:256], w(0, j), None, ALU.mult)
                chained(dve, ins, dve_step)
                for k in (1, 2):
                    for j in range(4):
                        ins = dve.scalar_tensor_tensor(cv[:, j], z[:, j, :, k:k + 256], w(k, j), cv[:, j], ALU.mult, ALU.add)
                    chained(dve, ins, dve_step)
                for j in range(4):
                    dve.tensor_tensor(st(XM[:, j, :]), cv[:, j], st(gu[:, j, :]), ALU.mult)

            @block.tensor
            def _(pe):
                n = 0
                for s in range(2):
                    for g in range(4):
                        for t in range(2):
                            if n >= 6:
                                pe.wait_ge(act_out.sem, ab + n - 5)
                            c0 = s * SEQ + t * P
                            pe.matmul(ps[:, n % 6, 0:256], gu[:, 12 + g, c0:c0 + P], dft1, start=True, stop=True).then_inc(pe_out.sem, 1)
                            n += 1
                for m in range(8):
                    pe.wait_ge(act_out.sem, ab + 16 + max(0, m - 1))
                    for t in range(2):
                        for c in range(2):
                            mm = pe.matmul(ps[:, 6 + m % 2, 0:256], spectrum[:, 2 * m + t, c, :], dft2[:, t, c, :],
                                           start=(t == 0 and c == 0), stop=(t == 1 and c == 1))
                    mm.then_inc(pe_out.sem, 1)

            @block.scalar
            def _(act):
                for n in range(16):
                    act.wait_ge(pe_out.sem, pb + n + 1)
                    act.activation(spectrum[:, n, :, :].rearrange("p c n -> p (c n)"), ps[:, n % 6, 0:256], ACT.Copy).then_inc(act_out.sem, 1)
                for m in range(8):
                    s, g = m // 4, m % 4
                    act.wait_ge(pe_out.sem, pb + 16 + m + 1)
                    act.activation(XM[:, 4 + g, s * SEQ:(s + 1) * SEQ], ps[:, 6 + m % 2, 0:256], ACT.Copy).then_inc(act_out.sem, 1)
        pe_out.n += 24
        act_out.n += 24
        product(in_place(XM, XM_R), TB, copy_out(into(Y)))
        residual(1, src=Y)
        ffn(2)

        adaln(1, MOD_PAIRS - LEFT)
        coefficients(1, [0, 1, 2])
        ffn(0)
        modulate(1)
        view = lambda buf, lo, k, t: buf[:, lo:lo + k * t].rearrange("p (k t) -> p k t", k=k)
        qda, kda = view(GU, 0, 8, SEQ), view(GU, 2048, 8, TB)
        vda, cq = view(GU, 6144, 4, D), view(GU, 10240, 3, SEQ)
        qm, km = view(EX, 0, 8, SEQ), view(EX, 2048, 8, TB)
        ckv, krope = SQ[:, 4:6, 0:TB], SQ[:, 6:7, 0:TB]
        vm = xmf[:, 2048:4096].rearrange("p (t n) -> p t n", t=4)
        heads_out = view(yf, 0, 12, SEQ)

        product(normed(TB), SEQ,
                copy_out(lambda tile: qda[:, tile.t:tile.t + 1, :] if tile.t < 8 else cq[:, tile.t - 8:tile.t - 7, :]))

        def kv_dest(tile):
            t = tile.t
            if t < 8:
                return kda[:, t:t + 1, :]
            if t < 16:
                return Y[:, t - 8:t - 7, :]
            if t < 18:
                return ckv[:, t - 16:t - 15, :]
            return krope[MLA_NOPE:MLA_DQK, :, :]
        product(normed(TB), TB, copy_out(kv_dest), fresh=False)
        transposes([([Y[:, 4 * h + j, t * P:(t + 1) * P] for j in range(4)], P, P,
                     vda[:, t, 4 * h * P:4 * (h + 1) * P].rearrange("p (j c) -> p j c", j=4)) for t in range(4) for h in range(2)])

        def rope(tiles, table, which, T, plain):
            pb, gb, db = pe_out.n, pool_step.n, dve_out.n
            second = (std, rstd)
            with nc.Block() as block:
                @block.gpsimd
                def _(pool):
                    for n, x in enumerate(tiles):
                        lo = x.start_partition()
                        hi = lo + x.shape[0]
                        if n and lo != tiles[n - 1].start_partition():
                            pool.wait_ge(pool_step.sem, gb + n)
                        pool.tensor_tensor(plain[lo:hi, n, :], x, table[lo:hi, 0, :], ALU.mult).then_inc(pool_step.sem, 1)

                @block.tensor
                def _(pe):
                    for n, x in enumerate(tiles):
                        lo = x.start_partition()
                        hi = lo + x.shape[0]
                        if n >= 8:
                            pe.wait_ge(dve_out.sem, db + n - 7)
                        pe.matmul(ps[lo:hi, n % 8, 0:T], swap[lo:hi, which, lo:hi], x, start=True, stop=True).then_inc(pe_out.sem, 1)

                @block.vector
                def _(dve):
                    for n, x in enumerate(tiles):
                        lo = x.start_partition()
                        hi = lo + x.shape[0]
                        dve.wait_ge(pe_out.sem, pb + n + 1)
                        ins = dve.tensor_tensor(second[n % 2][lo:hi, 0:T], ps[lo:hi, n % 8, 0:T], table[lo:hi, 1, :], ALU.mult)
                        ins.then_inc(dve_out.sem, 1)
                        dve.wait_ge(dve_out.sem, db + n + 1)
                        dve.wait_ge(pool_step.sem, gb + n + 1)
                        dve.tensor_tensor(x, plain[lo:hi, n, :], second[n % 2][lo:hi, 0:T], ALU.add)
            pe_out.n += len(tiles)
            dve_out.n += len(tiles)
            pool_step.n += len(tiles)

        rope([qda[:, i, :] for i in range(8)] + [kda[:, i, 0:SEQ] for i in range(8)], rope_da, 0, SEQ, view(xmf, 0, 16, SEQ))
        gained(lambda k: prm[:, 1, 72 + k:73 + k], lambda k: cq[:, k, :], lambda k: cq[:, k, :], 3, SEQ)
        gained(lambda k: prm[:, 1, 75 + k:76 + k], lambda k: ckv[:, k, :], lambda k: ckv[:, k, :], 2, TB)
        cq_r, ckv_r = view(GU_R, 10240, 3, SEQ), SQ_R[:, 4:6, 0:TB]
        product(Split(lambda k: cq[:, k, :], lambda k: Y_R[:, k, 0:SEQ], lambda k: cq_r[:, k, :]), SEQ, copy_out(lambda tile: qm[0:MLA_DQK, tile.t:tile.t + 1, :]))
        rope([qm[0:MLA_DQK, i, :] for i in range(8)] + [krope[MLA_NOPE:MLA_DQK, 0, 0:SEQ]], rope_mla, 1, SEQ, view(xmf, 0, 9, SEQ))
        with nc.Block() as block:
            @block.gpsimd
            def _(pool):
                for h in range(MLA_HEADS):
                    pool.tensor_copy(km[MLA_NOPE:MLA_DQK, h, :], krope[MLA_NOPE:MLA_DQK, 0, :])
        latent = Split(lambda k: ckv[:, k, :], lambda k: Y_R[:, k, :], lambda k: ckv_r[:, k, :])
        product(latent, TB, copy_out(lambda tile: km[0:MLA_NOPE, tile.t:tile.t + 1, :]))
        product(latent, TB, copy_out(lambda tile: XM[:, tile.t:tile.t + 1, :]), fresh=False)
        transposes([([XM[:, j, t * P:(t + 1) * P] for j in range(4)], P, P,
                     vm[:, t, :].rearrange("p (j c) -> p j c", j=4)) for t in range(4)])

        NK = TB // P
        items = []
        for h in range(DA_HEADS):
            for qt in range(SEQ // P):
                q = slice(qt * P, (qt + 1) * P)
                items.append(dict(
                    scores=[(qda[64 * m:64 * m + 64, h, q], kda[64 * m:64 * m + 64, h, :]) for m in range(2)], scale=DA_SCALE,
                    v=[vda[:, kt, h * P:(h + 1) * P] for kt in range(NK)], rows=(0, P), out=heads_out[:, h, q]))
        for h in range(MLA_HEADS):
            for qt in range(SEQ // P):
                q, lo = slice(qt * P, (qt + 1) * P), 64 * (h % 2)
                items.append(dict(
                    scores=[(qm[0:MLA_DQK, h, q], km[0:MLA_DQK, h, :])], scale=MLA_SCALE,
                    v=[vm[:, kt, h * 64:h * 64 + 64] for kt in range(NK)], rows=(lo, lo + 64), out=heads_out[lo:lo + 64, 8 + h // 2, q]))
        N = len(items)
        e = sqf[:, 0:2048].rearrange("p (b m k) -> p b m k", b=2, m=2)
        wT = sqf[:, 2048:3072].rearrange("p (b k q) -> p b k q", b=2, k=NK)
        scored, turned, summed = pe_out, pe_out2, pe_out3
        maxed, weighted, kept = dve_out, dve_out2, dve_out3
        raised, copied = act_out, act_out2
        sc0, tu0, su0, ma0, we0, ke0, ra0, co0 = (c.n for c in (scored, turned, summed, maxed, weighted, kept, raised, copied))
        with nc.Block() as block:
            @block.tensor
            def _(pe):
                def scores(n):
                    b = n % 3
                    if n >= 3:
                        pe.wait_ge(raised.sem, ra0 + n - 2)
                    for m, (q, k) in enumerate(items[n]["scores"]):
                        mm = pe.matmul(ps[:, 2 * b + m, :], q, k, start=True, stop=True)
                    mm.then_inc(scored.sem, 1)

                def values(n):
                    pe.wait_ge(copied.sem, co0 + n + 1)
                    if n >= 1:
                        pe.wait_ge(kept.sem, ke0 + n)
                    lo, hi = items[n]["rows"]
                    for kt in range(NK):
                        mm = pe.matmul(ps[lo:hi, 7, 0:P], items[n]["v"][kt], wT[:, n % 2, kt, :], start=(kt == 0), stop=(kt == NK - 1))
                    mm.then_inc(summed.sem, 1)

                scores(0)
                scores(1)
                for n in range(N):
                    if n + 2 < N:
                        scores(n + 2)
                    pe.wait_ge(weighted.sem, we0 + n + 1)
                    if n >= 1:
                        pe.wait_ge(copied.sem, co0 + n)
                    for kt in range(NK):
                        mm = pe.transpose(ps[:, 6, kt * P:(kt + 1) * P], e[:, n % 2, 0, kt * P:(kt + 1) * P], ident[:, :])
                    mm.then_inc(turned.sem, 1)
                    if n >= 1:
                        values(n - 1)
                values(N - 1)

            @block.vector
            def _(dve):
                def maxima(n):
                    b, nm = n % 2, len(items[n]["scores"])
                    s0 = 8 * b
                    dve.wait_ge(scored.sem, sc0 + n + 1)
                    chained(dve, dve.tensor_reduce(small[:, s0:s0 + nm], ps[:, 2 * (n % 3):2 * (n % 3) + nm, :], AX_X, ALU.max), dve_step)
                    dve.tensor_scalar(small[:, s0 + 2:s0 + 2 + nm], small[:, s0:s0 + nm], -items[n]["scale"], None, ALU.mult).then_inc(maxed.sem, 1)

                def weights(n):
                    b, nm = n % 2, len(items[n]["scores"])
                    s0 = 8 * b
                    dve.wait_ge(raised.sem, ra0 + n + 1)
                    chained(dve, dve.reciprocal(small[:, s0 + 6:s0 + 6 + nm], small[:, s0 + 4:s0 + 4 + nm]), dve_step)
                    if nm == 1:
                        dve.tensor_scalar(e[:, b, 0, :], e[:, b, 0, :], small[:, s0 + 6:s0 + 7], None, ALU.mult).then_inc(weighted.sem, 1)
                        return
                    dve.tensor_scalar(small[:, s0 + 7:s0 + 8], small[:, s0 + 7:s0 + 8], nlam[:, 0:1], None, ALU.mult)
                    chained(dve, dve.tensor_scalar(e[:, b, 0, :], e[:, b, 0, :], small[:, s0 + 6:s0 + 7], None, ALU.mult), dve_step)
                    dve.scalar_tensor_tensor(e[:, b, 0, :], e[:, b, 1, :], small[:, s0 + 7:s0 + 8], e[:, b, 0, :],
                                             ALU.mult, ALU.add).then_inc(weighted.sem, 1)

                def keep(n):
                    dve.wait_ge(summed.sem, su0 + n + 1)
                    lo, hi = items[n]["rows"]
                    dve.tensor_copy(items[n]["out"], ps[lo:hi, 7, 0:P]).then_inc(kept.sem, 1)

                maxima(0)
                for n in range(N):
                    if n + 1 < N:
                        maxima(n + 1)
                    weights(n)
                    if n >= 2:
                        keep(n - 2)
                keep(N - 2)
                keep(N - 1)

            @block.scalar
            def _(act):
                def exps(n):
                    b, nm = n % 2, len(items[n]["scores"])
                    s0 = 8 * b
                    act.wait_ge(maxed.sem, ma0 + n + 1)
                    if n >= 2:
                        act.wait_ge(turned.sem, tu0 + n - 1)
                    for m in range(nm):
                        ins = act.activation(e[:, b, m, :], ps[:, 2 * (n % 3) + m, :], ACT.Exp, bias=small[:, s0 + 2 + m:s0 + 3 + m],
                                             scale=items[n]["scale"], accum_out=small[:, s0 + 4 + m:s0 + 5 + m])
                    ins.then_inc(raised.sem, 1)

                exps(0)
                for n in range(N):
                    if n + 1 < N:
                        exps(n + 1)
                    b = n % 2
                    act.wait_ge(turned.sem, tu0 + n + 1)
                    if n >= 2:
                        act.wait_ge(summed.sem, su0 + n - 1)
                    act.activation(wT[:, b, :, :].rearrange("p k q -> p (k q)"), ps[:, 6, :], ACT.Copy).then_inc(copied.sem, 1)
        for c in (scored, turned, summed, maxed, weighted, kept, raised, copied):
            c.n += N

        da_out = yf[:, 0:2048]
        sb0, mb0, tb0 = sq_ready.n, sum_ready.n, std_ready.n
        with nc.Block() as block:
            @block.scalar
            def _(act):
                act.activation(sqf[:, 0:2048], da_out, ACT.Square).then_inc(sq_ready.sem, 1)
                act.wait_ge(sum_ready.sem, mb0 + 1)
                act.activation(sqf[:, 2048:4096].rearrange("p (b n) -> p b n", b=4), ps[:, 0:4, :], ACT.Sqrt,
                               bias=epsb[:, 0:1], scale=1.0 / DA_DV).then_inc(std_ready.sem, 1)

            @block.tensor
            def _(pe):
                pe.wait_ge(sq_ready.sem, sb0 + 1)
                for b in range(4):
                    mm = pe.matmul(ps[:, b, :], ones[:, :], sqf[:, b * 512:(b + 1) * 512], start=True, stop=True)
                mm.then_inc(sum_ready.sem, 1)

            @block.vector
            def _(dve):
                dve.wait_ge(std_ready.sem, tb0 + 1)
                chained(dve, dve.reciprocal(sqf[:, 0:2048], sqf[:, 2048:4096]), dve_step)
                dve.scalar_tensor_tensor(da_out, da_out, gsub[:, 0:1], sqf[:, 0:2048], ALU.mult, ALU.mult)
        for c in (sq_ready, sum_ready, std_ready):
            c.n += 1
        product(narrow(heads_out, view(Y_R[:, :, :].rearrange("p a b -> p (a b)"), 0, 12, SEQ)), SEQ, copy_out(into(XM, 0, SEQ)))
        residual(1, SEQ, src=XM, temp=SQ)
        ffn(2, SEQ)

        flat2 = lambda k: H[:, k, 0:T2]
        pj = view(GU, 0, 40, T2)
        cat = view(xmf, 0, 12, T2)
        cat_r = view(XM_R[:, :, :].rearrange("p a b -> p (a b)"), 0, 12, T2)
        exf = EX[:, :]
        va = view(exf, 0, 3, 512)
        vr = view(exf, 1536, 3, D)
        iw = view(exf, 4608, 3, 8)
        ikd, iwf = exf[:, 4640:4640 + T2], exf[0:8, 4912:4912 + T2]
        chosen = view(exf, 5184, 3, T2)
        m8 = small[:, 0:8]
        token_tiles = [(0, P), (P, P), (2 * P, T2 - 2 * P)]

        def gain2(row):
            return lambda k: prm[:, 2, row + k:row + k + 1]

        def add_to_h():
            with nc.Block() as block:
                @block.vector
                def _(dve):
                    dve.tensor_tensor(H[:, :, 0:T2], H[:, :, 0:T2], SQ[:, :, 0:T2], ALU.add)

        def conv_ffn(layer):
            gained(gain2(88 + 8 * layer), flat2, lambda k: Y[:, k, 0:T2], KD, T2)
            gp = sqf[:, 0:4 * (T2 + 2)].rearrange("p (j t) -> p j t", j=4)
            cv2 = sqf[:, 4 * (T2 + 2):4 * (2 * T2 + 2)].rearrange("p (j t) -> p j t", j=4)
            gu2 = view(GU, 0, KF, T2)
            with nc.Block() as block:
                @block.vector
                def _(dve):
                    dve.memset(gp[:, :, 0:2], 0.0)
            ab, db, sb_, cb, vb = act_freed.n, dve_freed.n, silu_done.n, conv_done.n, conv_step.n

            def evac(eng, mine, tile):
                j, n = tile.local, tile.n
                gate, is_act = tile.owner == "act", (tile.owner == "act") == mine
                if is_act and gate:
                    tile.wait(eng)
                    if not tile.first:
                        eng.wait_ge(conv_done.sem, n + cb - 3)
                    eng.activation(gp[:, j:j + 1, 2:2 + T2], tile.src, ACT.Copy).then_inc(act_freed.sem, 1)
                elif is_act:
                    eng.wait_ge(conv_done.sem, n + cb + 1)
                    eng.activation(cv2[:, j, :], cv2[:, j, :], ACT.Silu,
                                   bias=prm[:, 3 + layer, bass.ds(n + 66, 1)]).then_inc(silu_done.sem, 1)
                elif gate:
                    eng.wait_ge(act_freed.sem, n + ab + 1)
                    w = lambda k: prm[:, 3 + layer, bass.ds(n + KF * k, 1)]
                    eng.tensor_scalar(cv2[:, j, :], gp[:, j, 0:T2], w(0), None, ALU.mult).then_inc(conv_step.sem, 1)
                    eng.wait_ge(conv_step.sem, 2 * n + vb + 1)
                    eng.scalar_tensor_tensor(cv2[:, j, :], gp[:, j, 1:T2 + 1], w(1), cv2[:, j, :], ALU.mult, ALU.add).then_inc(conv_step.sem, 1)
                    eng.wait_ge(conv_step.sem, 2 * n + vb + 2)
                    eng.scalar_tensor_tensor(cv2[:, j, :], gp[:, j, 2:T2 + 2], w(2), cv2[:, j, :], ALU.mult, ALU.add).then_inc(conv_done.sem, 1)
                else:
                    tile.wait(eng)
                    eng.wait_ge(silu_done.sem, n + sb_ + 1)
                    eng.tensor_tensor(gu2[:, bass.ds(n, 1), :], cv2[:, j:j + 1, :], tile.src, ALU.mult).then_inc(dve_freed.sem, 1)
            product(normed(T2), T2, evac, group=2)
            silu_done.n += KF
            conv_done.n += KF
            conv_step.n += 2 * KF
            product(hidden(T2), T2, copy_out(into(SQ, 0, T2)))
            add_to_h()

        with nc.Block() as block:
            @block.sync
            def _(sp):
                sp.dma_start(kb[:, :], a["k_second"]).then_inc(loaded.sem, 16)
                sp.dma_start(tri[:, :, :], a["k_sparse"]).then_inc(loaded.sem, 16)
                sp.wait_ge(loaded.sem, loaded.n + 32)
        loaded.n += 32
        gained(gain2(72), flat2, lambda k: Y[:, k, 0:T2], KD, T2)
        product(normed(T2), T2, copy_out(into(pj, 0, T2)))
        product(normed(T2), T2,
                copy_out(lambda tile: ikd[0:64, :].rearrange("p (a t) -> p a t", a=1) if tile.t == 0
                         else iwf.rearrange("p (a t) -> p a t", a=1)), fresh=False)
        product(normed(T2), T2, copy_out(into(pj, 16, T2)), fresh=False)
        transposes([([pj[:, first + 4 * h + j, t0:t0 + tn] for j in range(4)], tn, P,
                     dst[0:tn, t, 4 * h * P:4 * (h + 1) * P].rearrange("p (j c) -> p j c", j=4))
                    for t, (t0, tn) in enumerate(token_tiles) for first, dst, n in ((8, va, 1), (24, vr, 2)) for h in range(n)]
                   + [([iwf[:, t0:t0 + tn]], tn, P, iw[0:tn, t:t + 1, :]) for t, (t0, tn) in enumerate(token_tiles)])
        with nc.Block() as block:
            @block.vector
            def _(dve):
                dve.tensor_copy(ikd[64:P, :], ikd[0:64, :])
                for t, (t0, tn) in enumerate(token_tiles):
                    dve.tensor_scalar(iw[0:tn, t, :], iw[0:tn, t, :], 8 ** -0.5, None, ALU.mult)
        rope([pj[:, 16 + i, :] for i in range(8)], rope_ret, 2, T2, view(yf, 0, 8, T2))

        relu_s = view(sqf, 0, 8, T2)
        bias = view(yf, 0, 8, T2)
        pT = yf[:, 2176:2176 + 1536].rearrange("p (k h q) -> p k h q", k=3, h=4)
        pT2 = sqf[:, 2176:2176 + 1536].rearrange("p (k h q) -> p k h q", k=3, h=4)
        prob = view(sqf, 0, 8, T2)
        score, work = std[:, 0:T2], rstd[:, 0:T2]
        causal = tri[:, 1, :]
        for qt, (q0, nq) in enumerate(token_tiles):
            nk = min(T2, q0 + P)
            kts = token_tiles[:qt + 1]
            pb, ab, lb = pe_out.n, act_out.n, loaded.n
            with nc.Block() as block:
                @block.sync
                def _(sp):
                    src = bass.AP(bias_rows.tensor, T2 - q0 - nq, [[1, nq], [BIAS_W, DSA_HEADS], [1, nk]])
                    sp.dma_start(bias[0:nq, :, 0:nk], src).then_inc(loaded.sem, 16)
                    sp.wait_ge(loaded.sem, lb + 16)

                @block.tensor
                def _(pe):
                    for h in range(8):
                        lo = 64 * (h % 2)
                        pe.matmul(ps[0:nq, h, 0:nk], pj[lo:lo + 64, 12 + h // 2, q0:q0 + nq], ikd[lo:lo + 64, 0:nk],
                                  start=True, stop=True).then_inc(pe_out.sem, 1)

                @block.scalar
                def _(act):
                    for h in range(8):
                        act.wait_ge(pe_out.sem, pb + h + 1)
                        act.activation(relu_s[0:nq, h, 0:nk], ps[0:nq, h, 0:nk], ACT.Relu, scale=DSA_D ** -0.5).then_inc(act_out.sem, 1)

                @block.vector
                def _(dve):
                    for h in range(8):
                        dve.wait_ge(act_out.sem, ab + h + 1)
                        w = iw[0:nq, qt, h:h + 1]
                        if h == 0:
                            ins = dve.tensor_scalar(score[0:nq, 0:nk], relu_s[0:nq, 0, 0:nk], w, None, ALU.mult)
                        else:
                            ins = dve.scalar_tensor_tensor(score[0:nq, 0:nk], relu_s[0:nq, h, 0:nk], w, score[0:nq, 0:nk], ALU.mult, ALU.add)
                        chained(dve, ins, dve_step)
                    chained(dve, dve.tensor_tensor(score[0:nq, q0:nk], score[0:nq, q0:nk], causal[0:nq, 0:nk - q0], ALU.add), dve_step)
                    wk = work[0:nq, META:nk]
                    src = score[0:nq, META:nk]
                    for _ in range((KEEP - META) // 8):
                        chained(dve, dve.max(m8[0:nq, :], src), dve_step)
                        chained(dve, dve.match_replace(wk, m8[0:nq, :], src, TAKEN), dve_step)
                        src = wk
                    ch = chosen[0:nq, qt, 0:nk]
                    dve.memset(ch[:, 0:META], 0.0)
                    chained(dve, dve.tensor_scalar(ch[:, META:nk], wk, TAKEN * 0.9, NEG, ALU.is_gt, ALU.mult), dve_step)
                    dve.tensor_tensor(ch[:, q0:nk], ch[:, q0:nk], causal[0:nq, 0:nk - q0], ALU.add)
            pe_out.n += 8
            act_out.n += 8
            loaded.n += 16

            pb, ab, db, tb = pe_out.n, act_out.n, dve_out.n, pe_out2.n
            ob, cb = pe_out3.n, act_out2.n
            with nc.Block() as block:
                @block.tensor
                def _(pe):
                    for gr in range(2):
                        for j in range(4):
                            lo = 64 * (j % 2)
                            f = 2 * gr + j // 2
                            pe.matmul(ps[0:nq, 4 * gr + j, 0:nk], pj[lo:lo + 64, f, q0:q0 + nq], pj[lo:lo + 64, 4 + f, 0:nk],
                                      start=True, stop=False)
                            mm = pe.matmul(ps[0:nq, 4 * gr + j, 0:nk], tri[0:nq, 0 if nq == P else 2, 0:nq], bias[0:nq, 4 * gr + j, 0:nk],
                                           start=False, stop=True)
                        mm.then_inc(pe_out.sem, 1)
                    for gr in range(2):
                        pe.wait_ge(dve_out.sem, db + gr + 1)
                        for kt, (k0, kn) in enumerate(kts):
                            for j in range(4):
                                mm = pe.transpose(ps[0:kn, 4 * gr + kt, j * P:j * P + nq], prob[0:nq, 4 * gr + j, k0:k0 + kn],
                                                  ident[0:nq, 0:nq])
                            mm.then_inc(pe_out2.sem, 1)
                    for gr in range(2):
                        pe.wait_ge(act_out2.sem, cb + (gr + 1) * len(kts))
                        for j in range(4):
                            h, lo = 4 * gr + j, 64 * (j % 2)
                            for kt, (k0, kn) in enumerate(kts):
                                mm = pe.matmul(ps[lo:lo + 64, 4 * gr + 3, (j // 2) * P:(j // 2) * P + nq], va[0:kn, kt, h * 64:h * 64 + 64],
                                               (pT, pT2)[gr][0:kn, kt, j, 0:nq], start=(kt == 0), stop=(kt == len(kts) - 1))
                        mm.then_inc(pe_out3.sem, 1)

                @block.vector
                def _(dve):
                    for gr in range(2):
                        hs = slice(4 * gr, 4 * gr + 4)
                        pr = prob[0:nq, hs, 0:nk]
                        row = lambda c: small[0:nq, 16 + 16 * gr + 4 * c:20 + 16 * gr + 4 * c]
                        wide = lambda x: x.unsqueeze(2).broadcast_to((nq, 4, nk))
                        dve.wait_ge(pe_out.sem, pb + gr + 1)
                        mask = chosen[0:nq, qt, 0:nk].unsqueeze(1).broadcast_to((nq, 4, nk))
                        chained(dve, dve.scalar_tensor_tensor(pr, ps[0:nq, hs, 0:nk], DSA_D ** -0.5, mask, ALU.mult, ALU.add), dve_step)
                        chained(dve, dve.tensor_reduce(row(0), pr, AX_X, ALU.max), dve_step)
                        dve.tensor_tensor(pr, pr, wide(row(0)), ALU.subtract).then_inc(dve_out2.sem, 1)
                    for gr in range(2):
                        hs = slice(4 * gr, 4 * gr + 4)
                        pr = prob[0:nq, hs, 0:nk]
                        row = lambda c: small[0:nq, 16 + 16 * gr + 4 * c:20 + 16 * gr + 4 * c]
                        wide = lambda x: x.unsqueeze(2).broadcast_to((nq, 4, nk))
                        dve.wait_ge(act_out.sem, ab + gr + 1)
                        chained(dve, dve.tensor_reduce(row(1), pr, AX_X, ALU.add), dve_step)
                        chained(dve, dve.reciprocal(row(2), row(1)), dve_step)
                        dve.tensor_tensor(pr, pr, wide(row(2)), ALU.mult).then_inc(dve_out.sem, 1)
                    for gr in range(2):
                        dve.wait_ge(pe_out3.sem, ob + gr + 1)
                        dve.tensor_copy(cat[:, 2 * gr:2 * gr + 2, q0:q0 + nq],
                                        ps[:, 4 * gr + 3, 0:2 * P].rearrange("p (j q) -> p j q", j=2)[:, :, 0:nq])

                @block.scalar
                def _(act):
                    for gr in range(2):
                        pr = prob[0:nq, 4 * gr:4 * gr + 4, 0:nk]
                        act.wait_ge(dve_out2.sem, dve_out2.n + gr + 1)
                        act.activation(pr, pr, ACT.Exp).then_inc(act_out.sem, 1)
                    for gr in range(2):
                        for kt, (k0, kn) in enumerate(kts):
                            act.wait_ge(pe_out2.sem, tb + gr * len(kts) + kt + 1)
                            src = ps[0:kn, 4 * gr + kt, :].rearrange("p (h q) -> p h q", h=4)[:, :, 0:nq]
                            act.activation((pT, pT2)[gr][0:kn, kt, :, 0:nq], src, ACT.Copy).then_inc(act_out2.sem, 1)
            pe_out.n += 2
            pe_out2.n += 2 * len(kts)
            pe_out3.n += 2
            act_out.n += 2
            act_out2.n += 2 * len(kts)
            dve_out.n += 2
            dve_out2.n += 2

        inner = yf[:, 0:6 * T2].rearrange("p (b t q) -> p b t q", b=2, t=3)
        pb, db, ob, ab = pe_out.n, dve_out.n, pe_out3.n, act_out.n
        with nc.Block() as block:
            @block.tensor
            def _(pe):
                def scores(h):
                    b = h % 2
                    if h >= 2:
                        pe.wait_ge(dve_out.sem, db + h - 1)
                    for t, (k0, kn) in enumerate(token_tiles):
                        mm = pe.matmul(ps[0:kn, 3 * b + t, 0:T2 - k0], pj[:, 20 + h, k0:k0 + kn], pj[:, 16 + h, k0:T2], start=True, stop=True)
                    mm.then_inc(pe_out.sem, 1)

                scores(0)
                for h in range(RET_HEADS):
                    if h + 1 < RET_HEADS:
                        scores(h + 1)
                    pe.wait_ge(dve_out.sem, db + h + 1)
                    for f in range(2):
                        n = 2 * h + f
                        if n >= 2:
                            pe.wait_ge(act_out.sem, ab + n - 1)
                        for t, (k0, kn) in enumerate(token_tiles):
                            c0 = h * RET_DV + f * P
                            mm = pe.matmul(ps[:, 6 + f, k0:T2], vr[0:kn, t, c0:c0 + P], inner[0:kn, h % 2, t, 0:T2 - k0],
                                           start=(t == 0), stop=(t == 2), skip_group_check=True)
                        mm.then_inc(pe_out3.sem, 1)

            @block.vector
            def _(dve):
                for h in range(RET_HEADS):
                    dve.wait_ge(pe_out.sem, pb + h + 1)
                    if h >= 2:
                        dve.wait_ge(pe_out3.sem, ob + 2 * h - 2)
                    for t, (k0, kn) in enumerate(token_tiles):
                        ins = dve.tensor_tensor(inner[0:kn, h % 2, t, 0:T2 - k0], ps[0:kn, 3 * (h % 2) + t, 0:T2 - k0],
                                                decay[0:kn, h, 0:T2 - k0], ALU.mult)
                    ins.then_inc(dve_out.sem, 1)

            @block.scalar
            def _(act):
                for n in range(2 * RET_HEADS):
                    act.wait_ge(pe_out3.sem, ob + n + 1)
                    act.activation(cat[:, 4 + n, :], ps[:, 6 + n % 2, 0:T2], ACT.Copy).then_inc(act_out.sem, 1)
                act.activation(pj[:, 32:40, :], pj[:, 32:40, :], ACT.Silu)
        pe_out.n += RET_HEADS
        pe_out3.n += 2 * RET_HEADS
        dve_out.n += RET_HEADS
        act_out.n += 2 * RET_HEADS

        pb, db, ab, tb0 = pe_out.n, dve_out.n, act_out.n, std_ready.n
        sq2 = view(sqf, 0, 8, T2)
        dev = view(sqf, 8 * T2, 4, T2)
        with nc.Block() as block:
            @block.tensor
            def _(pe):
                for h in range(RET_HEADS):
                    for f in range(2):
                        mm = pe.matmul(ps[:, h, 0:T2], ones[:, :], cat[:, 4 + 2 * h + f, :], start=(f == 0), stop=(f == 1))
                    mm.then_inc(pe_out.sem, 1)
                for h in range(RET_HEADS):
                    pe.wait_ge(act_out.sem, ab + h + 1)
                    for f in range(2):
                        mm = pe.matmul(ps[:, 4 + h, 0:T2], ones[:, :], sq2[:, 2 * h + f, :], start=(f == 0), stop=(f == 1))
                mm.then_inc(pe_out.sem, 1)

            @block.vector
            def _(dve):
                for h in range(RET_HEADS):
                    dve.wait_ge(pe_out.sem, pb + h + 1)
                    for f in range(2):
                        r = cat[:, 4 + 2 * h + f, :]
                        ins = dve.scalar_tensor_tensor(r, ps[:, h, 0:T2], -1.0 / RET_DV, r, ALU.mult, ALU.add)
                    ins.then_inc(dve_out.sem, 1)
                dve.wait_ge(std_ready.sem, tb0 + 1)
                chained(dve, dve.reciprocal(dev, dev), dve_step)
                for n in range(8):
                    r = cat[:, 4 + n, :]
                    ins = dve.scalar_tensor_tensor(r, r, prm[:, 2, 112 + n:113 + n], dev[:, n // 2, :], ALU.mult, ALU.mult)
                chained(dve, ins, dve_step)
                dve.tensor_tensor(cat[:, 4:12, :], cat[:, 4:12, :], pj[:, 32:40, :], ALU.mult)

            @block.scalar
            def _(act):
                for h in range(RET_HEADS):
                    act.wait_ge(dve_out.sem, db + h + 1)
                    act.activation(sq2[:, 2 * h:2 * h + 2, :], cat[:, 4 + 2 * h:6 + 2 * h, :], ACT.Square).then_inc(act_out.sem, 1)
                act.wait_ge(pe_out.sem, pb + RET_HEADS + 1)
                act.activation(dev, ps[:, 4:8, 0:T2], ACT.Sqrt, bias=epsb[:, 0:1], scale=1.0 / RET_DV).then_inc(std_ready.sem, 1)
        pe_out.n += RET_HEADS + 1
        dve_out.n += RET_HEADS
        act_out.n += RET_HEADS
        std_ready.n += 1
        product(narrow(cat, cat_r), T2, copy_out(into(SQ, 0, T2)))
        add_to_h()
        conv_ffn(0)

        with nc.Block() as block:
            @block.sync
            def _(sp):
                sp.dma_start(tri[:, :, :], a["k_tri"]).then_inc(loaded.sem, 16)
                sp.wait_ge(loaded.sem, loaded.n + 16)
        loaded.n += 16
        gained(gain2(80), flat2, lambda k: Y[:, k, 0:T2], KD, T2)
        product(normed(T2), T2, copy_out(into(pj, 0, T2)))
        vs = view(exf, 0, 3, D)
        transposes([([pj[:, 16 + 4 * h + j, t0:t0 + tn] for j in range(4)], tn, P,
                     vs[0:tn, t, 4 * h * P:4 * (h + 1) * P].rearrange("p (j c) -> p j c", j=4))
                    for t, (t0, tn) in enumerate(token_tiles) for h in range(2)])
        offs = [0, T2, T2 + (T2 - P)]
        full_w, all_w = offs[2], offs[2] + T2 - 2 * P
        last = T2 - 2 * P
        zs, sp_, lg, aw = (sqf[:, 1000 * i:1000 * i + 864].rearrange("p (b n) -> p b n", b=2) for i in range(4))
        parts = [(slice(0, P), slice(0, full_w)), (slice(0, last), slice(full_w, all_w))]
        zd, spd, ld, inc, exps_, out_ = pe_out, dve_out, act_out, pe_out2, dve_out2, act_out2
        vd, kd_ = pe_out3, dve_out3
        z0, s0_, l0, i0, t0_, a0, v0, k0_, c0_ = (c.n for c in (zd, spd, ld, inc, exps_, out_, vd, kd_, scaled))

        with nc.Block() as block:
            @block.tensor
            def _(pe):
                def logits(h):
                    b, lo = h % 2, 64 * (h % 2)
                    if h >= 2:
                        pe.wait_ge(scaled.sem, c0_ + h - 1)
                    for t, (k0, kn) in enumerate(token_tiles):
                        mm = pe.matmul(ps[0:kn, b, offs[t]:offs[t] + T2 - k0], pj[lo:lo + 64, 8 + h // 2, k0:k0 + kn],
                                       pj[lo:lo + 64, h // 2, k0:T2], start=True, stop=True)
                    mm.then_inc(zd.sem, 1)

                logits(0)
                for h in range(SB_HEADS):
                    if h + 1 < SB_HEADS:
                        logits(h + 1)
                    b, lo = h % 2, 64 * (h % 2)
                    pe.wait_ge(spd.sem, s0_ + h + 1)
                    if h >= 2:
                        pe.wait_ge(exps_.sem, t0_ + h - 1)
                    for t, (k0, kn) in enumerate(token_tiles):
                        for u in range(t, 3):
                            u0, un = token_tiles[u]
                            c = offs[t] + u0 - k0
                            lhs = tri[0:kn, 0, 0:kn] if u == t else ones[0:un, 0:kn]
                            mm = pe.matmul(ps[0:kn, 2 + b, c:c + T2 - u0], lhs, sp_[0:un, b, offs[u]:offs[u] + T2 - u0],
                                           start=(u == t), stop=(u == 2), skip_group_check=True)
                    mm.then_inc(inc.sem, 1)
                    pe.wait_ge(out_.sem, a0 + h + 1)
                    if h >= 2:
                        pe.wait_ge(kd_.sem, k0_ + h - 1)
                    for t, (k0, kn) in enumerate(token_tiles):
                        mm = pe.matmul(ps[lo:lo + 64, 4 + b, k0:T2], vs[0:kn, t, h * 64:h * 64 + 64], aw[0:kn, b, offs[t]:offs[t] + T2 - k0],
                                       start=(t == 0), stop=(t == 2), skip_group_check=True)
                    mm.then_inc(vd.sem, 1)

            @block.scalar
            def _(act):
                def softplus_tail(h):
                    b = h % 2
                    act.wait_ge(scaled.sem, c0_ + h + 1)
                    if h >= 2:
                        act.wait_ge(spd.sem, s0_ + h - 1)
                    for r, c in parts:
                        ins = act.activation(lg[r, b, c], zs[r, b, c], ACT.Abs)
                    chained(act, ins, act_step)
                    for r, c in parts:
                        ins = act.activation(lg[r, b, c], lg[r, b, c], ACT.Exp, scale=-1.0)
                    chained(act, ins, act_step)
                    for r, c in parts:
                        ins = act.activation(lg[r, b, c], lg[r, b, c], ACT.Ln, bias=1.0)
                    ins.then_inc(ld.sem, 1)

                softplus_tail(0)
                for h in range(SB_HEADS):
                    if h + 1 < SB_HEADS:
                        softplus_tail(h + 1)
                    b = h % 2
                    act.wait_ge(exps_.sem, t0_ + h + 1)
                    if h >= 2:
                        act.wait_ge(vd.sem, v0 + h - 1)
                    for r, c in parts:
                        ins = act.activation(aw[r, b, c], zs[r, b, c], ACT.Exp)
                    ins.then_inc(out_.sem, 1)

            @block.vector
            def _(dve):
                def mask(buf, b, which, op):
                    for t, (k0, kn) in enumerate(token_tiles):
                        x = buf[0:kn, b, offs[t]:offs[t] + kn]
                        ins = dve.tensor_tensor(x, x, tri[0:kn, which, 0:kn], op)
                    return ins

                def softplus(h):
                    b = h % 2
                    dve.wait_ge(zd.sem, z0 + h + 1)
                    if h >= 2:
                        dve.wait_ge(out_.sem, a0 + h - 1)
                        dve.wait_ge(inc.sem, i0 + h - 1)
                    for r, c in parts:
                        ins = dve.tensor_scalar(zs[r, b, c], ps[r, b, c], SB_D ** -0.5, None, ALU.mult)
                    ins.then_inc(scaled.sem, 1)
                    dve.wait_ge(scaled.sem, c0_ + h + 1)
                    dve.wait_ge(ld.sem, l0 + h + 1)
                    for r, c in parts:
                        ins = dve.scalar_tensor_tensor(sp_[r, b, c], zs[r, b, c], 0.0, lg[r, b, c], ALU.max, ALU.add)
                    chained(dve, ins, dve_step)
                    mask(sp_, b, 1, ALU.mult).then_inc(spd.sem, 1)

                def keep(h):
                    b, lo = h % 2, 64 * (h % 2)
                    dve.wait_ge(vd.sem, v0 + h + 1)
                    dve.tensor_copy(cat[lo:lo + 64, h // 2, :], ps[lo:lo + 64, 4 + b, 0:T2]).then_inc(kd_.sem, 1)

                softplus(0)
                for h in range(SB_HEADS):
                    if h + 1 < SB_HEADS:
                        softplus(h + 1)
                    b = h % 2
                    dve.wait_ge(inc.sem, i0 + h + 1)
                    for r, c in parts:
                        ins = dve.tensor_tensor(zs[r, b, c], zs[r, b, c], ps[r, 2 + b, c], ALU.subtract)
                    chained(dve, ins, dve_step)
                    mask(zs, b, 2, ALU.add).then_inc(exps_.sem, 1)
                    if h >= 1:
                        keep(h - 1)
                keep(SB_HEADS - 1)
        for c in (zd, spd, ld, inc, exps_, out_, vd, kd_, scaled):
            c.n += SB_HEADS
        product(narrow(cat, cat_r), T2, copy_out(into(SQ, 0, T2)))
        add_to_h()
        conv_ffn(1)
        gained(gain2(104), flat2, lambda k: Y[:, k, 0:T2], KD, T2)
        finish(nc, a, out, H, XM, XM, sqf, stored, transposes, ctx, src=Y)


def constants():
    import numpy as np
    f = np.float32
    k = np.arange(P)
    c = {"k_ident": np.eye(P, dtype=f), "k_ones": np.ones((P, P), f)}

    def swap_of(dim, offset, quarter, period):
        R = np.zeros((P, P), f)
        for i in range(offset, dim):
            r = (i - offset) % period
            if r < quarter:
                R[i, i + quarter] = -1
            else:
                R[i, i - quarter] = 1
        return R.T

    swap = np.stack([swap_of(P, 0, 16, 32), swap_of(96, 64, 8, 16), swap_of(P, 0, 64, 128)], 1)
    c["k_swap"] = np.ascontiguousarray(swap)
    c["k_tri"] = np.ascontiguousarray(np.stack([
        (k[:, None] >= k[None, :]).astype(f),
        (k[:, None] < k[None, :]).astype(f),
        np.where(k[:, None] < k[None, :], 0, NEG).astype(f)], 1))
    short = np.zeros((P, P), f)
    n = T2 - 2 * P
    short[:n, :n] = np.eye(n)[::-1] * DSA_D ** 0.5
    c["k_sparse"] = np.ascontiguousarray(np.stack([
        np.eye(P, dtype=f)[::-1] * f(DSA_D ** 0.5), np.where(k[None, :] > k[:, None], NEG, 0).astype(f), short], 1))

    def angles(n_tokens, dim):
        t = np.arange(n_tokens)
        nf = dim // 4
        freqs = (f(10000.0) ** (-np.arange(nf, dtype=f) / f(nf))).astype(f)
        pos = np.stack([(t // 64).astype(f), (t % 64).astype(f)], 0)
        ang = pos[:, None, :] * freqs[None, :, None]
        return np.concatenate([ang[ax] for ax in (0, 0, 1, 1)], 0)

    first = np.zeros((P, 2304), f)
    th = 2 * np.pi * np.outer(k, k) / P
    first[:, 0:128], first[:, 128:256] = np.cos(th), np.sin(th)
    t = np.arange(SEQ)
    tt = 2 * np.pi * (np.outer(t, t) % SEQ) / SEQ
    s = 1.0 / np.sqrt(SEQ * P)
    d2 = np.stack([np.cos(tt) * s, -np.sin(tt) * s], 1).reshape(2, P, 2, SEQ).transpose(1, 0, 2, 3)
    first[:, 256:1280] = d2.reshape(P, 1024)
    da = np.tile(angles(SEQ, 64), (2, 1))
    first[:, 1280:1536], first[:, 1536:1792] = np.cos(da), np.sin(da)
    first[:, 1792:2048] = 1
    ml = angles(SEQ, 32)
    first[64:96, 1792:2048], first[64:96, 2048:2304] = np.cos(ml), np.sin(ml)
    c["k_first"] = first

    second = np.zeros((P, 2304), f)
    inv = (f(1) / (f(10000.0) ** (np.arange(64, dtype=f) / f(64)))).astype(f)
    ang = np.arange(T2, dtype=f)[None, :] * np.tile(inv, 2)[:, None]
    second[:, 0:T2], second[:, T2:2 * T2] = np.cos(ang), np.sin(ang)
    diff = np.arange(T2)[None, :] - k[:, None]
    for h in range(RET_HEADS):
        lg = np.log(1.0 - 2.0 ** (-5.0 - h))
        second[:, (2 + h) * T2:(3 + h) * T2] = np.where(diff >= 0, np.exp(np.maximum(diff, 0) * lg), 0) * RET_DK ** -0.5
    c["k_second"] = second

    dist = np.maximum(T2 - 1 - np.arange(BIAS_W), 0)
    large = 16 + (np.log(np.maximum(dist, 1).astype(f) / f(16)) / f(np.log(8.0)) * f(16)).astype(np.int32)
    bucket = np.where(dist < 16, dist, np.minimum(large, 31))
    c["k_bucket"] = (np.arange(32)[:, None] == bucket[None, :]).astype(f)
    return c


def kernel(**inputs):
    import numpy as np
    import concourse.bacc as bacc
    from concourse.bass_utils import run_bass_kernel_spmd as run

    nc = bacc.Bacc("TRN2", target_bir_lowering=False, num_devices=1)
    arrays, args = {}, {}
    for name, value in [*inputs.items(), *constants().items()]:
        v = np.ascontiguousarray(value)
        arrays[f"in_{name}"] = v
        args[name] = nc.dram_tensor(f"in_{name}", v.shape, mybir.dt.from_np(v.dtype), kind="ExternalInput").ap()
    out = nc.dram_tensor("out_0", (1, SEQ, D), F32, kind="ExternalOutput").ap()
    bias_rows = nc.dram_tensor("bias_rows", (DSA_HEADS, BIAS_W), F32, kind="Internal").ap()
    build(nc, args, out, bias_rows)
    r = run(nc, [arrays], core_ids=[0])
    return r.results[0]["out_0"]
```

```python
from contextlib import ExitStack

import concourse.bass as bass
from concourse import mybir

ALU = mybir.AluOpType
ACT = mybir.ActivationFunctionType
F32 = mybir.dt.float32
F32R = mybir.dt.float32r
AX_X = mybir.AxisListType.X

P = 128
D = 1024
KD = D // P
SEQ = 256
CTX = 256
TB = SEQ + CTX
META = 16
T2 = META + SEQ
DFF = 2816
KF = DFF // P
EPS = 1e-6
NEG = -1e30
TAKEN = -3e38
BANK = 512
SLOTS = 4
HI_SLOTS = 2
NB = 4
KG = 8

DA_HEADS, DA_DK, DA_DV = 8, 64, 128
MLA_HEADS, MLA_NOPE, MLA_ROPE, MLA_DV = 8, 64, 32, 64
MLA_DQK = MLA_NOPE + MLA_ROPE
DA_SCALE = DA_DK ** -0.5
MLA_SCALE = MLA_DQK ** -0.5
Q_COLS = 1024 + 384
LAM_INIT = 0.8 - 0.6 * 2.718281828459045 ** -0.3
DSA_HEADS, DSA_D = 8, 64
KEEP = min(256, SEQ // 4)
RET_HEADS, RET_DK, RET_DV = 4, 128, 256
SB_HEADS, SB_D = 16, 64
BIAS_W = 400


class Count:

    def __init__(self, sem):
        self.sem, self.n = sem, 0


def chained(eng, ins, count):
    ins.then_inc(count.sem, 1)
    count.n += 1
    eng.wait_ge(count.sem, count.n)


def signal(ins, count):
    ins.then_inc(count.sem, 1)
    count.n += 1


class Gemm:

    def __init__(self, name, K, pairs, half=P, last=None, side=None, only_side=False):
        self.name, self.kt = name, K // P
        self.only_side = only_side
        self.groups = 0 if only_side else -(-self.kt // KG)
        self.kg = KG
        self.pairs, self.half, self.side = pairs, half, side
        self.last = last or (half, half)
        self.per_pair = self.groups + (side is not None)
        self.units = len(pairs) * self.per_pair
        self.per_rot = SLOTS
        self.rot_units = self.per_rot * self.per_pair
        self.full = (len(pairs) - (last is not None)) // self.per_rot

    def widths(self, p):
        return self.last if p == len(self.pairs) - 1 else (self.half, self.half)

    def source(self, unit, rot=0):
        pair, g = unit // self.per_pair, unit % self.per_pair - (self.per_pair - self.groups)
        if g < 0:
            w, _, first = self.side
            c0, step, width, k0, kn = 256 * (first + pair), 256 * self.per_rot, 256, 0, KD
        else:
            w, c0 = self.pairs[pair]
            k0, kn = g * self.kg, min(self.kg, self.kt - g * self.kg)
            width = sum(self.widths(pair))
            step = 0 if isinstance(rot, int) else self.pairs[pair + self.per_rot][1] - c0
        rows = w[k0 * P:(k0 + kn) * P, :].rearrange("(k p) n -> p k n", p=P)
        if isinstance(rot, int):
            return rows[:, :, c0:c0 + width], kn, width
        return rows[:, :, bass.ds(rot * step + c0, width)], kn, width


def finish(nc, a, out, H, XM, Y, sqf, stored, transposes, ctx, src=None):
    src = src or H
    tok = Y[:, :, :].rearrange("p a b -> p (a b)")[:, 0:2 * D].rearrange("p (t n) -> p t n", t=2)
    transposes([([src[:, 4 * h + j, META + t * P:META + (t + 1) * P] for j in range(4)], P, P,
                 tok[:, t, 4 * h * P:4 * (h + 1) * P].rearrange("p (j c) -> p j c", j=4)) for t in range(2) for h in range(2)])
    with nc.Block() as block:
        @block.sync
        def _(sp):
            sp.dma_start(out[0].rearrange("(t p) n -> p t n", p=P), tok).then_inc(stored.sem, 16)
            stored.n += 16
            sp.wait_ge(stored.sem, stored.n)


def build(nc, a, out, bias_rows):
    ctx = ExitStack()
    with ctx:
        def sb(name, shape):
            return ctx.enter_context(nc.sbuf_tensor(name, shape, F32))

        def sb_split(name, shape):
            at = nc.sbuf_base
            return sb(name, shape), nc.alloc_sbuf_tensor_at(name + "_r", shape, F32R, offset=at)

        def sem(name):
            return Count(ctx.enter_context(nc.semaphore(name)))

        H = sb("H", [P, KD, T2 + CTX])
        XM, XM_R = sb_split("XM", [P, KD, TB])
        Y, Y_R = sb_split("Y", [P, KD, TB])
        SQ, SQ_R = sb_split("SQ", [P, KD, 2 * T2])
        GU, GU_R = sb_split("GU", [P, KF * TB])
        EX, EX_R = sb_split("EX", [P, 6144])
        ring, ring_lo = sb_split("ring", [P, SLOTS, KG, 256])
        ring_hi = ctx.enter_context(nc.sbuf_tensor("ring_hi", [P, HI_SLOTS, KG, 256], F32R))
        ident = sb("ident", [P, P])
        ones = sb("ones", [P, P])
        swap = sb("swap", [P, 3, P])
        tri = sb("tri", [P, 3, P])
        kb = sb("kb", [P, 2304])
        dft1 = kb[:, 0:256]
        dft2 = kb[:, 256:1280].rearrange("p (t c n) -> p t c n", t=2, c=2)
        rope_da = kb[:, 1280:1792].rearrange("p (c t) -> p c t", c=2)
        rope_mla = kb[:, 1792:2304].rearrange("p (c t) -> p c t", c=2)
        rope_ret = kb[:, 0:2 * T2].rearrange("p (c t) -> p c t", c=2)
        decay = kb[:, 2 * T2:6 * T2].rearrange("p (h t) -> p h t", h=RET_HEADS)
        prm = sb("prm", [P, 5, P])
        cs = sb("cs", [P, KD, 2])
        mod = sb("mod", [P, 2, 72, 2])
        co = sb("co", [P, 9, KD, 2])
        adac = sb("adac", [P, 2, 256])
        std = sb("std", [P, TB])
        rstd = sb("rstd", [P, TB])
        epsb = sb("epsb", [P, 1])
        lam4 = sb("lam4", [1, 4, 64])
        lamv = sb("lamv", [1, 8])
        nlam = sb("nlam", [P, 2])
        gsub = sb("gsub", [P, 1])
        small = sb("small", [P, 64])
        ps = ctx.enter_context(nc.psum_tensor("ps", [P, 8, BANK], F32))

        loaded = sem("loaded")
        slot_loaded = [sem(f"slot_loaded{i}") for i in range(SLOTS)]
        w_used = sem("w_used")
        w_hi = sem("w_hi")
        w_split = sem("w_split")
        rhs_hi = sem("rhs_hi")
        rhs_split = sem("rhs_split")
        first_done = sem("first_done")
        act_freed = sem("act_freed")
        dve_freed = sem("dve_freed")
        side_step = sem("side_step")
        side_read = sem("side_read")
        side_summed = sem("side_summed")
        side_freed = sem("side_freed")
        conv_step = sem("conv_step")
        conv_done = sem("conv_done")
        silu_done = sem("silu_done")
        dve_step, act_step, pool_step = (sem(x) for x in ("dve_step", "act_step", "pool_step"))
        sq_ready = sem("sq_ready")
        sq_added = sem("sq_added")
        h_ready = sem("h_ready")
        sum_ready = sem("sum_ready")
        std_ready = sem("std_ready")
        rstd_ready = sem("rstd_ready")
        scaled = sem("scaled")
        pool_scaled = sem("pool_scaled")
        pool_h_ready = sem("pool_h_ready")
        pe_out = sem("pe_out")
        act_out = sem("act_out")
        dve_out = sem("dve_out")
        pe_out2 = sem("pe_out2")
        pe_out3 = sem("pe_out3")
        dve_out3 = sem("dve_out3")
        act_out2 = sem("act_out2")
        dve_out2 = sem("dve_out2")
        stored = sem("stored")

        def cols(w, c0, n):
            return [(w, c0 + 256 * i) for i in range(n)]

        def gate_up(wg, g0, wu, u0):
            return [x for j in range(DFF // 256) for x in ((wg, g0 + 256 * j), (wu, u0 + 256 * j))]

        def mod_gemm(layer, first, n):
            return Gemm("mod", D, [None] * n, side=(a["w_mod"][layer], layer, first), only_side=True)

        def ffn_gemms(layer, s, side=None):
            w = a["w_ffn_in"][layer, s]
            return [Gemm("ffn_in", D, gate_up(w, 0, w, DFF), side=side), Gemm("ffn_out", DFF, cols(a["w_ffn_out"][layer, s], 0, 4))]

        def ffn2_gemms(layer):
            return [Gemm("ffn2_in", D, gate_up(a["ffn_w_gate_2"][layer], 0, a["ffn_w_up_2"][layer], 0)),
                    Gemm("ffn2_out", DFF, cols(a["ffn_w_down_2"][layer], 0, 4))]

        w_in_odd = a["w_in_odd"][0]
        w_in_2 = a["even_w_in_2"][0]
        MOD_PAIRS = 36
        AT_ONCE = MOD_PAIRS - DFF // 128
        LEFT = MOD_PAIRS - DFF // 128 - 12
        w_mod = [a["w_mod"][layer] for layer in range(2)]
        plan = [mod_gemm(0, 0, AT_ONCE), *ffn_gemms(0, 0, side=(w_mod[0], 0, AT_ONCE)),
                Gemm("even_in", D, cols(a["w_in_even"][0], 0, 8), side=(w_mod[1], 1, 0)),
                Gemm("even_out", D, cols(a["w_out_even"][0], 0, 4), side=(w_mod[1], 1, 8)),
                *ffn_gemms(0, 1, side=(w_mod[1], 1, 12)),
                mod_gemm(1, MOD_PAIRS - LEFT, LEFT), *ffn_gemms(1, 0),
                Gemm("odd_q", D, cols(w_in_odd, 0, 6), last=(P, 0)),
                Gemm("odd_kv", D, cols(w_in_odd, Q_COLS, 10), last=(MLA_ROPE, 0)),
                Gemm("uq", 384, [(a["w_uq"][0], 192 * i) for i in range(4)], half=MLA_DQK),
                Gemm("uk", 256, [(a["w_uk"][0], 128 * i) for i in range(4)], half=MLA_NOPE),
                Gemm("uv", 256, cols(a["w_uv"][0], 0, 2)),
                Gemm("odd_out", 1536, cols(a["w_out_odd"][0], 0, 4)), *ffn_gemms(1, 1),
                Gemm("even2_a", D, cols(w_in_2, 0, 8)),
                Gemm("even2_i", D, [(w_in_2, 2048)], last=(64, 8)),
                Gemm("even2_b", D, cols(w_in_2, 2120, 12)),
                Gemm("even2_out", 1536, cols(a["even_w_out_2"][0], 0, 4)), *ffn2_gemms(0),
                Gemm("odd2_in", D, cols(a["odd_w_in_2"][0], 0, 12)),
                Gemm("odd2_out", D, cols(a["odd_w_out_2"][0], 0, 4)), *ffn2_gemms(1)]
        first_unit = [0]
        for g in plan:
            first_unit.append(first_unit[-1] + g.units)
        at = [0]
        kinds, seen = [], [0, 0]
        weight_units = []
        for g in plan:
            for u in range(g.units):
                side = g.side is not None and u % g.per_pair == 0
                if not side:
                    weight_units.append((len(kinds), *g.source(u)[1:]))
                kinds.append((side, seen[side]))
                seen[side] += 1

        def load_unit(sp, g, unit, n, rot=0, turn=0):
            src, kn, width = g.source(unit, rot)
            slot = n % SLOTS
            if n >= SLOTS or not isinstance(turn, int):
                m = n - SLOTS + (0 if isinstance(turn, int) else g.rot_units)
                side, before = kinds[m]
                step = g.per_rot * (1 if side else g.groups)
                count = side_read if side else w_used
                if isinstance(turn, int):
                    sp.wait_ge(count.sem, before + 1)
                else:
                    sp.wait_ge(count.sem, (turn - 1) * step + before + 1)
            sp.dma_start(ring[:, slot, 0:kn, 0:width], src).then_inc(slot_loaded[slot].sem, 16)

        def load_ahead(sp, p):
            lo, hi = first_unit[p] + SLOTS, min(first_unit[p + 1] + SLOTS, first_unit[-1])
            g, base = plan[p], first_unit[p]
            n = lo
            if g.full > 2:
                while n < base + g.rot_units:
                    load_unit(sp, g, n - base, n)
                    n += 1
                with sp.Fori(1, g.full) as r:
                    for i in range(g.rot_units):
                        load_unit(sp, g, i, base + i, rot=r, turn=r)
                n = base + g.rot_units * g.full
            while n < hi:
                q = max(i for i in range(len(plan)) if first_unit[i] <= n)
                load_unit(sp, plan[q], n - first_unit[q], n)
                n += 1

        def rotations(eng, g, body):
            def run(r, first=False):
                for i in range(g.per_rot):
                    body(i, r, first)
            done = 1 if g.full > 0 else 0
            if done:
                run(0, True)
            if g.full > 2:
                with eng.Fori(1, g.full) as r:
                    run(r)
                done = g.full
            for p in range(done * g.per_rot, len(g.pairs)):
                body(p % g.per_rot, p // g.per_rot, p < g.per_rot)

        def landed(eng, n, r=0, rot_units=0):
            eng.wait_ge(slot_loaded[n % SLOTS].sem, r * (16 * (rot_units // SLOTS)) + 16 * (n // SLOTS + 1))

        def split_weights(eng, who, w, r=0, step=0, rot_units=0):
            if w >= len(weight_units):
                return
            n, kn, width = weight_units[w]
            halves = [slice(0, (kn + 1) // 2), slice((kn + 1) // 2, kn)]
            if who == "act":
                if w >= HI_SLOTS or not isinstance(r, int):
                    eng.wait_ge(w_used.sem, r * step + w - HI_SLOTS + 1)
                landed(eng, n, r, rot_units)
            for i, ks in enumerate(halves):
                raw, hi = ring[:, n % SLOTS, ks, 0:width], ring_hi[:, w % HI_SLOTS, ks, 0:width]
                if who == "act":
                    eng.activation(hi, raw, ACT.Copy).then_inc(w_hi.sem, 1)
                else:
                    eng.wait_ge(w_hi.sem, r * (2 * step) + 2 * w + i + 1)
                    eng.tensor_tensor(ring_lo[:, n % SLOTS, ks, 0:width], raw, hi, ALU.subtract).then_inc(w_split.sem, 1)

        class Split:

            def __init__(self, src, hi, lo):
                self.src, self.hi, self.lo = src, hi, lo

        def product(x, T, evac, group=1, fresh=True):
            p = at[0]
            at[0] += 1
            g, base = plan[p], first_unit[p]
            assert base == w_used.n + side_read.n
            ub, rb_ = w_used.n, side_read.n
            extra = g.per_pair - g.groups
            fb, ab, db, mb = first_done.n, act_freed.n, dve_freed.n, side_summed.n
            hb, xb = rhs_hi.n, rhs_split.n
            unit_step = g.per_rot * g.groups

            def owner(i):
                return "act" if i % (2 * group) < group else "dve"

            def order(i):
                return i // (2 * group) * group + i % group

            def widths(i, r):
                return g.widths(r * g.per_rot + i) if isinstance(r, int) else (g.half, g.half)

            class Tile:
                def __init__(self, i, r, m):
                    t = 2 * i + m
                    self.t, self.m, self.w = r * (2 * g.per_rot) + t, m, widths(i, r)[m]
                    self.owner = owner(t)
                    self.src = ps[0:self.w, t % NB:t % NB + 1, 0:T]
                    self.first = isinstance(r, int) and r == 0
                    self.n = r * g.per_rot + order(t)
                    self.local = order(t)
                    alone = widths(i, r)[1] == 0
                    if m == 0 and not alone:
                        self.ready = (first_done, r * g.per_rot + fb + i + 1)
                    else:
                        self.ready = (w_used, r * (g.per_rot * g.groups) + ub + (i + 1) * g.groups)

                def wait(self, eng):
                    eng.wait_ge(self.ready[0].sem, self.ready[1])

            with nc.Block() as block:
                @block.sync
                def _(sp):
                    load_ahead(sp, p)

                @block.tensor
                def _(pe):
                    def pair(i, r, first):
                        w = widths(i, r)
                        for gr in range(g.groups):
                            n, w_ = base + i * g.per_pair + extra + gr, ub + i * g.groups + gr
                            kn = min(g.kg, g.kt - gr * g.kg)
                            for m in range(2 if w[1] else 1):
                                t = 2 * i + m
                                if gr == 0 and not (first and t < NB):
                                    freed, b0 = (act_freed, ab) if owner(t) == "act" else (dve_freed, db)
                                    pe.wait_ge(freed.sem, r * g.per_rot + b0 + order(t) - order(NB) + 1)
                                c = slice(m * w[0], m * w[0] + w[m])
                                for k in range(kn):
                                    kx = gr * g.kg + k
                                    if m == 0 and k in (0, (kn + 1) // 2):
                                        pe.wait_ge(w_split.sem, r * (2 * unit_step) + 2 * w_ + (1 if k == 0 else 2))
                                    if fresh and first and i == 0 and m == 0:
                                        pe.wait_ge(rhs_split.sem, xb + kx + 1)
                                    hi, lo = ring_hi[:, w_ % HI_SLOTS, k, c], ring_lo[:, n % SLOTS, k, c]
                                    passes = [(hi, x.hi(kx)[:, 0:T]), (hi, x.lo(kx)[:, 0:T]), (lo, x.hi(kx)[:, 0:T])]
                                    for j, (lhs, rhs) in enumerate(passes):
                                        mm = pe.matmul(ps[0:w[m], t % NB, 0:T], lhs, rhs, start=(kx == 0 and j == 0),
                                                       stop=(kx == g.kt - 1 and j == 2))
                                if m == 0 and w[1] and gr == g.groups - 1:
                                    mm.then_inc(first_done.sem, 1)
                            mm.then_inc(w_used.sem, 1)
                        if g.side:
                            adaln_sum(pe, r * g.per_rot + rb_ + i + 1)
                    rotations(pe, g, pair)

                def split_input(eng, who, gr):
                    for k in range(gr * g.kg, min(gr * g.kg + g.kg, g.kt)):
                        if who == "act":
                            eng.activation(x.hi(k), x.src(k), ACT.Copy).then_inc(rhs_hi.sem, 1)
                        else:
                            eng.wait_ge(rhs_hi.sem, hb + k + 1)
                            eng.tensor_tensor(x.lo(k), x.src(k), x.hi(k), ALU.subtract).then_inc(rhs_split.sem, 1)

                def evacuate(eng, who):
                    def pair(i, r, first):
                        if g.side and who == "dve":
                            if fresh and first and i == 0:
                                split_input(eng, who, 0)
                            landed(eng, base + i * g.per_pair, r, g.rot_units)
                            adaln_products(eng, (base + i * g.per_pair) % SLOTS, r * g.per_rot + i)
                        for gr in range(g.groups):
                            if fresh and first and i == 0 and not (g.side and who == "dve"):
                                split_input(eng, who, gr)
                            w_ = ub + i * g.groups + gr + 1
                            if isinstance(r, int):
                                split_weights(eng, who, w_ + r * unit_step)
                            else:
                                split_weights(eng, who, w_, r, unit_step, g.rot_units)
                        for m in range(2):
                            if widths(i, r)[m]:
                                tile = Tile(i, r, m)
                                evac(eng, tile.owner == who, tile)
                        if g.side and who == "dve":
                            adaln_columns(eng, g.side[1], r * (2 * g.per_rot) + 2 * (g.side[2] + i), r * g.per_rot + mb + i + 1)
                    rotations(eng, g, pair)

                @block.scalar
                def _(act):
                    evacuate(act, "act")

                @block.vector
                def _(dve):
                    evacuate(dve, "dve")

            w_used.n += len(g.pairs) * g.groups
            tiles = [(p_, m) for p_ in range(len(g.pairs)) for m in range(2) if g.widths(p_)[m]]
            first_done.n += sum(1 for p_ in range(len(g.pairs)) if g.widths(p_)[1])
            act_freed.n += sum(owner(2 * p_ + m) == "act" for p_, m in tiles)
            dve_freed.n += sum(owner(2 * p_ + m) == "dve" for p_, m in tiles)
            if g.side:
                side_done(len(g.pairs))
            if fresh:
                rhs_hi.n += g.kt
                rhs_split.n += g.kt

        def copy_out(dest):
            def evac(eng, mine, tile):
                if not mine:
                    return
                tile.wait(eng)
                if tile.owner == "act":
                    eng.activation(dest(tile), tile.src, ACT.Copy).then_inc(act_freed.sem, 1)
                else:
                    eng.tensor_copy(dest(tile), tile.src).then_inc(dve_freed.sem, 1)
            return evac

        sq2 = EX[:, 4096:4096 + 2 * TB].rearrange("p (b t) -> p b t", b=2)
        acc = EX[:, 5120:5120 + TB]

        def with_squares(T, slot=None):
            add = slot is None
            qb, eb, ab, db = sq_ready.n, sq_added.n, act_freed.n, dve_freed.n
            sq_ready.n += KD
            sq_added.n += KD

            def add_square(dve, n):
                dve.wait_ge(sq_ready.sem, qb + n + 1)
                if n == 0:
                    ins = dve.tensor_copy(acc[:, 0:T], sq2[:, 0, 0:T])
                else:
                    dve.wait_ge(sq_added.sem, eb + n)
                    ins = dve.tensor_tensor(acc[:, 0:T], acc[:, 0:T], sq2[:, n % 2, 0:T], ALU.add)
                ins.then_inc(sq_added.sem, 1)

            def evac(eng, mine, tile):
                n, is_act = tile.t, (tile.owner == "act") == mine
                freed, base = (act_freed, ab) if tile.owner == "act" else (dve_freed, db)
                src = ps[:, n % NB, 0:T]

                def gated(write):
                    for lo, hi, s in streams(T):
                        ins = write(SQ[:, n, lo:hi], src[:, lo:hi], co[:, 3 * slot + 2, n, s:s + 1])
                    ins.then_inc(freed.sem, 1)

                if is_act:
                    if n == 0:
                        eng.activation(small[:, 63:64], epsb[:, 0:1], ACT.Sqrt)
                    if n >= 2:
                        eng.wait_ge(sq_added.sem, eb + n - 1)
                    if add:
                        eng.wait_ge(freed.sem, base + n // 2 + 1)
                    else:
                        tile.wait(eng)
                    eng.activation(sq2[:, n % 2, 0:T], H[:, n, 0:T] if add else src, ACT.Square).then_inc(sq_ready.sem, 1)
                    if mine and not add:
                        gated(lambda dst, x, c: eng.activation(dst, x, ACT.Copy, scale=c))
                else:
                    if add:
                        tile.wait(eng)
                        eng.tensor_tensor(H[:, n, 0:T], H[:, n, 0:T], src, ALU.add).then_inc(freed.sem, 1)
                    elif mine:
                        eng.wait_ge(sq_ready.sem, qb + n + 1)
                        gated(lambda dst, x, c: eng.tensor_scalar(dst, x, c, None, ALU.mult))
                    if n >= 1:
                        add_square(eng, n - 1)
                    if n == KD - 1:
                        add_square(eng, n)
            return evac

        def into(buf, first_tile=0, T=TB):
            return lambda tile: buf[0:tile.w, bass.ds(tile.t + first_tile, 1), 0:T]

        def adaln_products(dve, slot, pair):
            for k in range(KD):
                for s in range(2):
                    w = ring[:, slot, k, :]
                    if k == 0:
                        ins = dve.tensor_scalar(adac[:, s, :], w, cs[:, k, s:s + 1], None, ALU.mult)
                    else:
                        ins = dve.scalar_tensor_tensor(adac[:, s, :], w, cs[:, k, s:s + 1], adac[:, s, :], ALU.mult, ALU.add)
                if k < KD - 1:
                    ins.then_inc(side_step.sem, 1)
                    dve.wait_ge(side_step.sem, (KD - 1) * pair + side_step.n + k + 1)
                else:
                    ins.then_inc(side_read.sem, 1)

        def adaln_sum(pe, count):
            pe.wait_ge(side_read.sem, count)
            for m in range(2):
                for s in range(2):
                    mm = pe.matmul(ps[:, 7, 2 * m + s:2 * m + s + 1], adac[:, s, m * P:(m + 1) * P], ones[:, 0:1], start=True, stop=True)
            mm.then_inc(side_summed.sem, 1)

        def adaln_columns(dve, layer, tile, count):
            dve.wait_ge(side_summed.sem, count)
            b = prm[:, 1 + layer, bass.ds(tile, 2)].unsqueeze(2).broadcast_to((P, 2, 2))
            dve.tensor_tensor(mod[:, layer, bass.ds(tile, 2), :], ps[:, 7, 0:4].rearrange("p (t s) -> p t s", s=2), b,
                              ALU.add).then_inc(side_freed.sem, 1)

        def side_done(pairs):
            side_read.n += pairs
            side_summed.n += pairs
            side_freed.n += pairs
            side_step.n += (KD - 1) * pairs

        def adaln(layer, first):
            p = at[0]
            at[0] += 1
            g, base = plan[p], first_unit[p]
            assert base == w_used.n + side_read.n
            n_pairs = len(g.pairs)
            as_rows = SQ[0:2, :, :].rearrange("p a b -> p (a b)")
            pb, ab = pe_out.n, act_out.n
            with nc.Block() as block:
                @block.sync
                def _(sp):
                    load_ahead(sp, p)

                @block.tensor
                def _(pe):
                    def turn(i):
                        pe.wait_ge(act_out.sem, ab + i + 1)
                        for t in (2 * i, 2 * i + 1):
                            mm = pe.transpose(ps[:, 7, 2 * t:2 * t + 2], as_rows[:, t * P:(t + 1) * P], ident[0:2, 0:2])
                        return mm

                    for i in range(n_pairs):
                        n = base + i
                        landed(pe, n)
                        for k in range(KD):
                            mm = pe.matmul(ps[0:2, i % 7, 0:256], cs[:, k, :], ring[:, n % SLOTS, k, :], start=(k == 0), stop=(k == KD - 1))
                        mm.then_inc(side_read.sem, 1)
                        if i >= 1:
                            turn(i - 1)
                    turn(n_pairs - 1).then_inc(pe_out.sem, 1)

                @block.scalar
                def _(act):
                    for i in range(n_pairs):
                        act.wait_ge(side_read.sem, side_read.n + i + 1)
                        act.activation(as_rows[:, i * 256:(i + 1) * 256], ps[0:2, i % 7, 0:256], ACT.Copy).then_inc(act_out.sem, 1)
                    if w_used.n == 0:
                        split_weights(act, "act", 0)

                @block.vector
                def _(dve):
                    if w_used.n == 0:
                        split_weights(dve, "dve", 0)
                    dve.wait_ge(pe_out.sem, pb + 1)
                    b = prm[:, 1 + layer, 2 * first:2 * (first + n_pairs)].unsqueeze(2).broadcast_to((P, 2 * n_pairs, 2))
                    dve.tensor_tensor(mod[:, layer, 2 * first:2 * (first + n_pairs), :],
                                      ps[:, 7, 0:4 * n_pairs].rearrange("p (t s) -> p t s", s=2), b, ALU.add)
            side_read.n += n_pairs
            pe_out.n += 1
            act_out.n += n_pairs

        def coefficients(layer, slots):
            with nc.Block() as block:
                @block.vector
                def _(dve):
                    for slot in slots:
                        pre = prm[:, 0, layer * 48 + 16 * slot:layer * 48 + 16 * slot + 8]
                        post = prm[:, 0, layer * 48 + 16 * slot + 8:layer * 48 + 16 * slot + 16]
                        for s in range(2):
                            m = [mod[:, layer, (3 * slot + j) * 8:(3 * slot + j + 1) * 8, s] for j in range(3)]
                            dve.scalar_tensor_tensor(co[:, 3 * slot, :, s], m[1], 1.0, pre, ALU.add, ALU.mult)
                            dve.tensor_copy(co[:, 3 * slot + 1, :, s], m[0])
                            dve.scalar_tensor_tensor(co[:, 3 * slot + 2, :, s], m[2], 1.0 if slot == 1 else 0.5, post,
                                                     ALU.mult, ALU.mult)

        def norm(src, Kt, T, dve_part, act_part=None, dim=None, squared=False, pe_part=None, pool_part=None):
            dim = dim or Kt * P
            qb, mb, tb_, rb_ = sq_ready.n, sum_ready.n, std_ready.n, rstd_ready.n
            with nc.Block() as block:
                @block.scalar
                def _(act):
                    for k in range(0 if squared else Kt):
                        act.activation(SQ[:, k, 0:T], src(k), ACT.Square).then_inc(sq_ready.sem, 1)
                    act.wait_ge(sum_ready.sem, mb + 1)
                    act.activation(std[:, 0:T], ps[:, 7, 0:T], ACT.Sqrt, bias=epsb[:, 0:1], scale=1.0 / dim).then_inc(std_ready.sem, 1)
                    if act_part:
                        act_part(act)

                @block.tensor
                def _(pe):
                    if squared:
                        mm = pe.matmul(ps[:, 7, 0:T], ones[:, :], acc[:, 0:T], start=True, stop=True)
                    else:
                        for k in range(Kt):
                            pe.wait_ge(sq_ready.sem, qb + k + 1)
                            mm = pe.matmul(ps[:, 7, 0:T], ones[:, :], SQ[:, k, 0:T], start=(k == 0), stop=(k == Kt - 1))
                    mm.then_inc(sum_ready.sem, 1)
                    if pe_part:
                        pe_part(pe)

                @block.vector
                def _(dve):
                    dve.wait_ge(std_ready.sem, tb_ + 1)
                    dve.reciprocal(rstd[:, 0:T], std[:, 0:T]).then_inc(rstd_ready.sem, 1)
                    dve.wait_ge(rstd_ready.sem, rb_ + 1)
                    dve_part(dve)

                if pool_part:
                    @block.gpsimd
                    def _(pool):
                        pool.wait_ge(rstd_ready.sem, rb_ + 1)
                        pool_part(pool)
            rstd_ready.n += 1
            sq_ready.n += 0 if squared else Kt
            sum_ready.n += 1
            std_ready.n += 1

        def streams(T):
            return [(0, SEQ, 0)] + ([(SEQ, TB, 1)] if T == TB else [])

        def h1(k, T=TB):
            return H[:, k, META:META + T]

        POOL_TILES = (2, 5, 7)

        def modulate(slot, T=TB, ready=True):
            sb_, pb = scaled.n, pool_scaled.n
            own = [k for k in range(KD) if k not in POOL_TILES]

            def scale(eng, k, count):
                eng.tensor_tensor(SQ[:, k, 0:T], h1(k, T), rstd[:, 0:T], ALU.mult).then_inc(count.sem, 1)

            def wait(eng, k):
                if k in POOL_TILES:
                    eng.wait_ge(pool_scaled.sem, pb + POOL_TILES.index(k) + 1)
                else:
                    eng.wait_ge(scaled.sem, sb_ + own.index(k) + 1)

            def coefs(k, s):
                return co[:, 3 * slot, k, s:s + 1], co[:, 3 * slot + 1, k, s:s + 1]

            def dve_part(dve):
                for k in own:
                    scale(dve, k, scaled)
                for k in range(5, KD):
                    wait(dve, k)
                    for lo, hi, s in streams(T):
                        gain, shift = coefs(k, s)
                        dve.tensor_scalar(Y[:, k, lo:hi], SQ[:, k, lo:hi], gain, shift, ALU.mult, ALU.add)

            def act_part(act):
                for k in range(5):
                    wait(act, k)
                    for lo, hi, s in streams(T):
                        gain, shift = coefs(k, s)
                        act.activation(Y[:, k, lo:hi], SQ[:, k, lo:hi], ACT.Identity, bias=shift, scale=gain)

            def pool_part(pool):
                for k in POOL_TILES:
                    scale(pool, k, pool_scaled)
            if ready:
                with nc.Block() as block:
                    @block.vector
                    def _(dve):
                        dve_part(dve)

                    @block.scalar
                    def _(act):
                        act_part(act)

                    @block.gpsimd
                    def _(pool):
                        pool_part(pool)
            else:
                norm(lambda k: h1(k, T), KD, T, dve_part, act_part, pool_part=pool_part)
            scaled.n += len(own)
            pool_scaled.n += len(POOL_TILES)

        def residual(slot, T=TB, then_norm=True):
            hb, phb, qb, mb, tb_ = h_ready.n, pool_h_ready.n, sq_ready.n, sum_ready.n, std_ready.n
            own = [k for k in range(KD) if k not in POOL_TILES]

            def update(eng, ks, step, ready):
                def scale(k):
                    eng.tensor_tensor(XM[:, k, 0:T], SQ[:, k, 0:T], rstd[:, 0:T], ALU.mult).then_inc(step.sem, 1)

                scale(ks[0])
                for i, k in enumerate(ks):
                    if i + 1 < len(ks):
                        scale(ks[i + 1])
                    eng.wait_ge(step.sem, step.n + i + 1)
                    eng.tensor_tensor(h1(k, T), h1(k, T), XM[:, k, 0:T], ALU.add).then_inc(ready.sem, 1)
                step.n += len(ks)

            def dve_part(dve):
                update(dve, own, dve_step, h_ready)
                if then_norm:
                    dve.wait_ge(std_ready.sem, tb_ + 2)
                    dve.wait_ge(pool_h_ready.sem, phb + len(POOL_TILES))
                    dve.reciprocal(rstd[:, 0:T], std[:, 0:T])

            def act_part(act):
                for k in range(KD):
                    if k in POOL_TILES:
                        act.wait_ge(pool_h_ready.sem, phb + POOL_TILES.index(k) + 1)
                    else:
                        act.wait_ge(h_ready.sem, hb + own.index(k) + 1)
                    act.activation(Y[:, k, 0:T], h1(k, T), ACT.Square).then_inc(sq_ready.sem, 1)
                act.wait_ge(sum_ready.sem, mb + 2)
                act.activation(std[:, 0:T], ps[:, 6, 0:T], ACT.Sqrt, bias=epsb[:, 0:1], scale=1.0 / D).then_inc(std_ready.sem, 1)

            def pe_part(pe):
                for k in range(KD):
                    pe.wait_ge(sq_ready.sem, qb + k + 1)
                    mm = pe.matmul(ps[:, 6, 0:T], ones[:, :], Y[:, k, 0:T], start=(k == 0), stop=(k == KD - 1))
                mm.then_inc(sum_ready.sem, 1)
            norm(None, KD, T, dve_part, act_part if then_norm else None, squared=True, pe_part=pe_part if then_norm else None,
                 pool_part=lambda pool: update(pool, POOL_TILES, pool_step, pool_h_ready))
            h_ready.n += len(own)
            pool_h_ready.n += len(POOL_TILES)
            if then_norm:
                sq_ready.n += KD
                sum_ready.n += 1
                std_ready.n += 1

        def gained(gain, src, dst, Kt, T, dim=None, squared=False):
            def dve_part(dve):
                for k in range(Kt):
                    dve.scalar_tensor_tensor(dst(k), src(k), gain(k), rstd[:, 0:T], ALU.mult, ALU.mult)
            norm(src, Kt, T, dve_part, dim=dim, squared=squared)

        def normed(T):
            return Split(lambda k: Y[:, k, 0:T], lambda k: XM_R[:, k, 0:T], lambda k: EX_R[:, k * TB:k * TB + T])

        def in_place(src, src_r):
            return Split(lambda k: src[:, k, :], lambda k: EX_R[:, k * TB:k * TB + src.shape[2]], lambda k: src_r[:, k, :])

        def narrow(src, src_r):
            T = src.shape[2]
            return Split(lambda k: src[:, k, :], lambda k: EX_R[:, k * T:(k + 1) * T], lambda k: src_r[:, k, :])

        def hidden(T):
            def hi(k):
                if k < KD:
                    return XM_R[:, k, 0:T]
                return Y_R[:, k - KD, 0:T] if k < 2 * KD else EX_R[:, (k - 2 * KD) * TB:(k - 2 * KD) * TB + T]
            return Split(lambda k: GU[:, k * T:(k + 1) * T], hi, lambda k: GU_R[:, k * T:(k + 1) * T])

        def transposes(groups):
            pb, ab, db = pe_out.n, act_out.n, dve_out.n
            with nc.Block() as block:
                @block.tensor
                def _(pe):
                    for n, (srcs, rows, width, dst) in enumerate(groups):
                        if n >= 8:
                            pe.wait_ge((act_out, dve_out)[n % 2].sem, (ab, db)[n % 2] + (n - 8) // 2 + 1)
                        for j, src in enumerate(srcs):
                            kp = src.shape[0]
                            mm = pe.transpose(ps[0:rows, n % 8, j * width:j * width + kp], src, ident[0:kp, 0:kp])
                        mm.then_inc(pe_out.sem, 1)

                def copies(eng, who, count):
                    for n, (srcs, rows, width, dst) in enumerate(groups):
                        if n % 2 != who:
                            continue
                        eng.wait_ge(pe_out.sem, pb + n + 1)
                        src = ps[0:rows, n % 8, 0:len(srcs) * width].rearrange("p (j c) -> p j c", j=len(srcs))[:, :, 0:srcs[0].shape[0]]
                        if who == 0:
                            eng.activation(dst, src, ACT.Copy).then_inc(count.sem, 1)
                        else:
                            eng.tensor_copy(dst, src).then_inc(count.sem, 1)

                @block.scalar
                def _(act):
                    copies(act, 0, act_out)

                @block.vector
                def _(dve):
                    copies(dve, 1, dve_out)
            pe_out.n += len(groups)
            act_out.n += (len(groups) + 1) // 2
            dve_out.n += len(groups) // 2

        gu = GU[:, :].rearrange("p (k t) -> p k t", t=TB)

        def ffn(slot, T=TB, ready=True, then_norm=True):
            modulate(slot, T, ready)
            hold = SQ[:, 0:4, 0:TB]
            hid = GU[:, 0:KF * T].rearrange("p (k t) -> p k t", t=T)
            ab, db = act_freed.n, dve_freed.n

            def evac(eng, mine, tile):
                if not mine:
                    return
                j = tile.local
                tile.wait(eng)
                if tile.owner == "act":
                    if not tile.first:
                        eng.wait_ge(dve_freed.sem, tile.n + db - 3)
                    eng.activation(hold[:, j:j + 1, 0:T], tile.src, ACT.Silu).then_inc(act_freed.sem, 1)
                else:
                    eng.wait_ge(act_freed.sem, tile.n + ab + 1)
                    eng.tensor_tensor(hid[:, bass.ds(tile.n, 1), :], hold[:, j:j + 1, 0:T], tile.src, ALU.mult).then_inc(dve_freed.sem, 1)
            product(normed(T), T, evac, group=2)
            product(hidden(T), T, with_squares(T, slot))
            residual(slot, T, then_norm)

        sqf = SQ[:, :, :].rearrange("p a b -> p (a b)")
        xmf = XM[:, :, :].rearrange("p a b -> p (a b)")
        yf = Y[:, :, :].rearrange("p a b -> p (a b)")
        raw = xmf[:, 0:5 * P].rearrange("p (i n) -> p i n", i=5)
        tok = yf.rearrange("p (t n) -> p t n", t=4)
        meta_tok = sqf[0:META, 0:D]
        onehot, relb, brow = EX[0:32, 0:BIAS_W], EX[0:32, 512:520], EX[0:8, 1024:1024 + BIAS_W]
        rows = lambda ap, n: ap.rearrange("(r p) -> r p", p=P) if n == 1 else ap.rearrange("a (r p) -> (a r) p", p=P)
        row_list = [
            (0, 0, a["norm_g"].rearrange("l i (r p) -> (l i r) p", p=P), 96),
            (0, 96, rows(a["c"], 2), 8), (0, 104, rows(a["c_ctx"], 1), 8),
            (1, 0, rows(a["b_mod"][0:1], 2), 72), (1, 72, rows(a["g_q_mla"], 2), 3), (1, 75, rows(a["g_kv_mla"], 2), 2),
            (1, 77, rows(a["g_subln"], 2), 1), (1, 78, rows(a["conv_w"][0], 2), 12),
            (2, 0, rows(a["b_mod"][1:2], 2), 72), (2, 72, rows(a["norm_mix_2"], 2), 16), (2, 88, rows(a["norm_ffn_2"], 2), 16),
            (2, 104, rows(a["norm_final_2"], 1), 8), (2, 112, rows(a["even_gn_gain_2"], 2), 8),
            (3, 0, rows(a["ffn_conv_w_2"][0], 2), 66), (3, 66, rows(a["ffn_conv_b_2"][0:1], 2), 22),
            (4, 0, rows(a["ffn_conv_w_2"][1], 2), 66), (4, 66, rows(a["ffn_conv_b_2"][1:2], 2), 22)]
        row_counts = [112, 90, 120, 88, 88]
        first_loads = [
            (ident[:, :], a["k_ident"]), (ones[:, :], a["k_ones"]), (swap[:, :, :], a["k_swap"]), (tri[:, :, :], a["k_tri"]),
            (kb[:, :], a["k_first"]), (onehot, a["k_bucket"]), (relb, a["rel_bias_2"]),
            (tok[:, 0:2, :], a["x"][0].rearrange("(t p) n -> p t n", p=P)),
            (tok[:, 2:4, :], a["ctx"][0].rearrange("(t p) n -> p t n", p=P)), (meta_tok, a["meta_tokens_2"]),
            (lam4[:, 0, :], a["lam_q1"]), (lam4[:, 1, :], a["lam_k1"]), (lam4[:, 2, :], a["lam_q2"]), (lam4[:, 3, :], a["lam_k2"]),
            *[(raw[r:r + n, i, :], src) for i, r, src, n in row_list]]
        with nc.Block() as block:
            @block.sync
            def _(sp):
                for dst, src in first_loads:
                    sp.dma_start(dst, src).then_inc(loaded.sem, 16)
                for n in range(SLOTS):
                    q = max(i for i in range(len(plan)) if first_unit[i] <= n)
                    load_unit(sp, plan[q], n - first_unit[q], n)
                sp.wait_ge(loaded.sem, 16 * len(first_loads))

            @block.gpsimd
            def _(pool):
                pool.memset(epsb[:, :], EPS)
        loaded.n += 16 * len(first_loads)

        transposes([([raw[0:n, i, :]], P, P, prm[:, i:i + 1, 0:n]) for i, n in enumerate(row_counts)]
                   + [([tok[:, t, (4 * h + j) * P:(4 * h + j + 1) * P] for j in range(4)], P, P,
                       H[:, 4 * h:4 * h + 4, META + t * P:META + (t + 1) * P]) for t in range(4) for h in range(2)]
                   + [([meta_tok[:, (4 * h + j) * P:(4 * h + j + 1) * P] for j in range(4)], P, P,
                       H[:, 4 * h:4 * h + 4, 0:META]) for h in range(2)])

        ab, db, pb = act_out.n, dve_out.n, pe_out.n
        with nc.Block() as block:
            @block.tensor
            def _(pe):
                pe.matmul(ps[0:8, 0, 0:BIAS_W], relb, onehot, start=True, stop=True).then_inc(pe_out.sem, 1)
                pe.wait_ge(dve_out.sem, db + 2)
                pe.matmul(ps[:, 1, 0:2], ones[0:1, :], lamv[:, 4:6], start=True, stop=True).then_inc(pe_out.sem, 1)

            @block.vector
            def _(dve):
                dve.tensor_tensor(lam4[:, 0, :], lam4[:, 0, :], lam4[:, 1, :], ALU.mult)
                chained(dve, dve.tensor_tensor(lam4[:, 2, :], lam4[:, 2, :], lam4[:, 3, :], ALU.mult), dve_step)
                dve.tensor_reduce(lamv[:, 0:1], lam4[:, 0, :], AX_X, ALU.add)
                dve.tensor_reduce(lamv[:, 1:2], lam4[:, 2, :], AX_X, ALU.add).then_inc(dve_out.sem, 1)
                dve.wait_ge(act_out.sem, ab + 1)
                chained(dve, dve.tensor_tensor(lamv[:, 4:5], lamv[:, 3:4], lamv[:, 2:3], ALU.subtract), dve_step)
                chained(dve, dve.tensor_scalar(lamv[:, 4:5], lamv[:, 4:5], -LAM_INIT, None, ALU.add), dve_step)
                dve.tensor_copy(lamv[:, 5:6], lamv[:, 4:5]).then_inc(dve_out.sem, 1)
                dve.wait_ge(pe_out.sem, pb + 2)
                dve.tensor_copy(nlam[:, :], ps[:, 1, 0:2])
                dve.tensor_copy(brow, ps[0:8, 0, 0:BIAS_W]).then_inc(dve_out.sem, 1)
                dve.tensor_scalar(gsub[:, :], prm[:, 1, 77:78], 1.0 - LAM_INIT, None, ALU.mult)

            @block.scalar
            def _(act):
                act.wait_ge(dve_out.sem, db + 1)
                act.activation(lamv[:, 2:4], lamv[:, 0:2], ACT.Exp).then_inc(act_out.sem, 1)
                for s in range(2):
                    act.activation(cs[:, :, s], prm[:, 0, 96 + 8 * s:104 + 8 * s], ACT.Silu)

            @block.sync
            def _(sp):
                sp.wait_ge(dve_out.sem, db + 3)
                sp.dma_start(bias_rows, brow).then_inc(stored.sem, 16)
                sp.wait_ge(stored.sem, 16)
        act_out.n += 1
        dve_out.n += 3
        pe_out.n += 2
        stored.n += 16

        adaln(0, 0)
        coefficients(0, [0])
        ffn(0, ready=False)
        coefficients(0, [1, 2])
        modulate(1)
        product(normed(TB), TB, copy_out(into(gu)))

        z = sqf[:, 0:4 * 2 * 258].rearrange("p (j s t) -> p j s t", j=4, s=2)
        cv = EX[:, 0:4 * TB].rearrange("p (j s t) -> p j s t", j=4, s=2)
        spectrum = yf.rearrange("p (i c n) -> p i c n", c=2, n=P)
        pb, ab = pe_out.n, act_out.n
        with nc.Block() as block:
            @block.vector
            def _(dve):
                dve.memset(z[:, :, :, 0:1], 0.0)
                dve.memset(z[:, :, :, 257:258], 0.0)
                st = lambda ap: ap.rearrange("p (s t) -> p s t", s=2)
                for j in range(4):
                    ins = dve.tensor_tensor(z[:, j, :, 1:257], st(gu[:, 4 + j, :]), st(gu[:, 8 + j, :]), ALU.mult)
                chained(dve, ins, dve_step)
                w = lambda k, j: prm[:, 1, 78 + 4 * k + j:79 + 4 * k + j]
                for j in range(4):
                    ins = dve.tensor_scalar(cv[:, j], z[:, j, :, 0:256], w(0, j), None, ALU.mult)
                chained(dve, ins, dve_step)
                for k in (1, 2):
                    for j in range(4):
                        ins = dve.scalar_tensor_tensor(cv[:, j], z[:, j, :, k:k + 256], w(k, j), cv[:, j], ALU.mult, ALU.add)
                    chained(dve, ins, dve_step)
                for j in range(4):
                    dve.tensor_tensor(st(XM[:, j, :]), cv[:, j], st(gu[:, j, :]), ALU.mult)

            @block.tensor
            def _(pe):
                n = 0
                for s in range(2):
                    for g in range(4):
                        for t in range(2):
                            if n >= 6:
                                pe.wait_ge(act_out.sem, ab + n - 5)
                            c0 = s * SEQ + t * P
                            pe.matmul(ps[:, n % 6, 0:256], gu[:, 12 + g, c0:c0 + P], dft1, start=True, stop=True).then_inc(pe_out.sem, 1)
                            n += 1
                for m in range(8):
                    pe.wait_ge(act_out.sem, ab + 16 + max(0, m - 1))
                    for t in range(2):
                        for c in range(2):
                            mm = pe.matmul(ps[:, 6 + m % 2, 0:256], spectrum[:, 2 * m + t, c, :], dft2[:, t, c, :],
                                           start=(t == 0 and c == 0), stop=(t == 1 and c == 1))
                    mm.then_inc(pe_out.sem, 1)

            @block.scalar
            def _(act):
                for n in range(16):
                    act.wait_ge(pe_out.sem, pb + n + 1)
                    act.activation(spectrum[:, n, :, :].rearrange("p c n -> p (c n)"), ps[:, n % 6, 0:256], ACT.Copy).then_inc(act_out.sem, 1)
                for m in range(8):
                    s, g = m // 4, m % 4
                    act.wait_ge(pe_out.sem, pb + 16 + m + 1)
                    act.activation(XM[:, 4 + g, s * SEQ:(s + 1) * SEQ], ps[:, 6 + m % 2, 0:256], ACT.Copy).then_inc(act_out.sem, 1)
        pe_out.n += 24
        act_out.n += 24
        product(in_place(XM, XM_R), TB, with_squares(TB, 1))
        residual(1)
        ffn(2)

        adaln(1, MOD_PAIRS - LEFT)
        coefficients(1, [0, 1, 2])
        ffn(0)
        modulate(1)
        view = lambda buf, lo, k, t: buf[:, lo:lo + k * t].rearrange("p (k t) -> p k t", k=k)
        qda, kda = view(GU, 0, 8, SEQ), view(GU, 2048, 8, TB)
        vda, cq = view(GU, 6144, 4, D), view(GU, 10240, 3, SEQ)
        qm, km = view(EX, 0, 8, SEQ), view(EX, 2048, 8, TB)
        ckv, krope = SQ[:, 4:6, 0:TB], SQ[:, 6:7, 0:TB]
        vm = xmf[:, 2048:4096].rearrange("p (t n) -> p t n", t=4)
        heads_out = view(yf, 0, 12, SEQ)

        product(normed(TB), SEQ,
                copy_out(lambda tile: qda[:, tile.t:tile.t + 1, :] if tile.t < 8 else cq[:, tile.t - 8:tile.t - 7, :]))

        def kv_dest(tile):
            t = tile.t
            if t < 8:
                return kda[:, t:t + 1, :]
            if t < 16:
                return Y[:, t - 8:t - 7, :]
            if t < 18:
                return ckv[:, t - 16:t - 15, :]
            return krope[MLA_NOPE:MLA_DQK, :, :]
        product(normed(TB), TB, copy_out(kv_dest), fresh=False)
        transposes([([Y[:, 4 * h + j, t * P:(t + 1) * P] for j in range(4)], P, P,
                     vda[:, t, 4 * h * P:4 * (h + 1) * P].rearrange("p (j c) -> p j c", j=4)) for t in range(4) for h in range(2)])

        def rope(tiles, table, which, T, plain):
            pb, gb, db = pe_out.n, pool_step.n, dve_out.n
            second = (std, rstd)
            with nc.Block() as block:
                @block.gpsimd
                def _(pool):
                    for n, x in enumerate(tiles):
                        lo = x.start_partition()
                        hi = lo + x.shape[0]
                        if n and lo != tiles[n - 1].start_partition():
                            pool.wait_ge(pool_step.sem, gb + n)
                        pool.tensor_tensor(plain[lo:hi, n, :], x, table[lo:hi, 0, :], ALU.mult).then_inc(pool_step.sem, 1)

                @block.tensor
                def _(pe):
                    for n, x in enumerate(tiles):
                        lo = x.start_partition()
                        hi = lo + x.shape[0]
                        if n >= 8:
                            pe.wait_ge(dve_out.sem, db + n - 7)
                        pe.matmul(ps[lo:hi, n % 8, 0:T], swap[lo:hi, which, lo:hi], x, start=True, stop=True).then_inc(pe_out.sem, 1)

                @block.vector
                def _(dve):
                    for n, x in enumerate(tiles):
                        lo = x.start_partition()
                        hi = lo + x.shape[0]
                        dve.wait_ge(pe_out.sem, pb + n + 1)
                        ins = dve.tensor_tensor(second[n % 2][lo:hi, 0:T], ps[lo:hi, n % 8, 0:T], table[lo:hi, 1, :], ALU.mult)
                        ins.then_inc(dve_out.sem, 1)
                        dve.wait_ge(dve_out.sem, db + n + 1)
                        dve.wait_ge(pool_step.sem, gb + n + 1)
                        dve.tensor_tensor(x, plain[lo:hi, n, :], second[n % 2][lo:hi, 0:T], ALU.add)
            pe_out.n += len(tiles)
            dve_out.n += len(tiles)
            pool_step.n += len(tiles)

        rope([qda[:, i, :] for i in range(8)] + [kda[:, i, 0:SEQ] for i in range(8)], rope_da, 0, SEQ, view(xmf, 0, 16, SEQ))
        gained(lambda k: prm[:, 1, 72 + k:73 + k], lambda k: cq[:, k, :], lambda k: cq[:, k, :], 3, SEQ)
        gained(lambda k: prm[:, 1, 75 + k:76 + k], lambda k: ckv[:, k, :], lambda k: ckv[:, k, :], 2, TB)
        cq_r, ckv_r = view(GU_R, 10240, 3, SEQ), SQ_R[:, 4:6, 0:TB]
        product(Split(lambda k: cq[:, k, :], lambda k: Y_R[:, k, 0:SEQ], lambda k: cq_r[:, k, :]), SEQ, copy_out(lambda tile: qm[0:MLA_DQK, tile.t:tile.t + 1, :]))
        rope([qm[0:MLA_DQK, i, :] for i in range(8)] + [krope[MLA_NOPE:MLA_DQK, 0, 0:SEQ]], rope_mla, 1, SEQ, view(xmf, 0, 9, SEQ))
        shared = krope[MLA_NOPE:MLA_DQK, :, :].broadcast_to((MLA_ROPE, 4, TB))
        with nc.Block() as block:
            @block.scalar
            def _(act):
                act.activation(km[MLA_NOPE:MLA_DQK, 0:4, :], shared, ACT.Copy)

            @block.vector
            def _(dve):
                dve.tensor_copy(km[MLA_NOPE:MLA_DQK, 4:8, :], shared)
        latent = Split(lambda k: ckv[:, k, :], lambda k: Y_R[:, k, :], lambda k: ckv_r[:, k, :])
        product(latent, TB, copy_out(lambda tile: km[0:MLA_NOPE, tile.t:tile.t + 1, :]))
        product(latent, TB, copy_out(lambda tile: XM[:, tile.t:tile.t + 1, :]), fresh=False)
        transposes([([XM[:, j, t * P:(t + 1) * P] for j in range(4)], P, P,
                     vm[:, t, :].rearrange("p (j c) -> p j c", j=4)) for t in range(4)])

        NK = TB // P
        items = []
        for h in range(DA_HEADS):
            for qt in range(SEQ // P):
                q = slice(qt * P, (qt + 1) * P)
                items.append(dict(
                    scores=[(qda[64 * m:64 * m + 64, h, q], kda[64 * m:64 * m + 64, h, :]) for m in range(2)], scale=DA_SCALE,
                    v=[vda[:, kt, h * P:(h + 1) * P] for kt in range(NK)], rows=(0, P), out=heads_out[:, h, q]))
        for h in range(MLA_HEADS):
            for qt in range(SEQ // P):
                q, lo = slice(qt * P, (qt + 1) * P), 64 * (h % 2)
                items.append(dict(
                    scores=[(qm[0:MLA_DQK, h, q], km[0:MLA_DQK, h, :])], scale=MLA_SCALE,
                    v=[vm[:, kt, h * 64:h * 64 + 64] for kt in range(NK)], rows=(lo, lo + 64), out=heads_out[lo:lo + 64, 8 + h // 2, q]))
        N = len(items)
        e = sqf[:, 0:2048].rearrange("p (b m k) -> p b m k", b=2, m=2)
        wT = sqf[:, 2048:3072].rearrange("p (b k q) -> p b k q", b=2, k=NK)
        scored, turned, summed = pe_out, pe_out2, pe_out3
        maxed, weighted, kept = dve_out, dve_out2, dve_out3
        raised, copied = act_out, act_out2
        sc0, tu0, su0, ma0, we0, ke0, ra0, co0 = (c.n for c in (scored, turned, summed, maxed, weighted, kept, raised, copied))
        with nc.Block() as block:
            @block.tensor
            def _(pe):
                def scores(n):
                    b = n % 3
                    if n >= 3:
                        pe.wait_ge(raised.sem, ra0 + n - 2)
                    for m, (q, k) in enumerate(items[n]["scores"]):
                        mm = pe.matmul(ps[:, 2 * b + m, :], q, k, start=True, stop=True)
                    mm.then_inc(scored.sem, 1)

                def values(n):
                    pe.wait_ge(copied.sem, co0 + n + 1)
                    if n >= 1:
                        pe.wait_ge(kept.sem, ke0 + n)
                    lo, hi = items[n]["rows"]
                    for kt in range(NK):
                        mm = pe.matmul(ps[lo:hi, 7, 0:P], items[n]["v"][kt], wT[:, n % 2, kt, :], start=(kt == 0), stop=(kt == NK - 1))
                    mm.then_inc(summed.sem, 1)

                scores(0)
                scores(1)
                for n in range(N):
                    if n + 2 < N:
                        scores(n + 2)
                    pe.wait_ge(weighted.sem, we0 + n + 1)
                    if n >= 1:
                        pe.wait_ge(copied.sem, co0 + n)
                    for kt in range(NK):
                        mm = pe.transpose(ps[:, 6, kt * P:(kt + 1) * P], e[:, n % 2, 0, kt * P:(kt + 1) * P], ident[:, :])
                    mm.then_inc(turned.sem, 1)
                    if n >= 1:
                        values(n - 1)
                values(N - 1)

            @block.vector
            def _(dve):
                def maxima(n):
                    b, nm = n % 2, len(items[n]["scores"])
                    s0 = 8 * b
                    dve.wait_ge(scored.sem, sc0 + n + 1)
                    chained(dve, dve.tensor_reduce(small[:, s0:s0 + nm], ps[:, 2 * (n % 3):2 * (n % 3) + nm, :], AX_X, ALU.max), dve_step)
                    dve.tensor_scalar(small[:, s0 + 2:s0 + 2 + nm], small[:, s0:s0 + nm], -items[n]["scale"], None, ALU.mult).then_inc(maxed.sem, 1)

                def weights(n):
                    b, nm = n % 2, len(items[n]["scores"])
                    s0 = 8 * b
                    dve.wait_ge(raised.sem, ra0 + n + 1)
                    chained(dve, dve.reciprocal(small[:, s0 + 6:s0 + 6 + nm], small[:, s0 + 4:s0 + 4 + nm]), dve_step)
                    if nm == 1:
                        dve.tensor_scalar(e[:, b, 0, :], e[:, b, 0, :], small[:, s0 + 6:s0 + 7], None, ALU.mult).then_inc(weighted.sem, 1)
                        return
                    dve.tensor_scalar(small[:, s0 + 7:s0 + 8], small[:, s0 + 7:s0 + 8], nlam[:, 0:1], None, ALU.mult)
                    chained(dve, dve.tensor_scalar(e[:, b, 0, :], e[:, b, 0, :], small[:, s0 + 6:s0 + 7], None, ALU.mult), dve_step)
                    dve.scalar_tensor_tensor(e[:, b, 0, :], e[:, b, 1, :], small[:, s0 + 7:s0 + 8], e[:, b, 0, :],
                                             ALU.mult, ALU.add).then_inc(weighted.sem, 1)

                def keep(n):
                    dve.wait_ge(summed.sem, su0 + n + 1)
                    lo, hi = items[n]["rows"]
                    dve.tensor_copy(items[n]["out"], ps[lo:hi, 7, 0:P]).then_inc(kept.sem, 1)

                maxima(0)
                for n in range(N):
                    if n + 1 < N:
                        maxima(n + 1)
                    weights(n)
                    if n >= 2:
                        keep(n - 2)
                keep(N - 2)
                keep(N - 1)

            @block.scalar
            def _(act):
                def exps(n):
                    b, nm = n % 2, len(items[n]["scores"])
                    s0 = 8 * b
                    act.wait_ge(maxed.sem, ma0 + n + 1)
                    if n >= 2:
                        act.wait_ge(turned.sem, tu0 + n - 1)
                    for m in range(nm):
                        ins = act.activation(e[:, b, m, :], ps[:, 2 * (n % 3) + m, :], ACT.Exp, bias=small[:, s0 + 2 + m:s0 + 3 + m],
                                             scale=items[n]["scale"], accum_out=small[:, s0 + 4 + m:s0 + 5 + m])
                    ins.then_inc(raised.sem, 1)

                exps(0)
                for n in range(N):
                    if n + 1 < N:
                        exps(n + 1)
                    b = n % 2
                    act.wait_ge(turned.sem, tu0 + n + 1)
                    if n >= 2:
                        act.wait_ge(summed.sem, su0 + n - 1)
                    act.activation(wT[:, b, :, :].rearrange("p k q -> p (k q)"), ps[:, 6, :], ACT.Copy).then_inc(copied.sem, 1)
        for c in (scored, turned, summed, maxed, weighted, kept, raised, copied):
            c.n += N

        da_out = yf[:, 0:2048]
        sb0, mb0, tb0 = sq_ready.n, sum_ready.n, std_ready.n
        with nc.Block() as block:
            @block.scalar
            def _(act):
                act.activation(sqf[:, 0:2048], da_out, ACT.Square).then_inc(sq_ready.sem, 1)
                act.wait_ge(sum_ready.sem, mb0 + 1)
                act.activation(sqf[:, 2048:4096].rearrange("p (b n) -> p b n", b=4), ps[:, 0:4, :], ACT.Sqrt,
                               bias=epsb[:, 0:1], scale=1.0 / DA_DV).then_inc(std_ready.sem, 1)

            @block.tensor
            def _(pe):
                pe.wait_ge(sq_ready.sem, sb0 + 1)
                for b in range(4):
                    mm = pe.matmul(ps[:, b, :], ones[:, :], sqf[:, b * 512:(b + 1) * 512], start=True, stop=True)
                mm.then_inc(sum_ready.sem, 1)

            @block.vector
            def _(dve):
                dve.wait_ge(std_ready.sem, tb0 + 1)
                chained(dve, dve.reciprocal(sqf[:, 0:2048], sqf[:, 2048:4096]), dve_step)
                dve.scalar_tensor_tensor(da_out, da_out, gsub[:, 0:1], sqf[:, 0:2048], ALU.mult, ALU.mult)
        for c in (sq_ready, sum_ready, std_ready):
            c.n += 1
        product(narrow(heads_out, view(Y_R[:, :, :].rearrange("p a b -> p (a b)"), 0, 12, SEQ)), SEQ, with_squares(SEQ, 1))
        residual(1, SEQ)
        ffn(2, SEQ, then_norm=False)

        flat2 = lambda k: H[:, k, 0:T2]
        pj = view(GU, 0, 40, T2)
        cat = view(xmf, 0, 12, T2)
        cat_r = view(XM_R[:, :, :].rearrange("p a b -> p (a b)"), 0, 12, T2)
        exf = EX[:, :]
        va = view(exf, 0, 3, 512)
        vr = view(exf, 1536, 3, D)
        iw = view(exf, 4608, 3, 8)
        ikd, iwf = exf[:, 4640:4640 + T2], exf[0:8, 4912:4912 + T2]
        chosen = view(exf, 5184, 3, T2)
        m8 = small[:, 0:8]
        token_tiles = [(0, P), (P, P), (2 * P, T2 - 2 * P)]

        def gain2(row):
            return lambda k: prm[:, 2, row + k:row + k + 1]

        def conv_ffn(layer):
            gained(gain2(88 + 8 * layer), flat2, lambda k: Y[:, k, 0:T2], KD, T2, squared=True)
            gp = sqf[:, 0:4 * (T2 + 2)].rearrange("p (j t) -> p j t", j=4)
            cv2 = sqf[:, 4 * (T2 + 2):4 * (2 * T2 + 2)].rearrange("p (j t) -> p j t", j=4)
            gu2 = view(GU, 0, KF, T2)
            with nc.Block() as block:
                @block.vector
                def _(dve):
                    dve.memset(gp[:, :, 0:2], 0.0)
            ab, db, sb_, cb, vb = act_freed.n, dve_freed.n, silu_done.n, conv_done.n, conv_step.n

            def evac(eng, mine, tile):
                j, n = tile.local, tile.n
                gate, is_act = tile.owner == "act", (tile.owner == "act") == mine
                if is_act and gate:
                    tile.wait(eng)
                    if not tile.first:
                        eng.wait_ge(conv_done.sem, n + cb - 3)
                    eng.activation(gp[:, j:j + 1, 2:2 + T2], tile.src, ACT.Copy).then_inc(act_freed.sem, 1)
                elif is_act:
                    eng.wait_ge(conv_done.sem, n + cb + 1)
                    eng.activation(cv2[:, j, :], cv2[:, j, :], ACT.Silu,
                                   bias=prm[:, 3 + layer, bass.ds(n + 66, 1)]).then_inc(silu_done.sem, 1)
                elif gate:
                    eng.wait_ge(act_freed.sem, n + ab + 1)
                    w = lambda k: prm[:, 3 + layer, bass.ds(n + KF * k, 1)]
                    eng.tensor_scalar(cv2[:, j, :], gp[:, j, 0:T2], w(0), None, ALU.mult).then_inc(conv_step.sem, 1)
                    eng.wait_ge(conv_step.sem, 2 * n + vb + 1)
                    eng.scalar_tensor_tensor(cv2[:, j, :], gp[:, j, 1:T2 + 1], w(1), cv2[:, j, :], ALU.mult, ALU.add).then_inc(conv_step.sem, 1)
                    eng.wait_ge(conv_step.sem, 2 * n + vb + 2)
                    eng.scalar_tensor_tensor(cv2[:, j, :], gp[:, j, 2:T2 + 2], w(2), cv2[:, j, :], ALU.mult, ALU.add).then_inc(conv_done.sem, 1)
                else:
                    tile.wait(eng)
                    eng.wait_ge(silu_done.sem, n + sb_ + 1)
                    eng.tensor_tensor(gu2[:, bass.ds(n, 1), :], cv2[:, j:j + 1, :], tile.src, ALU.mult).then_inc(dve_freed.sem, 1)
            product(normed(T2), T2, evac, group=2)
            silu_done.n += KF
            conv_done.n += KF
            conv_step.n += 2 * KF
            product(hidden(T2), T2, with_squares(T2))

        with nc.Block() as block:
            @block.sync
            def _(sp):
                sp.dma_start(kb[:, :], a["k_second"]).then_inc(loaded.sem, 16)
                sp.dma_start(tri[:, :, :], a["k_sparse"]).then_inc(loaded.sem, 16)
                sp.wait_ge(loaded.sem, loaded.n + 32)
        loaded.n += 32
        gained(gain2(72), flat2, lambda k: Y[:, k, 0:T2], KD, T2)
        product(normed(T2), T2, copy_out(into(pj, 0, T2)))
        product(normed(T2), T2,
                copy_out(lambda tile: ikd[0:64, :].rearrange("p (a t) -> p a t", a=1) if tile.t == 0
                         else iwf.rearrange("p (a t) -> p a t", a=1)), fresh=False)
        product(normed(T2), T2, copy_out(into(pj, 16, T2)), fresh=False)
        transposes([([pj[:, first + 4 * h + j, t0:t0 + tn] for j in range(4)], tn, P,
                     dst[0:tn, t, 4 * h * P:4 * (h + 1) * P].rearrange("p (j c) -> p j c", j=4))
                    for t, (t0, tn) in enumerate(token_tiles) for first, dst, n in ((8, va, 1), (24, vr, 2)) for h in range(n)]
                   + [([iwf[:, t0:t0 + tn]], tn, P, iw[0:tn, t:t + 1, :]) for t, (t0, tn) in enumerate(token_tiles)])
        with nc.Block() as block:
            @block.vector
            def _(dve):
                dve.tensor_copy(ikd[64:P, :], ikd[0:64, :])
                for t, (t0, tn) in enumerate(token_tiles):
                    dve.tensor_scalar(iw[0:tn, t, :], iw[0:tn, t, :], 8 ** -0.5, None, ALU.mult)
        rope([pj[:, 16 + i, :] for i in range(8)], rope_ret, 2, T2, view(yf, 0, 8, T2))

        relu_s = view(sqf, 0, 8, T2)
        bias = view(yf, 0, 8, T2)
        pT = yf[:, 2176:2176 + 1536].rearrange("p (k h q) -> p k h q", k=3, h=4)
        pT2 = sqf[:, 2176:2176 + 1536].rearrange("p (k h q) -> p k h q", k=3, h=4)
        prob = view(sqf, 0, 8, T2)
        score, work = std[:, 0:T2], rstd[:, 0:T2]
        causal = tri[:, 1, :]
        for qt, (q0, nq) in enumerate(token_tiles):
            nk = min(T2, q0 + P)
            kts = token_tiles[:qt + 1]
            pb, ab, lb = pe_out.n, act_out.n, loaded.n
            with nc.Block() as block:
                @block.sync
                def _(sp):
                    src = bass.AP(bias_rows.tensor, T2 - q0 - nq, [[1, nq], [BIAS_W, DSA_HEADS], [1, nk]])
                    sp.dma_start(bias[0:nq, :, 0:nk], src).then_inc(loaded.sem, 16)
                    sp.wait_ge(loaded.sem, lb + 16)

                @block.tensor
                def _(pe):
                    for h in range(8):
                        lo = 64 * (h % 2)
                        pe.matmul(ps[0:nq, h, 0:nk], pj[lo:lo + 64, 12 + h // 2, q0:q0 + nq], ikd[lo:lo + 64, 0:nk],
                                  start=True, stop=True).then_inc(pe_out.sem, 1)
                    pe.wait_ge(loaded.sem, lb + 16)
                    for h in range(8):
                        lo = 64 * (h % 2)
                        pe.wait_ge(act_out.sem, ab + h + 1)
                        pe.matmul(ps[0:nq, h, 0:nk], pj[lo:lo + 64, h // 2, q0:q0 + nq], pj[lo:lo + 64, 4 + h // 2, 0:nk],
                                  start=True, stop=False)
                        pe.matmul(ps[0:nq, h, 0:nk], tri[0:nq, 0 if nq == P else 2, 0:nq], bias[0:nq, h, 0:nk],
                                  start=False, stop=True)

                @block.scalar
                def _(act):
                    for h in range(8):
                        act.wait_ge(pe_out.sem, pb + h + 1)
                        act.activation(relu_s[0:nq, h, 0:nk], ps[0:nq, h, 0:nk], ACT.Relu, scale=DSA_D ** -0.5).then_inc(act_out.sem, 1)

                @block.vector
                def _(dve):
                    for h in range(8):
                        dve.wait_ge(act_out.sem, ab + h + 1)
                        w = iw[0:nq, qt, h:h + 1]
                        if h == 0:
                            ins = dve.tensor_scalar(score[0:nq, 0:nk], relu_s[0:nq, 0, 0:nk], w, None, ALU.mult)
                        else:
                            ins = dve.scalar_tensor_tensor(score[0:nq, 0:nk], relu_s[0:nq, h, 0:nk], w, score[0:nq, 0:nk], ALU.mult, ALU.add)
                        chained(dve, ins, dve_step)
                    chained(dve, dve.tensor_tensor(score[0:nq, q0:nk], score[0:nq, q0:nk], causal[0:nq, 0:nk - q0], ALU.add), dve_step)
                    wk = work[0:nq, META:nk]
                    src = score[0:nq, META:nk]
                    for _ in range((KEEP - META) // 8):
                        chained(dve, dve.max(m8[0:nq, :], src), dve_step)
                        chained(dve, dve.match_replace(wk, m8[0:nq, :], src, TAKEN), dve_step)
                        src = wk
                    ch = chosen[0:nq, qt, 0:nk]
                    dve.memset(ch[:, 0:META], 0.0)
                    chained(dve, dve.tensor_scalar(ch[:, META:nk], wk, TAKEN * 0.9, NEG, ALU.is_gt, ALU.mult), dve_step)
                    dve.tensor_tensor(ch[:, q0:nk], ch[:, q0:nk], causal[0:nq, 0:nk - q0], ALU.add)
            pe_out.n += 8
            act_out.n += 8
            loaded.n += 16

            pb, ab, db, tb = pe_out.n, act_out.n, dve_out.n, pe_out2.n
            ob, cb = pe_out3.n, act_out2.n
            with nc.Block() as block:
                @block.tensor
                def _(pe):
                    for gr in range(2):
                        pe.wait_ge(dve_out.sem, db + gr + 1)
                        for kt, (k0, kn) in enumerate(kts):
                            for j in range(4):
                                mm = pe.transpose(ps[0:kn, 4 * gr + kt, j * P:j * P + nq], prob[0:nq, 4 * gr + j, k0:k0 + kn],
                                                  ident[0:nq, 0:nq])
                            mm.then_inc(pe_out2.sem, 1)
                    for gr in range(2):
                        pe.wait_ge(act_out2.sem, cb + (gr + 1) * len(kts))
                        for j in range(4):
                            h, lo = 4 * gr + j, 64 * (j % 2)
                            for kt, (k0, kn) in enumerate(kts):
                                mm = pe.matmul(ps[lo:lo + 64, 4 * gr + 3, (j // 2) * P:(j // 2) * P + nq], va[0:kn, kt, h * 64:h * 64 + 64],
                                               (pT, pT2)[gr][0:kn, kt, j, 0:nq], start=(kt == 0), stop=(kt == len(kts) - 1))
                        mm.then_inc(pe_out3.sem, 1)

                @block.vector
                def _(dve):
                    for gr in range(2):
                        hs = slice(4 * gr, 4 * gr + 4)
                        pr = prob[0:nq, hs, 0:nk]
                        row = lambda c: small[0:nq, 16 + 16 * gr + 4 * c:20 + 16 * gr + 4 * c]
                        mask = chosen[0:nq, qt, 0:nk].unsqueeze(1).broadcast_to((nq, 4, nk))
                        chained(dve, dve.scalar_tensor_tensor(pr, ps[0:nq, hs, 0:nk], DSA_D ** -0.5, mask, ALU.mult, ALU.add), dve_step)
                        chained(dve, dve.tensor_reduce(row(0), pr, AX_X, ALU.max), dve_step)
                        dve.tensor_scalar(row(3), row(0), -1.0, None, ALU.mult).then_inc(dve_out2.sem, 1)
                    for gr in range(2):
                        hs = slice(4 * gr, 4 * gr + 4)
                        pr = prob[0:nq, hs, 0:nk]
                        row = lambda c: small[0:nq, 16 + 16 * gr + 4 * c:20 + 16 * gr + 4 * c]
                        wide = lambda x: x.unsqueeze(2).broadcast_to((nq, 4, nk))
                        dve.wait_ge(act_out.sem, ab + gr + 1)
                        chained(dve, dve.reciprocal(row(2), row(1)), dve_step)
                        dve.tensor_tensor(pr, pr, wide(row(2)), ALU.mult).then_inc(dve_out.sem, 1)
                    for gr in range(2):
                        dve.wait_ge(pe_out3.sem, ob + gr + 1)
                        dve.tensor_copy(cat[:, 2 * gr:2 * gr + 2, q0:q0 + nq],
                                        ps[:, 4 * gr + 3, 0:2 * P].rearrange("p (j q) -> p j q", j=2)[:, :, 0:nq])

                @block.scalar
                def _(act):
                    for gr in range(2):
                        act.wait_ge(dve_out2.sem, dve_out2.n + gr + 1)
                        for j in range(4):
                            pr, c = prob[0:nq, 4 * gr + j, 0:nk], 16 + 16 * gr + j
                            ins = act.activation(pr, pr, ACT.Exp, bias=small[0:nq, c + 12:c + 13], accum_out=small[0:nq, c + 4:c + 5])
                        ins.then_inc(act_out.sem, 1)
                    for gr in range(2):
                        for kt, (k0, kn) in enumerate(kts):
                            act.wait_ge(pe_out2.sem, tb + gr * len(kts) + kt + 1)
                            src = ps[0:kn, 4 * gr + kt, :].rearrange("p (h q) -> p h q", h=4)[:, :, 0:nq]
                            act.activation((pT, pT2)[gr][0:kn, kt, :, 0:nq], src, ACT.Copy).then_inc(act_out2.sem, 1)
            pe_out2.n += 2 * len(kts)
            pe_out3.n += 2
            act_out.n += 2
            act_out2.n += 2 * len(kts)
            dve_out.n += 2
            dve_out2.n += 2

        inner = yf[:, 0:6 * T2].rearrange("p (b t q) -> p b t q", b=2, t=3)
        pb, db, ob, ab = pe_out.n, dve_out.n, pe_out3.n, act_out.n
        with nc.Block() as block:
            @block.tensor
            def _(pe):
                def scores(h):
                    b = h % 2
                    if h >= 2:
                        pe.wait_ge(dve_out.sem, db + h - 1)
                    for t, (k0, kn) in enumerate(token_tiles):
                        mm = pe.matmul(ps[0:kn, 3 * b + t, 0:T2 - k0], pj[:, 20 + h, k0:k0 + kn], pj[:, 16 + h, k0:T2], start=True, stop=True)
                    mm.then_inc(pe_out.sem, 1)

                scores(0)
                for h in range(RET_HEADS):
                    if h + 1 < RET_HEADS:
                        scores(h + 1)
                    pe.wait_ge(dve_out.sem, db + h + 1)
                    for f in range(2):
                        n = 2 * h + f
                        if n >= 2:
                            pe.wait_ge(act_out.sem, ab + n - 1)
                        for t, (k0, kn) in enumerate(token_tiles):
                            c0 = h * RET_DV + f * P
                            mm = pe.matmul(ps[:, 6 + f, k0:T2], vr[0:kn, t, c0:c0 + P], inner[0:kn, h % 2, t, 0:T2 - k0],
                                           start=(t == 0), stop=(t == 2), skip_group_check=True)
                        mm.then_inc(pe_out3.sem, 1)

            @block.vector
            def _(dve):
                for h in range(RET_HEADS):
                    dve.wait_ge(pe_out.sem, pb + h + 1)
                    if h >= 2:
                        dve.wait_ge(pe_out3.sem, ob + 2 * h - 2)
                    for t, (k0, kn) in enumerate(token_tiles):
                        ins = dve.tensor_tensor(inner[0:kn, h % 2, t, 0:T2 - k0], ps[0:kn, 3 * (h % 2) + t, 0:T2 - k0],
                                                decay[0:kn, h, 0:T2 - k0], ALU.mult)
                    ins.then_inc(dve_out.sem, 1)

            @block.scalar
            def _(act):
                for n in range(2 * RET_HEADS):
                    act.wait_ge(pe_out3.sem, ob + n + 1)
                    act.activation(cat[:, 4 + n, :], ps[:, 6 + n % 2, 0:T2], ACT.Copy).then_inc(act_out.sem, 1)
                act.activation(pj[:, 32:40, :], pj[:, 32:40, :], ACT.Silu)
        pe_out.n += RET_HEADS
        pe_out3.n += 2 * RET_HEADS
        dve_out.n += RET_HEADS
        act_out.n += 2 * RET_HEADS

        pb, db, ab, tb0 = pe_out.n, dve_out.n, act_out.n, std_ready.n
        sq2 = view(sqf, 0, 8, T2)
        dev = view(sqf, 8 * T2, 4, T2)
        with nc.Block() as block:
            @block.tensor
            def _(pe):
                for h in range(RET_HEADS):
                    for f in range(2):
                        mm = pe.matmul(ps[:, h, 0:T2], ones[:, :], cat[:, 4 + 2 * h + f, :], start=(f == 0), stop=(f == 1))
                    mm.then_inc(pe_out.sem, 1)
                for h in range(RET_HEADS):
                    pe.wait_ge(act_out.sem, ab + h + 1)
                    for f in range(2):
                        mm = pe.matmul(ps[:, 4 + h, 0:T2], ones[:, :], sq2[:, 2 * h + f, :], start=(f == 0), stop=(f == 1))
                mm.then_inc(pe_out.sem, 1)

            @block.vector
            def _(dve):
                for h in range(RET_HEADS):
                    dve.wait_ge(pe_out.sem, pb + h + 1)
                    for f in range(2):
                        r = cat[:, 4 + 2 * h + f, :]
                        ins = dve.scalar_tensor_tensor(r, ps[:, h, 0:T2], -1.0 / RET_DV, r, ALU.mult, ALU.add)
                    ins.then_inc(dve_out.sem, 1)
                dve.wait_ge(std_ready.sem, tb0 + 1)
                chained(dve, dve.reciprocal(dev, dev), dve_step)
                for n in range(8):
                    r = cat[:, 4 + n, :]
                    ins = dve.scalar_tensor_tensor(r, r, prm[:, 2, 112 + n:113 + n], dev[:, n // 2, :], ALU.mult, ALU.mult)
                chained(dve, ins, dve_step)
                dve.tensor_tensor(cat[:, 4:12, :], cat[:, 4:12, :], pj[:, 32:40, :], ALU.mult)

            @block.scalar
            def _(act):
                for h in range(RET_HEADS):
                    act.wait_ge(dve_out.sem, db + h + 1)
                    act.activation(sq2[:, 2 * h:2 * h + 2, :], cat[:, 4 + 2 * h:6 + 2 * h, :], ACT.Square).then_inc(act_out.sem, 1)
                act.wait_ge(pe_out.sem, pb + RET_HEADS + 1)
                act.activation(dev, ps[:, 4:8, 0:T2], ACT.Sqrt, bias=epsb[:, 0:1], scale=1.0 / RET_DV).then_inc(std_ready.sem, 1)
        pe_out.n += RET_HEADS + 1
        dve_out.n += RET_HEADS
        act_out.n += RET_HEADS
        std_ready.n += 1
        product(narrow(cat, cat_r), T2, with_squares(T2))
        conv_ffn(0)

        with nc.Block() as block:
            @block.sync
            def _(sp):
                sp.dma_start(tri[:, :, :], a["k_tri"]).then_inc(loaded.sem, 16)
                sp.wait_ge(loaded.sem, loaded.n + 16)
        loaded.n += 16
        gained(gain2(80), flat2, lambda k: Y[:, k, 0:T2], KD, T2, squared=True)
        product(normed(T2), T2, copy_out(into(pj, 0, T2)))
        vs = view(exf, 0, 3, D)
        transposes([([pj[:, 16 + 4 * h + j, t0:t0 + tn] for j in range(4)], tn, P,
                     vs[0:tn, t, 4 * h * P:4 * (h + 1) * P].rearrange("p (j c) -> p j c", j=4))
                    for t, (t0, tn) in enumerate(token_tiles) for h in range(2)])
        offs = [0, T2, T2 + (T2 - P)]
        full_w, all_w = offs[2], offs[2] + T2 - 2 * P
        last = T2 - 2 * P
        DEEP = 4
        zs, sp_, lg, aw = (buf[:, at_:at_ + DEEP * all_w].rearrange("p (b n) -> p b n", b=DEEP)
                           for buf, at_ in ((sqf, 0), (sqf, 2048), (yf, 0), (yf, 2048)))
        parts = [(slice(0, P), slice(0, full_w)), (slice(0, last), slice(full_w, all_w))]
        zd, spd, ld, inc, exps_, out_ = pe_out, dve_out, act_out, pe_out2, dve_out2, act_out2
        vd, kd_ = pe_out3, dve_out3
        hb, e0 = h_ready.n, act_step.n
        z0, s0_, l0, i0, t0_, a0, v0, k0_, c0_ = (c.n for c in (zd, spd, ld, inc, exps_, out_, vd, kd_, scaled))

        with nc.Block() as block:
            @block.tensor
            def _(pe):
                def logits(h):
                    b, lo = h % 2, 64 * (h % 2)
                    if h >= 2:
                        pe.wait_ge(scaled.sem, c0_ + h - 1)
                    for t, (k0, kn) in enumerate(token_tiles):
                        mm = pe.matmul(ps[0:kn, b, offs[t]:offs[t] + T2 - k0], pj[lo:lo + 64, 8 + h // 2, k0:k0 + kn],
                                       pj[lo:lo + 64, h // 2, k0:T2], start=True, stop=True)
                    mm.then_inc(zd.sem, 1)

                def sums(h):
                    b = h % DEEP
                    pe.wait_ge(spd.sem, s0_ + h + 1)
                    if h >= DEEP:
                        pe.wait_ge(exps_.sem, t0_ + h - DEEP + 1)
                    for t, (k0, kn) in enumerate(token_tiles):
                        for u in range(t, 3):
                            u0, un = token_tiles[u]
                            c = offs[t] + u0 - k0
                            lhs = tri[0:kn, 0, 0:kn] if u == t else ones[0:un, 0:kn]
                            mm = pe.matmul(ps[0:kn, 2 + b, c:c + T2 - u0], lhs, sp_[0:un, b, offs[u]:offs[u] + T2 - u0],
                                           start=(u == t), stop=(u == 2), skip_group_check=True)
                    mm.then_inc(inc.sem, 1)

                def values(h):
                    b, lo = h % DEEP, 64 * (h % 2)
                    pe.wait_ge(out_.sem, a0 + h + 1)
                    if h >= 2:
                        pe.wait_ge(kd_.sem, k0_ + h - 1)
                    for t, (k0, kn) in enumerate(token_tiles):
                        mm = pe.matmul(ps[lo:lo + 64, 6 + h % 2, k0:T2], vs[0:kn, t, h * 64:h * 64 + 64],
                                       aw[0:kn, b, offs[t]:offs[t] + T2 - k0], start=(t == 0), stop=(t == 2), skip_group_check=True)
                    mm.then_inc(vd.sem, 1)

                logits(0)
                logits(1)
                for h in range(0, SB_HEADS, 2):
                    if h + 2 < SB_HEADS:
                        logits(h + 2)
                        logits(h + 3)
                    sums(h)
                    sums(h + 1)
                    if h:
                        values(h - 2)
                        values(h - 1)
                values(SB_HEADS - 2)
                values(SB_HEADS - 1)

            @block.scalar
            def _(act):
                def exp_z(h):
                    b = h % DEEP
                    act.wait_ge(h_ready.sem, hb + h + 1)
                    for r, c in parts:
                        ins = act.activation(lg[r, b, c], lg[r, b, c], ACT.Exp)
                    ins.then_inc(act_step.sem, 1)

                def log(h):
                    b = h % DEEP
                    act.wait_ge(act_step.sem, e0 + h + 1)
                    for r, c in parts:
                        ins = act.activation(lg[r, b, c], lg[r, b, c], ACT.Ln, bias=1.0)
                    ins.then_inc(ld.sem, 1)

                def weights(h):
                    b = h % DEEP
                    act.wait_ge(exps_.sem, t0_ + h + 1)
                    if h >= DEEP:
                        act.wait_ge(vd.sem, v0 + h - DEEP + 1)
                    for r, c in parts:
                        ins = act.activation(aw[r, b, c], zs[r, b, c], ACT.Exp)
                    ins.then_inc(out_.sem, 1)

                exp_z(0)
                exp_z(1)
                for h in range(0, SB_HEADS, 2):
                    log(h)
                    log(h + 1)
                    if h:
                        weights(h - 2)
                        weights(h - 1)
                    if h + 2 < SB_HEADS:
                        exp_z(h + 2)
                        exp_z(h + 3)
                weights(SB_HEADS - 2)
                weights(SB_HEADS - 1)

            @block.vector
            def _(dve):
                def mask(buf, b, which, op):
                    for t, (k0, kn) in enumerate(token_tiles):
                        x = buf[0:kn, b, offs[t]:offs[t] + kn]
                        ins = dve.tensor_tensor(x, x, tri[0:kn, which, 0:kn], op)
                    return ins

                def scale(h):
                    b = h % DEEP
                    dve.wait_ge(zd.sem, z0 + h + 1)
                    if h >= DEEP:
                        dve.wait_ge(out_.sem, a0 + h - DEEP + 1)
                    for r, c in parts:
                        ins = dve.tensor_scalar(zs[r, b, c], ps[r, h % 2, c], SB_D ** -0.5, None, ALU.mult)
                    ins.then_inc(scaled.sem, 1)
                    dve.wait_ge(scaled.sem, c0_ + h + 1)
                    for r, c in parts:
                        ins = dve.scalar_tensor_tensor(lg[r, b, c], zs[r, b, c], -1.0, zs[r, b, c], ALU.mult, ALU.min)
                    ins.then_inc(h_ready.sem, 1)

                def softplus(h):
                    b = h % DEEP
                    if h >= DEEP:
                        dve.wait_ge(inc.sem, i0 + h - DEEP + 1)
                    dve.wait_ge(scaled.sem, c0_ + h + 1)
                    dve.wait_ge(ld.sem, l0 + h + 1)
                    for r, c in parts:
                        ins = dve.scalar_tensor_tensor(sp_[r, b, c], zs[r, b, c], 0.0, lg[r, b, c], ALU.max, ALU.add)
                    chained(dve, ins, dve_step)
                    mask(sp_, b, 1, ALU.mult).then_inc(spd.sem, 1)

                def keep(h):
                    lo = 64 * (h % 2)
                    dve.wait_ge(vd.sem, v0 + h + 1)
                    dve.tensor_copy(cat[lo:lo + 64, h // 2, :], ps[lo:lo + 64, 6 + h % 2, 0:T2]).then_inc(kd_.sem, 1)

                def minus_sums(h):
                    b = h % DEEP
                    dve.wait_ge(inc.sem, i0 + h + 1)
                    for r, c in parts:
                        ins = dve.tensor_tensor(zs[r, b, c], zs[r, b, c], ps[r, 2 + b, c], ALU.subtract)
                    chained(dve, ins, dve_step)
                    mask(zs, b, 2, ALU.add).then_inc(exps_.sem, 1)

                scale(0)
                scale(1)
                for h in range(0, SB_HEADS, 2):
                    softplus(h)
                    softplus(h + 1)
                    if h + 2 < SB_HEADS:
                        scale(h + 2)
                        scale(h + 3)
                    minus_sums(h)
                    minus_sums(h + 1)
                    if h:
                        keep(h - 2)
                        keep(h - 1)
                keep(SB_HEADS - 2)
                keep(SB_HEADS - 1)
        for c in (zd, spd, ld, inc, exps_, out_, vd, kd_, scaled, h_ready, act_step):
            c.n += SB_HEADS
        product(narrow(cat, cat_r), T2, with_squares(T2))
        conv_ffn(1)
        gained(gain2(104), flat2, lambda k: Y[:, k, 0:T2], KD, T2, squared=True)
        finish(nc, a, out, H, XM, XM, sqf, stored, transposes, ctx, src=Y)


def constants():
    import numpy as np
    f = np.float32
    k = np.arange(P)
    c = {"k_ident": np.eye(P, dtype=f), "k_ones": np.ones((P, P), f)}

    def swap_of(dim, offset, quarter, period):
        R = np.zeros((P, P), f)
        for i in range(offset, dim):
            r = (i - offset) % period
            if r < quarter:
                R[i, i + quarter] = -1
            else:
                R[i, i - quarter] = 1
        return R.T

    swap = np.stack([swap_of(P, 0, 16, 32), swap_of(96, 64, 8, 16), swap_of(P, 0, 64, 128)], 1)
    c["k_swap"] = np.ascontiguousarray(swap)
    c["k_tri"] = np.ascontiguousarray(np.stack([
        (k[:, None] >= k[None, :]).astype(f),
        (k[:, None] < k[None, :]).astype(f),
        np.where(k[:, None] < k[None, :], 0, NEG).astype(f)], 1))
    short = np.zeros((P, P), f)
    n = T2 - 2 * P
    short[:n, :n] = np.eye(n)[::-1] * DSA_D ** 0.5
    c["k_sparse"] = np.ascontiguousarray(np.stack([
        np.eye(P, dtype=f)[::-1] * f(DSA_D ** 0.5), np.where(k[None, :] > k[:, None], NEG, 0).astype(f), short], 1))

    def angles(n_tokens, dim):
        t = np.arange(n_tokens)
        nf = dim // 4
        freqs = (f(10000.0) ** (-np.arange(nf, dtype=f) / f(nf))).astype(f)
        pos = np.stack([(t // 64).astype(f), (t % 64).astype(f)], 0)
        ang = pos[:, None, :] * freqs[None, :, None]
        return np.concatenate([ang[ax] for ax in (0, 0, 1, 1)], 0)

    first = np.zeros((P, 2304), f)
    th = 2 * np.pi * np.outer(k, k) / P
    first[:, 0:128], first[:, 128:256] = np.cos(th), np.sin(th)
    t = np.arange(SEQ)
    tt = 2 * np.pi * (np.outer(t, t) % SEQ) / SEQ
    s = 1.0 / np.sqrt(SEQ * P)
    d2 = np.stack([np.cos(tt) * s, -np.sin(tt) * s], 1).reshape(2, P, 2, SEQ).transpose(1, 0, 2, 3)
    first[:, 256:1280] = d2.reshape(P, 1024)
    da = np.tile(angles(SEQ, 64), (2, 1))
    first[:, 1280:1536], first[:, 1536:1792] = np.cos(da), np.sin(da)
    first[:, 1792:2048] = 1
    ml = angles(SEQ, 32)
    first[64:96, 1792:2048], first[64:96, 2048:2304] = np.cos(ml), np.sin(ml)
    c["k_first"] = first

    second = np.zeros((P, 2304), f)
    inv = (f(1) / (f(10000.0) ** (np.arange(64, dtype=f) / f(64)))).astype(f)
    ang = np.arange(T2, dtype=f)[None, :] * np.tile(inv, 2)[:, None]
    second[:, 0:T2], second[:, T2:2 * T2] = np.cos(ang), np.sin(ang)
    diff = np.arange(T2)[None, :] - k[:, None]
    for h in range(RET_HEADS):
        lg = np.log(1.0 - 2.0 ** (-5.0 - h))
        second[:, (2 + h) * T2:(3 + h) * T2] = np.where(diff >= 0, np.exp(np.maximum(diff, 0) * lg), 0) * RET_DK ** -0.5
    c["k_second"] = second

    dist = np.maximum(T2 - 1 - np.arange(BIAS_W), 0)
    large = 16 + (np.log(np.maximum(dist, 1).astype(f) / f(16)) / f(np.log(8.0)) * f(16)).astype(np.int32)
    bucket = np.where(dist < 16, dist, np.minimum(large, 31))
    c["k_bucket"] = (np.arange(32)[:, None] == bucket[None, :]).astype(f)
    return c


def kernel(**inputs):
    import numpy as np
    import concourse.bacc as bacc
    from concourse.bass_utils import run_bass_kernel_spmd as run

    nc = bacc.Bacc("TRN2", target_bir_lowering=False, num_devices=1)
    arrays, args = {}, {}
    for name, value in [*inputs.items(), *constants().items()]:
        v = np.ascontiguousarray(value)
        arrays[f"in_{name}"] = v
        args[name] = nc.dram_tensor(f"in_{name}", v.shape, mybir.dt.from_np(v.dtype), kind="ExternalInput").ap()
    out = nc.dram_tensor("out_0", (1, SEQ, D), F32, kind="ExternalOutput").ap()
    bias_rows = nc.dram_tensor("bias_rows", (DSA_HEADS, BIAS_W), F32, kind="Internal").ap()
    build(nc, args, out, bias_rows)
    r = run(nc, [arrays], core_ids=[0])
    return r.results[0]["out_0"]
```
